# Optimizing a Trainium2 kernel written in Bass

```python
import math, functools
import jax, jax.numpy as jnp
from jax import lax
import numpy as np

D_MODEL = 1024
BATCH = 1
SEQ = 256
DEPTH = 4

N_MIXERS = 3
MEM_LEN = 256
BLOCK = 128
ROPE_THETA = 10000.0
NEG = -1e30
LN_EPS = 1e-5
RMS_EPS = 1e-6

A_HEADS = 16
A_KV_HEADS = 4
A_HEAD_DIM = 64
A_WINDOW = 128

LRU_WIDTH = D_MODEL
LRU_BLOCKS = 4
LRU_BLOCK_W = LRU_WIDTH // LRU_BLOCKS
LRU_CONV = 4
LRU_C = 8.0

C_HEADS = 8
C_NOPE = 128
C_ROPE = 64
C_V = 128
C_Q_RANK = 384
C_KV_RANK = 256

X_HEADS = 4
X_HEAD_DIM = D_MODEL // X_HEADS

D_FF = 2816
FFN_CONV = 3

ALPHA = (2.0 * DEPTH) ** 0.25
BETA = (8.0 * DEPTH) ** -0.25

N_A = (DEPTH + 2) // 3
N_B = (DEPTH + 1) // 3
N_C = DEPTH // 3


def layer_norm(x, g, b):
    xf = x.astype(jnp.float32)
    mu = jnp.mean(xf, axis=-1, keepdims=True)
    var = jnp.mean(jnp.square(xf - mu), axis=-1, keepdims=True)
    y = (xf - mu) * lax.rsqrt(var + LN_EPS) * g.astype(jnp.float32) + b.astype(jnp.float32)
    return y.astype(x.dtype)

def rms_norm(x, g):
    xf = x.astype(jnp.float32)
    y = xf * lax.rsqrt(jnp.mean(jnp.square(xf), axis=-1, keepdims=True) + RMS_EPS)
    return (y * g.astype(jnp.float32)).astype(x.dtype)

def rope_tables(seq, dim):
    inv = 1.0 / (ROPE_THETA ** (jnp.arange(0, dim, 2, dtype=jnp.float32) / dim))
    ang = jnp.arange(seq, dtype=jnp.float32)[:, None] * inv[None, :]
    return jnp.cos(ang), jnp.sin(ang)

def apply_rope(x, cos, sin):
    c = cos[None, :, None, :].astype(x.dtype)
    s = sin[None, :, None, :].astype(x.dtype)
    x1, x2 = jnp.split(x, 2, axis=-1)
    return jnp.concatenate([x1 * c - x2 * s, x2 * c + x1 * s], axis=-1)

def causal_depthwise_conv(x, w, b):
    k_width = w.shape[0]
    s = x.shape[1]
    xp = jnp.pad(x, ((0, 0), (k_width - 1, 0), (0, 0)))
    y = xp[:, 0:s] * w[0]
    for k in range(1, k_width):
        y = y + xp[:, k:k + s] * w[k]
    return y + b

def swa_sink_attention(x, w_qkv, sinks, w_o, cos, sin):
    bsz, s, _ = x.shape
    grp = A_HEADS // A_KV_HEADS
    nb = s // BLOCK
    qkv = x @ w_qkv
    q, k, v = jnp.split(qkv, [A_HEADS * A_HEAD_DIM, (A_HEADS + A_KV_HEADS) * A_HEAD_DIM], axis=-1)
    q = apply_rope(q.reshape(bsz, s, A_HEADS, A_HEAD_DIM), cos, sin)
    k = apply_rope(k.reshape(bsz, s, A_KV_HEADS, A_HEAD_DIM), cos, sin)
    v = v.reshape(bsz, s, A_KV_HEADS, A_HEAD_DIM)
    qb = q.reshape(bsz, nb, BLOCK, A_KV_HEADS, grp, A_HEAD_DIM)

    def with_prev(t):
        tb = t.reshape(bsz, nb, BLOCK, A_KV_HEADS, A_HEAD_DIM)
        prev = jnp.pad(tb[:, :-1], ((0, 0), (1, 0), (0, 0), (0, 0), (0, 0)))
        return jnp.concatenate([prev, tb], axis=2)

    kb, vb = with_prev(k), with_prev(v)
    scores = jnp.einsum('bnqhgd,bnkhd->bnhgqk', qb, kb).astype(jnp.float32) * (A_HEAD_DIM ** -0.5)
    qi = jnp.arange(BLOCK)[:, None]
    kj = jnp.arange(2 * BLOCK)[None, :]
    dist = qi + BLOCK - kj
    band = (dist >= 0) & (dist < A_WINDOW)
    real_key = (jnp.arange(nb)[:, None, None] > 0) | (kj >= BLOCK)[None]
    valid = band[None] & real_key
    scores = jnp.where(valid[None, :, None, None], scores, NEG)
    sink = sinks.astype(jnp.float32).reshape(A_KV_HEADS, grp)[None, None, :, :, None, None]
    sink = jnp.broadcast_to(sink, scores.shape[:-1] + (1,))
    probs = jax.nn.softmax(jnp.concatenate([scores, sink], axis=-1), axis=-1)[..., :-1]
    out = jnp.einsum('bnhgqk,bnkhd->bnqhgd', probs.astype(v.dtype), vb)
    return out.reshape(bsz, s, A_HEADS * A_HEAD_DIM) @ w_o

def rglru_block(x, w_in, conv_w, conv_b, w_rgate, b_rgate, w_igate, b_igate, lam, w_o):
    bsz, s, _ = x.shape
    gate, u = jnp.split(x @ w_in, 2, axis=-1)
    u = causal_depthwise_conv(u, conv_w, conv_b)
    ub = u.reshape(bsz, s, LRU_BLOCKS, LRU_BLOCK_W)
    r = jax.nn.sigmoid(jnp.einsum('bshi,hij->bshj', ub, w_rgate).reshape(bsz, s, LRU_WIDTH) + b_rgate)
    i = jax.nn.sigmoid(jnp.einsum('bshi,hij->bshj', ub, w_igate).reshape(bsz, s, LRU_WIDTH) + b_igate)
    log_a = -LRU_C * r.astype(jnp.float32) * jax.nn.softplus(-lam.astype(jnp.float32))
    a = jnp.exp(log_a)
    b_in = jnp.sqrt(-jnp.expm1(2.0 * log_a)) * (i * u).astype(jnp.float32)

    def combine(c1, c2):
        a1, b1 = c1
        a2, b2 = c2
        return a1 * a2, a2 * b1 + b2

    _, h = lax.associative_scan(combine, (a, b_in), axis=1)
    y = h.astype(x.dtype) * jax.nn.gelu(gate)
    return y @ w_o

def mla_attention(x, w_down, q_norm, kv_norm, w_uq, w_ukv, w_o, cos_r, sin_r):
    bsz, s, _ = x.shape
    nb = s // BLOCK
    c = x @ w_down
    cq, ckv, k_rope = jnp.split(c, [C_Q_RANK, C_Q_RANK + C_KV_RANK], axis=-1)
    cq = rms_norm(cq, q_norm)
    ckv = rms_norm(ckv, kv_norm)
    q = (cq @ w_uq).reshape(bsz, s, C_HEADS, C_NOPE + C_ROPE)
    q_nope, q_rope = jnp.split(q, [C_NOPE], axis=-1)
    q_rope = apply_rope(q_rope, cos_r, sin_r)
    k_rope = apply_rope(k_rope[:, :, None, :], cos_r, sin_r)[:, :, 0]
    kv = (ckv @ w_ukv).reshape(bsz, s, C_HEADS, C_NOPE + C_V)
    k_nope, v = jnp.split(kv, [C_NOPE], axis=-1)
    scale = (C_NOPE + C_ROPE) ** -0.5
    qn = q_nope.reshape(bsz, nb, BLOCK, C_HEADS, C_NOPE).transpose(1, 0, 2, 3, 4)
    qr = q_rope.reshape(bsz, nb, BLOCK, C_HEADS, C_ROPE).transpose(1, 0, 2, 3, 4)
    key_pos = jnp.arange(s)

    def attend(args):
        n, qn_b, qr_b = args
        sc = (jnp.einsum('bqhd,bkhd->bhqk', qn_b, k_nope)
              + jnp.einsum('bqhd,bkd->bhqk', qr_b, k_rope)).astype(jnp.float32) * scale
        q_pos = n * BLOCK + jnp.arange(BLOCK)
        sc = jnp.where(key_pos[None, :] <= q_pos[:, None], sc, NEG)
        p = jax.nn.softmax(sc, axis=-1)
        return jnp.einsum('bhqk,bkhd->bqhd', p.astype(v.dtype), v)

    out = lax.map(attend, (jnp.arange(nb), qn, qr))
    out = out.transpose(1, 0, 2, 3, 4).reshape(bsz, s, C_HEADS * C_V)
    return out @ w_o

def memory_cross_attention(x, mem_k, mem_v, w_q, w_o):
    bsz, s, _ = x.shape
    q = (x @ w_q).reshape(bsz, s, X_HEADS, X_HEAD_DIM)
    sc = jnp.einsum('bshd,bmhd->bhsm', q, mem_k).astype(jnp.float32) * (X_HEAD_DIM ** -0.5)
    p = jax.nn.softmax(sc, axis=-1)
    o = jnp.einsum('bhsm,bmhd->bshd', p.astype(mem_v.dtype), mem_v).reshape(bsz, s, D_MODEL)
    return o @ w_o

def conv_glu_ffn(x, w_up, conv_w, conv_b, w_down):
    h = causal_depthwise_conv(x @ w_up, conv_w, conv_b)
    g, u = jnp.split(h, 2, axis=-1)
    return (jax.nn.silu(g) * u) @ w_down

def first_inputs(seed: int = 0) -> dict:
    key = jax.random.key(seed)
    ks = iter(jax.random.split(key, 40))

    def dense(shape, fan_in, scale=1.0):
        return jax.random.normal(next(ks), shape, jnp.float32) * (scale * fan_in ** -0.5)

    def small(shape, scale=0.01):
        return jax.random.normal(next(ks), shape, jnp.float32) * scale

    def gain(shape):
        return 1.0 + small(shape)

    qkv_w = (A_HEADS + 2 * A_KV_HEADS) * A_HEAD_DIM
    a0 = jax.random.uniform(next(ks), (N_B, LRU_WIDTH), jnp.float32, 0.9, 0.999) ** (1.0 / LRU_C)
    return {
        "x": jax.random.normal(next(ks), (BATCH, SEQ, D_MODEL), jnp.float32),
        "mem": jax.random.normal(next(ks), (BATCH, MEM_LEN, D_MODEL), jnp.float32),
        "a_w_qkv": dense((N_A, D_MODEL, qkv_w), D_MODEL),
        "a_sinks": small((N_A, A_HEADS), 1.0),
        "a_w_o": dense((N_A, A_HEADS * A_HEAD_DIM, D_MODEL), A_HEADS * A_HEAD_DIM, BETA),
        "b_w_in": dense((N_B, D_MODEL, 2 * LRU_WIDTH), D_MODEL),
        "b_conv_w": dense((N_B, LRU_CONV, LRU_WIDTH), LRU_CONV),
        "b_conv_b": small((N_B, LRU_WIDTH)),
        "b_w_rgate": dense((N_B, LRU_BLOCKS, LRU_BLOCK_W, LRU_BLOCK_W), LRU_BLOCK_W),
        "b_b_rgate": small((N_B, LRU_WIDTH)),
        "b_w_igate": dense((N_B, LRU_BLOCKS, LRU_BLOCK_W, LRU_BLOCK_W), LRU_BLOCK_W),
        "b_b_igate": small((N_B, LRU_WIDTH)),
        "b_lambda": jnp.log(a0) - jnp.log1p(-a0),
        "b_w_o": dense((N_B, LRU_WIDTH, D_MODEL), LRU_WIDTH, BETA),
        "c_w_down": dense((N_C, D_MODEL, C_Q_RANK + C_KV_RANK + C_ROPE), D_MODEL),
        "c_q_norm": gain((N_C, C_Q_RANK)),
        "c_kv_norm": gain((N_C, C_KV_RANK)),
        "c_w_uq": dense((N_C, C_Q_RANK, C_HEADS * (C_NOPE + C_ROPE)), C_Q_RANK),
        "c_w_ukv": dense((N_C, C_KV_RANK, C_HEADS * (C_NOPE + C_V)), C_KV_RANK),
        "c_w_o": dense((N_C, C_HEADS * C_V, D_MODEL), C_HEADS * C_V, BETA),
        "mem_w_kv": dense((D_MODEL, 2 * D_MODEL), D_MODEL),
        "x_w_q": dense((DEPTH, D_MODEL, D_MODEL), D_MODEL),
        "x_w_o": dense((DEPTH, D_MODEL, D_MODEL), D_MODEL, BETA),
        "f_w_up": dense((DEPTH, D_MODEL, 2 * D_FF), D_MODEL),
        "f_conv_w": dense((DEPTH, FFN_CONV, 2 * D_FF), FFN_CONV),
        "f_conv_b": small((DEPTH, 2 * D_FF)),
        "f_w_down": dense((DEPTH, D_FF, D_MODEL), D_FF, BETA),
        "ln_g": gain((DEPTH, 3, D_MODEL)),
        "ln_b": small((DEPTH, 3, D_MODEL)),
    }

def first_block(x, mem, a_w_qkv, a_sinks, a_w_o, b_w_in, b_conv_w, b_conv_b, b_w_rgate, b_b_rgate,
              b_w_igate, b_b_igate, b_lambda, b_w_o, c_w_down, c_q_norm, c_kv_norm, c_w_uq, c_w_ukv,
              c_w_o, mem_w_kv, x_w_q, x_w_o, f_w_up, f_conv_w, f_conv_b, f_w_down, ln_g, ln_b):
    bsz, s, _ = x.shape
    cos_a, sin_a = rope_tables(s, A_HEAD_DIM)
    cos_c, sin_c = rope_tables(s, C_ROPE)
    mem_k, mem_v = jnp.split(mem @ mem_w_kv, 2, axis=-1)
    mem_k = mem_k.reshape(bsz, MEM_LEN, X_HEADS, X_HEAD_DIM)
    mem_v = mem_v.reshape(bsz, MEM_LEN, X_HEADS, X_HEAD_DIM)
    for i in range(DEPTH):
        kind, j = i % N_MIXERS, i // N_MIXERS
        if kind == 0:
            y = swa_sink_attention(x, a_w_qkv[j], a_sinks[j], a_w_o[j], cos_a, sin_a)
        elif kind == 1:
            y = rglru_block(x, b_w_in[j], b_conv_w[j], b_conv_b[j], b_w_rgate[j], b_b_rgate[j],
                            b_w_igate[j], b_b_igate[j], b_lambda[j], b_w_o[j])
        else:
            y = mla_attention(x, c_w_down[j], c_q_norm[j], c_kv_norm[j], c_w_uq[j], c_w_ukv[j],
                              c_w_o[j], cos_c, sin_c)
        x = layer_norm(ALPHA * x + y, ln_g[i, 0], ln_b[i, 0])
        x = layer_norm(ALPHA * x + memory_cross_attention(x, mem_k, mem_v, x_w_q[i], x_w_o[i]),
                       ln_g[i, 1], ln_b[i, 1])
        x = layer_norm(ALPHA * x + conv_glu_ffn(x, f_w_up[i], f_conv_w[i], f_conv_b[i], f_w_down[i]),
                       ln_g[i, 2], ln_b[i, 2])
    return x


DEPTH_2 = 2

HEAD_DIM = 64
N_HEADS_TOTAL = D_MODEL // HEAD_DIM
N_MEM_HEADS = 4
N_MIX_HEADS = N_HEADS_TOTAL - N_MEM_HEADS
D_MIX = N_MIX_HEADS * HEAD_DIM
D_MEMQ = N_MEM_HEADS * HEAD_DIM
MEM_TOKENS = 256
CONV_WIDTH = 3
Q_BLOCK = 128
DILATED_BRANCHES = ((128, 1), (512, 4), (2048, 16))
N_MIXERS_2 = 2
N_A_LAYERS = (DEPTH_2 + 1) // 2
N_B_LAYERS = DEPTH_2 // 2
FOX_IN = 3 * D_MIX + N_MIX_HEADS + D_MEMQ
DIL_IN = 3 * D_MIX + D_MEMQ
NORM_EPS = 1e-6
NEG_2 = -1e30


def rmsnorm(x, g):
    xf = x.astype(jnp.float32)
    y = xf * lax.rsqrt(jnp.mean(xf * xf, axis=-1, keepdims=True) + NORM_EPS)
    return (y * g.astype(jnp.float32)).astype(x.dtype)

def split_heads(t, n_heads):
    b, s, _ = t.shape
    return t.reshape(b, s, n_heads, HEAD_DIM).transpose(0, 2, 1, 3)

def merge_heads(t):
    b, h, s, d = t.shape
    return t.transpose(0, 2, 1, 3).reshape(b, s, h * d)

def rope_tables_2(seq):
    inv = 1.0 / (ROPE_THETA ** (jnp.arange(0, HEAD_DIM, 2, dtype=jnp.float32) / HEAD_DIM))
    ang = jnp.arange(seq, dtype=jnp.float32)[:, None] * inv[None, :]
    return jnp.cos(ang), jnp.sin(ang)

def apply_rope_2(x, cos, sin):
    x1, x2 = jnp.split(x.astype(jnp.float32), 2, axis=-1)
    y = jnp.concatenate([x1 * cos - x2 * sin, x2 * cos + x1 * sin], axis=-1)
    return y.astype(x.dtype)

def fox_attention(q, k, v, log_f):
    b, h, s, dh = q.shape
    c = lax.cumsum(log_f, axis=2)
    nb = s // Q_BLOCK
    scale = dh ** -0.5
    qb = q.reshape(b, h, nb, Q_BLOCK, dh).transpose(2, 0, 1, 3, 4)
    cb = c.reshape(b, h, nb, Q_BLOCK).transpose(2, 0, 1, 3)
    starts = jnp.arange(nb, dtype=jnp.int32) * Q_BLOCK
    kpos = jnp.arange(s, dtype=jnp.int32)

    def one_block(args):
        qi, ci, st = args
        sc = jnp.einsum('bhqd,bhkd->bhqk', qi, k, preferred_element_type=jnp.float32) * scale
        sc = sc + ci[..., :, None] - c[..., None, :]
        qpos = st + jnp.arange(Q_BLOCK, dtype=jnp.int32)
        sc = jnp.where(kpos[None, :] <= qpos[:, None], sc, NEG_2)
        p = jax.nn.softmax(sc, axis=-1)
        return jnp.einsum('bhqk,bhkd->bhqd', p.astype(v.dtype), v)

    out = lax.map(one_block, (qb, cb, starts))
    return out.transpose(1, 2, 0, 3, 4).reshape(b, h, s, dh)

def dilated_branch(q, k, v, window, dilation):
    b, h, s, dh = q.shape
    L = window // dilation
    chunk = dilation * L
    sp = -(-s // chunk) * chunk
    n = sp // dilation
    nb = n // L
    scale = dh ** -0.5

    def strided(t):
        t = jnp.pad(t, ((0, 0), (0, 0), (0, sp - s), (0, 0)))
        t = t.reshape(b, h, n, dilation, dh).transpose(0, 1, 3, 2, 4)
        return t.reshape(b, h, dilation, nb, L, dh)

    def with_prev(t):
        prev = jnp.pad(t, ((0, 0), (0, 0), (0, 0), (1, 0), (0, 0), (0, 0)))[:, :, :, :-1]
        return jnp.concatenate([prev, t], axis=4)

    qs = strided(q)
    kb = with_prev(strided(k))
    vb = with_prev(strided(v))
    sc = jnp.einsum('bhrnqd,bhrnkd->bhrnqk', qs, kb, preferred_element_type=jnp.float32) * scale
    a = jnp.arange(L, dtype=jnp.int32)
    cidx = jnp.arange(2 * L, dtype=jnp.int32)
    blk = jnp.arange(nb, dtype=jnp.int32)
    dist = a[:, None] + L - cidx[None, :]
    valid = (dist >= 0) & (dist <= L)
    valid = valid[None] & ((blk[:, None, None] > 0) | (cidx[None, None, :] >= L))
    sc = jnp.where(valid, sc, NEG_2)
    m = jnp.max(sc, axis=-1, keepdims=True)
    e = jnp.exp(sc - m)
    den = jnp.sum(e, axis=-1, keepdims=True)
    o = jnp.einsum('bhrnqk,bhrnkd->bhrnqd', (e / den).astype(v.dtype), vb)
    lse = (m + jnp.log(den))[..., 0]
    o = o.reshape(b, h, dilation, n, dh).transpose(0, 1, 3, 2, 4).reshape(b, h, sp, dh)[:, :, :s]
    lse = lse.reshape(b, h, dilation, n).transpose(0, 1, 3, 2).reshape(b, h, sp)[:, :, :s]
    return o, lse

def dilated_attention(q, k, v):
    outs, lses = [], []
    for window, dilation in DILATED_BRANCHES:
        o, lse = dilated_branch(q, k, v, window, dilation)
        outs.append(o)
        lses.append(lse)
    wts = jax.nn.softmax(jnp.stack(lses, axis=0), axis=0)
    return jnp.einsum('gbhs,gbhsd->bhsd', wts.astype(v.dtype), jnp.stack(outs, axis=0))

def memory_attention(qm, mem_n, w_mem_kv):
    km, vm = jnp.split(mem_n @ w_mem_kv, 2, axis=-1)
    km = split_heads(km, N_MEM_HEADS)
    vm = split_heads(vm, N_MEM_HEADS)
    sc = jnp.einsum('bhqd,bhkd->bhqk', qm, km, preferred_element_type=jnp.float32) * (HEAD_DIM ** -0.5)
    p = jax.nn.softmax(sc, axis=-1)
    return jnp.einsum('bhqk,bhkd->bhqd', p.astype(vm.dtype), vm)

def conv_ffn(xn, w_up, conv_w, conv_b, w_down):
    u = xn @ w_up
    s = u.shape[1]
    up = jnp.pad(u, ((0, 0), (CONV_WIDTH - 1, 0), (0, 0)))
    c = conv_b
    for j in range(CONV_WIDTH):
        c = c + conv_w[j] * up[:, j:j + s]
    val, gate = jnp.split(c, 2, axis=-1)
    return (jax.nn.silu(gate) * val) @ w_down

def second_inputs(seed: int = 0) -> dict:
    key = jax.random.key(seed)
    ks = jax.random.split(key, 16)
    f32 = jnp.float32
    nrm = lambda k, shape, scale: jax.random.normal(k, shape, f32) * scale
    forget_bias_init = 3.0
    return {
        'x': nrm(ks[0], (BATCH, SEQ, D_MODEL), 1.0),
        'mem': nrm(ks[1], (BATCH, MEM_TOKENS, D_MODEL), 1.0),
        'norm_mix': 1.0 + nrm(ks[2], (DEPTH_2, D_MODEL), 0.1),
        'norm_mem': 1.0 + nrm(ks[3], (DEPTH_2, D_MODEL), 0.1),
        'norm_ffn': 1.0 + nrm(ks[4], (DEPTH_2, D_MODEL), 0.1),
        'w_in_fox': nrm(ks[5], (N_A_LAYERS, D_MODEL, FOX_IN), D_MODEL ** -0.5),
        'b_forget': forget_bias_init + nrm(ks[6], (N_A_LAYERS, N_MIX_HEADS), 0.5),
        'w_in_dil': nrm(ks[7], (N_B_LAYERS, D_MODEL, DIL_IN), D_MODEL ** -0.5),
        'w_mem_kv': nrm(ks[8], (DEPTH_2, D_MODEL, 2 * D_MEMQ), D_MODEL ** -0.5),
        'w_out': nrm(ks[9], (DEPTH_2, D_MODEL, D_MODEL), D_MODEL ** -0.5),
        'w_up': nrm(ks[10], (DEPTH_2, D_MODEL, 2 * D_FF), D_MODEL ** -0.5),
        'conv_w': nrm(ks[11], (DEPTH_2, CONV_WIDTH, 2 * D_FF), CONV_WIDTH ** -0.5),
        'conv_b': nrm(ks[12], (DEPTH_2, 2 * D_FF), 0.02),
        'w_down': nrm(ks[13], (DEPTH_2, D_FF, D_MODEL), D_FF ** -0.5),
        'norm_final': 1.0 + nrm(ks[14], (D_MODEL,), 0.1),
    }

def second_block(x, mem, norm_mix, norm_mem, norm_ffn, w_in_fox, b_forget, w_in_dil,
              w_mem_kv, w_out, w_up, conv_w, conv_b, w_down, norm_final):
    s = x.shape[1]
    cos, sin = rope_tables_2(s)
    h = x
    for layer in range(DEPTH_2):
        kind = layer % N_MIXERS_2
        slot = layer // N_MIXERS_2
        xn = rmsnorm(h, norm_mix[layer])
        mn = rmsnorm(mem, norm_mem[layer])
        if kind == 0:
            proj = xn @ w_in_fox[slot]
            q, k, v, f_logit, qm = jnp.split(
                proj, [D_MIX, 2 * D_MIX, 3 * D_MIX, 3 * D_MIX + N_MIX_HEADS], axis=-1)
            log_f = jax.nn.log_sigmoid(
                (f_logit + b_forget[slot]).astype(jnp.float32)).transpose(0, 2, 1)
            mix = fox_attention(split_heads(q, N_MIX_HEADS), split_heads(k, N_MIX_HEADS),
                                split_heads(v, N_MIX_HEADS), log_f)
        else:
            proj = xn @ w_in_dil[slot]
            q, k, v, qm = jnp.split(proj, [D_MIX, 2 * D_MIX, 3 * D_MIX], axis=-1)
            qh = apply_rope_2(split_heads(q, N_MIX_HEADS), cos, sin)
            kh = apply_rope_2(split_heads(k, N_MIX_HEADS), cos, sin)
            mix = dilated_attention(qh, kh, split_heads(v, N_MIX_HEADS))
        mem_out = memory_attention(split_heads(qm, N_MEM_HEADS), mn, w_mem_kv[layer])
        heads = jnp.concatenate([mix, mem_out], axis=1)
        h = h + merge_heads(heads) @ w_out[layer]
        h = h + conv_ffn(rmsnorm(h, norm_ffn[layer]), w_up[layer], conv_w[layer],
                         conv_b[layer], w_down[layer])
    return rmsnorm(h, norm_final)


def setup_inputs(seed=0):
    out = dict(first_inputs(seed))
    for name, value in second_inputs(seed + 1).items():
        if name != "x":
            out[name + "_2"] = value
    return out


def reference(
    x, mem, a_w_qkv, a_sinks, a_w_o, b_w_in, b_conv_w, b_conv_b, b_w_rgate, b_b_rgate,
    b_w_igate, b_b_igate, b_lambda, b_w_o, c_w_down, c_q_norm, c_kv_norm, c_w_uq, c_w_ukv,
    c_w_o, mem_w_kv, x_w_q, x_w_o, f_w_up, f_conv_w, f_conv_b, f_w_down, ln_g, ln_b, mem_2,
    norm_mix_2, norm_mem_2, norm_ffn_2, w_in_fox_2, b_forget_2, w_in_dil_2, w_mem_kv_2, w_out_2,
    w_up_2, conv_w_2, conv_b_2, w_down_2, norm_final_2,
):
    x = first_block(
        x, mem, a_w_qkv, a_sinks, a_w_o, b_w_in, b_conv_w, b_conv_b, b_w_rgate, b_b_rgate,
        b_w_igate, b_b_igate, b_lambda, b_w_o, c_w_down, c_q_norm, c_kv_norm, c_w_uq, c_w_ukv,
        c_w_o, mem_w_kv, x_w_q, x_w_o, f_w_up, f_conv_w, f_conv_b, f_w_down, ln_g, ln_b,
    )
    return second_block(
        x, mem_2, norm_mix_2, norm_mem_2, norm_ffn_2, w_in_fox_2, b_forget_2, w_in_dil_2,
        w_mem_kv_2, w_out_2, w_up_2, conv_w_2, conv_b_2, w_down_2, norm_final_2,
    )


_drawn_inputs = setup_inputs


def setup_inputs(seed=0):
    import zlib

    import numpy as np

    out = dict(_drawn_inputs(seed))
    spreads = {}
    factors = {'a_sinks': 4.158,
     'b_conv_b': 6.776,
     'b_b_rgate': 8.0,
     'b_b_igate': 8.0,
     'c_q_norm': 8.0,
     'c_kv_norm': 8.0,
     'f_conv_b': 8.0,
     'norm_mem_2': 4.576,
     'conv_b_2': 2.719}
    for name, (base, spread) in spreads.items():
        noise = np.random.default_rng([zlib.crc32(name.encode()), seed]).standard_normal(out[name].shape)
        drawn = base * np.exp(spread * noise) if base else spread * noise
        out[name] = __import__('jax').numpy.asarray(drawn.astype(out[name].dtype))
    for name, factor in factors.items():
        out[name] = (out[name] * factor).astype(out[name].dtype)
    return out
```

```python
from contextlib import ExitStack, contextmanager
import concourse.bass as bass
from concourse import mybir

F32 = mybir.dt.float32
F32R = mybir.dt.float32r
ACT = mybir.ActivationFunctionType
ALU = mybir.AluOpType
AX = mybir.AxisListType.X

P = 128
SEQ = 256
TB = SEQ // P
D = 1024
KT = D // P
DEPTH = 4
DEPTH_2 = 2
ALPHA = (2.0 * DEPTH) ** 0.25
LN_EPS = 1e-5
RMS_EPS = 1e-6
FF = 2816
FT = FF // P
TAPS = 3

A_HEADS, A_KV, HD = 16, 4, 64
C_HEADS, C_NOPE, C_ROPE, C_V, C_QR, C_KVR = 8, 128, 64, 128, 384, 256
X_HEADS, X_HD = 4, 256
LRU_TAPS, LRU_C = 4, 8.0
MIX_HEADS, MEM_HEADS = 12, 4
D_MIX, D_MEMQ = MIX_HEADS * HD, MEM_HEADS * HD

UNIT = 1024
RING = 6
AHEAD = 4
BANK = 512


class Count:

    def __init__(self, prog, name, by=1):
        self.prog, self.by, self.n = prog, by, 0
        self.sem = prog.ctx.enter_context(prog.nc.semaphore(name))

    def up(self, ins):
        ins.then_inc(self.sem, self.by)
        self.n += 1
        return self.now()

    def now(self):
        return (self, self.n, self.prog.loop is not None)

    def at(self, n):
        return (self, n, self.prog.loop is not None)


class Lane:

    def __init__(self, prog, eng, name):
        self.prog, self.eng = prog, eng
        self.done = Count(prog, name)
        self.seen = {}

    def wait(self, *marks):
        for m in marks:
            if isinstance(m, list):
                self.wait(*m)
                continue
            count, n, inside = m
            if n <= 0 and not inside:
                continue
            key = (count, inside)
            if self.seen.get(key, -1) >= n:
                continue
            self.seen[key] = n
            if inside:
                i, per = self.prog.loop
                self.eng.wait_ge(count.sem, i * (per[count] * count.by) + n * count.by)
            else:
                self.eng.wait_ge(count.sem, n * count.by)

    def __call__(self, after, issue):
        self.wait(*after)
        return self.done.up(issue(self.eng))


class Program:
    def __init__(self, nc, ctx):
        self.nc, self.ctx, self.loop = nc, ctx, None
        self.pe = Lane(self, nc.tensor, "pe_done")
        self.act = Lane(self, nc.scalar, "act_done")
        self.dve = Lane(self, nc.vector, "dve_done")
        self.pool = Lane(self, nc.gpsimd, "pool_done")
        self.sp = Lane(self, nc.sync, "sp_done")
        self.lanes = [self.pe, self.act, self.dve, self.pool, self.sp]

    @contextmanager
    def repeat(self, times, per):
        start = {c: c.n for c in per}
        for lane in self.lanes:
            lane.seen = {k: v for k, v in lane.seen.items() if not k[1]}
        with self.nc.Fori(0, times) as i:
            self.loop = (i, per)
            yield i
        self.loop = None
        for c, n in per.items():
            assert c.n - start[c] == n, (c.sem, c.n - start[c], n)
            c.n = start[c] + n * times
        for lane in self.lanes:
            lane.seen = {k: v for k, v in lane.seen.items() if not k[1]}

    def sbuf(self, name, shape, dt=F32):
        return self.ctx.enter_context(self.nc.sbuf_tensor(name, shape, dt))


class Split:

    def __init__(self, prog, name, tiles):
        self.hi = prog.sbuf(name + "_hi", [P, tiles, SEQ], F32R)
        self.lo = prog.sbuf(name + "_lo", [P, tiles, SEQ], F32R)
        self.ready, self.busy = [], []


class WeightStream:

    def __init__(self, prog, total):
        self.prog, self.total = prog, total
        self.raw = prog.sbuf("w_raw", [P, RING, UNIT])
        self.hi = prog.sbuf("w_hi", [P, RING, UNIT], F32R)
        self.lo = prog.sbuf("w_lo", [P, RING, UNIT], F32R)
        self.landed = [Count(prog, f"w_landed{s}", 16) for s in range(RING)]
        self.hi_done = Count(prog, "w_hi_done")
        self.lo_done = Count(prog, "w_lo_done")
        self.used = Count(prog, "w_used")
        self.next = 0
        self.split_next = 0

    def counts(self, units):
        per = {c: units // RING for c in self.landed}
        per.update({self.hi_done: units, self.lo_done: units, self.used: units})
        return per

    def skip(self, units):
        self.next += units
        self.split_next += units

    def split(self):
        v, p = self.split_next, self.prog
        self.split_next += 1
        if v >= self.total and p.loop is None:
            return
        s = v % RING
        p.act.wait(self.landed[s].at(v // RING + 1), self.used.at(v - RING + 1))
        self.hi_done.up(p.nc.scalar.copy(self.hi[:, s, :], self.raw[:, s, :]))
        p.dve.wait(self.hi_done.at(v + 1))
        self.lo_done.up(p.nc.vector.tensor_tensor(
            self.lo[:, s, :], self.raw[:, s, :], self.hi[:, s, :].bitcast(F32), ALU.subtract))

    def take(self, src):
        u, p = self.next, self.prog
        self.next += 1
        s, (_, k, n) = u % RING, src.shape
        p.sp.wait(self.lo_done.at(u - RING + 1))
        self.landed[s].up(p.nc.sync.dma_start(
            self.raw[:, s, 0:k * n].rearrange("p (k n) -> p k n", k=k), src))
        while self.split_next <= u + AHEAD:
            self.split()
        p.pe.wait(self.lo_done.at(u + 1))
        return [t[:, s, 0:k * n].rearrange("p (k n) -> p k n", k=k) for t in (self.hi, self.lo)]


def product(nc, out, stat, mov, first, last):
    nc.tensor.matmul(out, stat[0], mov[0], start=first, stop=False)
    nc.tensor.matmul(out, stat[0], mov[1], start=False, stop=False)
    return nc.tensor.matmul(out, stat[1], mov[0], start=False, stop=last)


def rows(ap, n=P):
    return ap.rearrange("(k p) n -> p k n", p=n)


class Model:
    def __init__(self, nc, ctx, t, total, stop=None):
        self.nc, self.t = nc, t
        p = self.p = Program(nc, ctx)
        self.pe, self.act, self.dve, self.pool, self.sp = p.pe, p.act, p.dve, p.pool, p.sp
        self.w = WeightStream(p, total)
        self.loads = [Count(p, f"load{i}", 16) for i in range(8)]
        self.load_turn = 0
        self.par_loads = Count(p, "parameter_loads", 16)
        self.const_loads = Count(p, "constant_loads", 16)
        self.stores = Count(p, "stores", 16)
        self.psum = ctx.enter_context(nc.psum_tensor("psum", [P, 8, BANK], F32))
        self.bank_free = [[] for _ in range(8)]
        self.turn = 0
        self.x_tok = p.sbuf("x_tok", [P, TB, D])
        self.n_tok = p.sbuf("n_tok", [P, TB, D])
        self.x_ready, self.n_busy = [], []
        self.xt = Split(p, "xt", KT)
        self.fresh = p.sbuf("fresh", [P, 2, 2, SEQ])
        self.fresh_busy = [[], []]
        self.fresh_turn = 0
        self.gain_row = p.sbuf("gain_row", [P, D])
        self.bias_row = p.sbuf("bias_row", [P, D])
        self.row_busy = []
        self.ident = p.sbuf("ident", [P, P])
        self.rope_cos = p.sbuf("rope_cos", [P, TB, HD])
        self.rope_sin = p.sbuf("rope_sin", [P, TB, HD])
        self.mask = p.sbuf("mask", [P, TB, SEQ])
        self.mask_busy = []
        self.mem_kt = p.sbuf("mem_kt", [P, KT, SEQ])
        self.mem_v = p.sbuf("mem_v", [P, TB, D])
        self.qt = p.sbuf("qt", [P, KT, SEQ])
        self.kt = p.sbuf("kt", [P, KT, SEQ])
        self.v = p.sbuf("v", [P, TB, D])
        self.qrt = p.sbuf("qrt", [P, 4, SEQ])
        self.krt = p.sbuf("krt", [P, SEQ])
        self.e = p.sbuf("e", [P, 2, 2, TB, SEQ])
        self.pt = p.sbuf("pt", [P, 2, 2, TB, SEQ])
        self.tok = p.sbuf("tok", [P, TB, D])
        self.tok_busy = []
        self.swap = p.sbuf("swap", [P, BANK])
        self.swap_busy = []
        self.stat = p.sbuf("stat", [P, 2, 4, 4])
        self.norm = p.sbuf("norm", [P, 32])
        self.eps_pow = p.sbuf("eps_pow", [P, 2])
        self.small = p.sbuf("small", [P, 8, 24])
        self.half_neg = self.pool([], lambda e: e.memset(self.eps_pow[:], -0.5))
        for dst, src in ((self.ident[:], t["c_ident"]), (self.rope_cos[:], rows(t["c_cos"])),
                         (self.rope_sin[:], rows(t["c_sin"]))):
            self.load(dst, src, (), self.const_loads)
        self.consts = self.const_loads.now()
        self.stop = stop


    def load(self, dst, src, after=(), count=None):
        if count is None:
            count = self.loads[self.load_turn % len(self.loads)]
            self.load_turn += 1
            self.pool.wait(count.now())
        self.pool.wait(*after)
        with self.nc.allow_non_contiguous_dma(reason="small parameter"):
            ins = self.nc.gpsimd.dma_start(dst, src)
        return count.up(ins)

    def bank(self, wide=False):
        k = self.turn % 8 if wide else 4 + self.turn % 4
        self.turn += 1
        self.pe.wait(*self.bank_free[k])
        return k

    def params(self):
        t = self.t
        tile = lambda ap: ap.rearrange("t (m p) -> (t m) p", p=P)
        vec = lambda ap: ap.rearrange("(m p) -> m p", p=P)
        batches, self.col = [], {}
        half = (TAPS + 1) * 2 * FT // 2
        for name, w, b, depth in (("f", t["f_conv_w"], t["f_conv_b"], DEPTH),
                                  ("g", t["conv_w_2"], t["conv_b_2"], DEPTH_2)):
            for l in range(depth):
                taps = tile(w[l])
                batches.append(((name, l), [taps[0:half]]))
                batches.append((None, [taps[half:TAPS * 2 * FT], vec(b[l])]))
        batches.append(("ln_g", [tile(t["ln_g"].rearrange("l k n -> (l k) n"))]))
        batches.append(("ln_b", [tile(t["ln_b"].rearrange("l k n -> (l k) n"))]))
        batches.append(("norms_2", [tile(t["norm_mix_2"]), tile(t["norm_mem_2"]), tile(t["norm_ffn_2"])]))
        batches.append(("lru", [tile(t["b_conv_w"][0]), tile(t["b_conv_b"]), tile(t["b_b_rgate"]),
                                tile(t["b_b_igate"]), tile(t["b_lambda"]), tile(t["c_q_norm"]),
                                tile(t["c_kv_norm"])]))
        total = sum(a.shape[0] for _, parts in batches for a in parts)
        self.par = self.p.sbuf("par", [P, total])
        stage = self.e[:].rearrange("p a b c n -> p (a b c n)")
        self.par_jobs = []
        at = 0
        for j, (name, parts) in enumerate(batches):
            if name is not None:
                self.col[name] = at
            r = 0
            for a in parts:
                self.load(stage[r:r + a.shape[0], j * P:(j + 1) * P], a, (), self.par_loads)
                r += a.shape[0]
            self.par_jobs.append((stage[0:r, j * P:(j + 1) * P], r, at))
            at += r
        self.par_loaded = self.par_loads.now()

    def turn_params(self):
        for src, r, at in self.par_jobs:
            k = self.bank()
            m = self.pe([self.par_loaded, self.consts],
                        lambda e: e.transpose(self.psum[:, k, 0:r], src, self.ident[0:r, 0:r]))
            m = self.act([m], lambda e: e.copy(self.par[:, at:at + r], self.psum[:, k, 0:r]))
            self.bank_free[k] = [m]
        self.par_ready = m
        self.dve.wait(m)

    def cols(self, name, off, n):
        a = self.col[name] + off
        return self.par[:, a:a + n]

    def split_out(self, dst, tiles, src, after=(), scale=None):
        hi, lo = dst.hi[:, tiles, :], dst.lo[:, tiles, :]
        m = self.act([*after, *dst.busy], lambda e: e.copy(hi, src))
        m2 = self.dve([m], lambda e: e.tensor_tensor(lo, src, hi.bitcast(F32), ALU.subtract))
        dst.ready = [m2]
        return m2

    def to_features(self, src, ntiles, dst, tile0, after, gain=None, bias=None):
        for j in range(0, ntiles, 2):
            nt = min(2, ntiles - j)
            k = self.bank()
            out = self.psum[:, k, :].rearrange("p (a n) -> p a n", a=2)
            self.pe.wait(*after, self.consts)
            for a in range(nt):
                for b in range(TB):
                    ins = self.nc.tensor.transpose(out[:, a, b * P:(b + 1) * P], src(b, j + a), self.ident[:])
            m = self.pe.done.up(ins)
            if gain is None:
                m = self.split_out(dst, slice(tile0 + j, tile0 + j + nt), out[:, 0:nt, :], [m])
                self.bank_free[k] = [m]
                continue
            f = self.fresh_turn % 2
            self.fresh_turn += 1
            tmp = self.fresh[:, f]
            for a in range(nt):
                g = gain[:, j + a:j + a + 1]
                if bias is None:
                    m1 = self.dve([m, *self.fresh_busy[f]], lambda e: e.tensor_scalar(
                        tmp[:, a, :], out[:, a, :], g, None, ALU.mult))
                else:
                    m1 = self.dve([m, *self.fresh_busy[f]], lambda e: e.tensor_scalar(
                        tmp[:, a, :], out[:, a, :], g, bias[:, j + a:j + a + 1], ALU.mult, ALU.add))
            self.bank_free[k] = [m1]
            m2 = self.split_out(dst, slice(tile0 + j, tile0 + j + nt), tmp[:, 0:nt, :], [m1])
            self.fresh_busy[f] = [m2]
        return m2 if gain is not None else m

    def rsqrt(self, src, col, eps, after):
        r = self.norm[:, col:col + 2]
        m = self.dve(after, lambda e: e.tensor_scalar(r, src, eps, None, ALU.add))
        return self.pool([m, self.half_neg], lambda e: e.tensor_tensor(r, r, self.eps_pow[:], ALU.pow))

    def feature_out(self, out, unit, x, x0=0):
        hi, lo = unit
        n = hi.shape[1]
        for k in range(n):
            ins = product(self.nc, out, (hi[:, k, :], lo[:, k, :]),
                          (x.hi[:, x0 + k, :], x.lo[:, x0 + k, :]), k == 0, k == n - 1)
        return ins

    def token_out(self, outs, units, x, ktiles):
        self.pe.wait(*x.ready)
        k0 = 0
        for src in units:
            hi, lo = self.w.take(src)
            kn = hi.shape[1]
            for b in range(TB):
                tb = slice(b * P, (b + 1) * P)
                for k in range(kn):
                    ins = product(self.nc, outs[b], (x.hi[:, k0 + k, tb], x.lo[:, k0 + k, tb]),
                                  (hi[:, k, :], lo[:, k, :]), k0 + k == 0, k0 + k == ktiles - 1)
            k0 += kn
            m = self.w.used.up(ins)
        x.busy = [m]
        return m

    def project_features(self, w, col0, tiles, dst, x, scale=None):
        self.pe.wait(*x.ready)
        marks = []
        for j in range(0, tiles, 2):
            nt = min(2, tiles - j)
            k = self.bank()
            out = self.psum[:, k, :].rearrange("p (a n) -> p a n", a=2)
            for a in range(nt):
                c = col0 + (j + a) * P
                unit = self.w.take(rows(w)[:, :, c:c + P])
                m = self.w.used.up(self.feature_out(out[:, a, :], unit, x))
            d = dst[:, j:j + nt, :]
            if scale is None:
                m1 = self.act([m], lambda e: e.copy(d, out[:, 0:nt, :]))
            else:
                m1 = self.act([m], lambda e: e.activation(d, out[:, 0:nt, :], ACT.Copy, scale=scale))
            self.bank_free[k] = [m1]
        x.busy = [m]
        return m1

    def project_tokens(self, w, col0, n, x):
        kn = 2 if n > 256 else 4 if n > P else KT
        ks = [self.bank() for _ in range(TB)]
        outs = [self.psum[:, k, 0:n] for k in ks]
        units = [rows(w)[:, j:j + kn, col0:col0 + n] for j in range(0, KT, kn)]
        m = self.token_out(outs, units, x, KT)
        return ks, outs, m

    def out_project(self, w, x):
        for c in range(2):
            for b in range(TB):
                self.pe.wait(*self.bank_free[2 * b + c])
            units = [rows(w)[:, j:j + 2, c * BANK:(c + 1) * BANK] for j in range(0, KT, 2)]
            m = self.token_out([self.psum[:, 2 * b + c, :] for b in range(TB)], units, x, KT)
        return m

    def acc(self, b):
        return self.psum[:, 2 * b:2 * b + 2, :]

    def rope(self, src, heads, b, dst, after):
        src = src.rearrange("p (h d) -> p h d", d=HD)
        cos = self.rope_cos[:, b, :].unsqueeze(1).broadcast_to([P, heads, HD])
        sin = self.rope_sin[:, b, :].unsqueeze(1).broadcast_to([P, heads, HD])
        swap = self.swap[:, 0:heads * HD].rearrange("p (h d) -> p h d", d=HD)
        h = HD // 2
        self.dve(after, lambda e: e.tensor_tensor(dst, src, cos, ALU.mult))
        self.dve(self.swap_busy, lambda e: e.tensor_tensor(swap[:, :, 0:h], src[:, :, h:HD], sin[:, :, 0:h],
                                                           ALU.mult))
        m = self.dve([], lambda e: e.tensor_tensor(swap[:, :, h:HD], src[:, :, 0:h], sin[:, :, h:HD], ALU.mult))
        done = self.dve([m], lambda e: e.tensor_tensor(dst, dst, swap, ALU.add))
        self.swap_busy = [done]
        return m, done

    def turn_tokens(self, src, ntiles, dst, after):
        for j in range(0, ntiles, 2):
            nt = min(2, ntiles - j)
            k = self.bank()
            out = self.psum[:, k, :].rearrange("p (a n) -> p a n", a=2)
            self.pe.wait(*after)
            for a in range(nt):
                for b in range(TB):
                    ins = self.nc.tensor.transpose(out[:, a, b * P:(b + 1) * P], src(b, j + a), self.ident[:])
            m = self.pe.done.up(ins)
            m1 = self.act([m], lambda e: e.copy(dst[:, j:j + nt, :], out[:, 0:nt, :]))
            self.bank_free[k] = [m1]
        self.tok_busy = [m]
        return m1

    def attend(self, groups, per, score, value, dst, ready, scale=1.0, mask=False, row_add=None,
               sink=None):
        pending = None
        self.pe.wait(*ready)
        if mask:
            self.dve.wait(self.mask_in)
        pt_busy = [[], []]
        for g in range(len(groups) + 1):
            if g < len(groups):
                s, (heads, tiles) = g % 2, groups[g]
                n = per * TB
                mx, nm, sm, rs = (self.stat[:, s, q, 0:n] for q in range(4))
                ms = []
                for i, h in enumerate(heads):
                    k = self.bank(wide=True)
                    out = self.psum[:, k, :].rearrange("p (b n) -> p b n", b=TB)
                    m = self.pe.done.up(score(h, out))
                    src = out
                    if mask:
                        e = self.e[:, s, i]
                        if row_add is None:
                            m = self.dve([m], lambda v: v.scalar_tensor_tensor(
                                e, out, scale, self.mask[:], ALU.mult, ALU.add))
                        else:
                            for b in range(TB):
                                m = self.dve([m], lambda v: v.scalar_tensor_tensor(
                                    e[:, b, :], out[:, b, :], row_add(h, b), self.mask[:, b, :],
                                    ALU.add, ALU.add))
                        self.bank_free[k] = [m]
                        src = e
                    m = self.dve([m], lambda v: v.tensor_reduce(mx[:, TB * i:TB * i + TB], src, AX, ALU.max))
                    ms.append((src, k))
                if sink is not None:
                    h0 = heads[0] * TB
                    m = self.dve([m], lambda v: v.tensor_tensor(mx, mx, sink[:, h0:h0 + n], ALU.max))
                m = self.dve([m], lambda v: v.tensor_scalar(
                    nm, mx, -(1.0 if mask else scale), None, ALU.mult))
                nm_done = m
                if sink is not None:
                    es = self.small[:, s, 0:n]
                    m = self.dve([m], lambda v: v.tensor_tensor(es, nm, sink[:, h0:h0 + n], ALU.add))
                    es_done = self.act([m], lambda v: v.activation(es, es, ACT.Exp))
                for i, (src, k) in enumerate(ms):
                    for b in range(TB):
                        m = self.act([nm_done], lambda v: v.activation(
                            self.e[:, s, i, b, :], src[:, b, :], ACT.Exp,
                            bias=nm[:, TB * i + b:TB * i + b + 1], scale=1.0 if mask else scale,
                            accum_out=sm[:, TB * i + b:TB * i + b + 1]))
                    if not mask:
                        self.bank_free[k] = [m]
                cur = (s, heads, tiles, sm, rs, [m])
                if sink is not None:
                    m = self.dve([m, es_done], lambda v: v.tensor_tensor(sm, sm, es, ALU.add))
                    cur = (s, heads, tiles, sm, rs, [m])
            else:
                cur = None
            if pending is not None:
                s, heads, tiles, sm, rs, after = pending
                m = self.dve(after, lambda v: v.reciprocal(rs, sm))
                for i in range(len(heads)):
                    for b in range(TB):
                        e = self.e[:, s, i, b, :]
                        mn = self.dve([m], lambda v: v.tensor_scalar(
                            e, e, rs[:, TB * i + b:TB * i + b + 1], None, ALU.mult))
                for i, h in enumerate(heads):
                    k = self.bank(wide=True)
                    out = self.psum[:, k, :].rearrange("p (c n) -> p c n", c=TB)
                    self.pe.wait(mn)
                    for c in range(TB):
                        for b in range(TB):
                            ins = self.nc.tensor.transpose(
                                out[:, c, b * P:(b + 1) * P],
                                self.e[:, s, i, b, c * P:(c + 1) * P], self.ident[:])
                    m = self.pe.done.up(ins)
                    mt = self.act([m, *pt_busy[s]], lambda v: v.copy(self.pt[:, s, i], out))
                    self.bank_free[k] = [mt]
                k = self.bank(wide=True)
                out = self.psum[:, k, :].rearrange("p (a n) -> p a n", a=2)
                self.pe.wait(mt)
                for i, h in enumerate(heads):
                    for slot, p0, width, vals in value(h):
                        for c in range(TB):
                            ins = self.nc.tensor.matmul(out[p0:p0 + width, slot, :], vals(c),
                                                        self.pt[:, s, i, c, :],
                                                        start=c == 0, stop=c == TB - 1)
                m = self.pe.done.up(ins)
                pt_busy[s] = [m]
                nt = tiles.stop - tiles.start
                self.bank_free[k] = [self.split_out(dst, tiles, out[:, 0:nt, :], [m])]
            pending = cur
        return m


    def residual_norm(self, l, k, last=False):
        t, idx = self.t, l * 3 + k
        ld1 = self.load(self.gain_row[:], t["ln_g"][l, k].partition_broadcast(P), self.row_busy)
        ld2 = self.load(self.bias_row[:], t["ln_b"][l, k].partition_broadcast(P), [])
        stats = self.small[:, 2:4, 0:12]
        mv = self.norm[:, 0:4].rearrange("p (b s) -> p b s", b=TB)
        acc_done = self.w.used.now()
        for b in range(TB):
            z = self.n_tok[:, b, :]
            m = self.dve([acc_done, *self.x_ready, *self.n_busy], lambda e: e.scalar_tensor_tensor(
                z, self.x_tok[:, b, :], ALPHA, self.acc(b).rearrange("p a n -> p (a n)"),
                ALU.mult, ALU.add))
            for c in range(2):
                m1 = self.dve([m], lambda e: e.bn_stats(stats[:, b, 6 * c:6 * c + 6],
                                                       z[:, c * BANK:(c + 1) * BANK]))
            m2 = self.dve([m1], lambda e: e.bn_aggr(mv[:, b, :], stats[:, b, :]))
        self.bank_free[0] = self.bank_free[1] = self.bank_free[2] = self.bank_free[3] = [m]
        r = self.rsqrt(mv[:, :, 1], 4, LN_EPS, [m2])
        for b in range(TB):
            z = self.n_tok[:, b, :]
            mz = self.dve([r, m2], lambda e: e.tensor_scalar(
                z, z, mv[:, b, 0:1], self.norm[:, 4 + b:5 + b], ALU.subtract, ALU.mult))
        for b in range(TB):
            z, x = self.n_tok[:, b, :], self.x_tok[:, b, :]
            m = self.pool([mz, ld1, ld2], lambda e: e.tensor_tensor(x, z, self.gain_row[:], ALU.mult))
            m = self.pool([m], lambda e: e.tensor_tensor(x, x, self.bias_row[:], ALU.add))
        self.x_ready = self.row_busy = [m]
        self.n_busy = [m]
        if not last:
            self.to_features(lambda b, j: self.n_tok[:, b, j * P:(j + 1) * P], KT, self.xt, 0, [mz],
                             self.cols("ln_g", idx * KT, KT), self.cols("ln_b", idx * KT, KT))
            self.n_busy = [m, self.pe.done.now()]

    def rms(self, src, width, dst, after, col, busy=()):
        for b in range(TB):
            m = self.act([*after, *busy], lambda e: e.activation(
                dst(b), src(b), ACT.Square, accum_out=self.norm[:, col + b:col + b + 1]))
        m = self.dve([m], lambda e: e.tensor_scalar(
            self.norm[:, col:col + 2], self.norm[:, col:col + 2], 1.0 / width, None, ALU.mult))
        r = self.rsqrt(self.norm[:, col:col + 2], col + 2, RMS_EPS, [m])
        for b in range(TB):
            m = self.dve([r], lambda e: e.tensor_scalar(
                dst(b), src(b), self.norm[:, col + 2 + b:col + 3 + b], None, ALU.mult))
        return m

    def log1p(self, e, s, w, after):
        m = self.dve(after, lambda v: v.tensor_scalar(w, e, 2.0, None, ALU.add))
        m = self.dve([m], lambda v: v.reciprocal(w, w))
        m = self.dve([m], lambda v: v.tensor_tensor(s, e, w, ALU.mult))
        m = self.dve([m], lambda v: v.tensor_tensor(w, s, s, ALU.mult))
        m = self.dve([m], lambda v: v.tensor_scalar(e, w, 1.0 / 15, None, ALU.mult))
        for c in (13, 11, 9, 7, 5, 3):
            m = self.dve([m], lambda v: v.scalar_tensor_tensor(e, e, 1.0 / c, w, ALU.add, ALU.mult))
        m = self.dve([m], lambda v: v.scalar_tensor_tensor(s, e, 1.0, s, ALU.add, ALU.mult))
        return self.dve([m], lambda v: v.tensor_scalar(s, s, 2.0, None, ALU.mult))


    def mem_keys_values(self):
        t = self.t
        m = self.load(self.tok[:], rows(t["mem"]))
        self.x_ready = [self.load(self.x_tok[:], rows(t["x"]))]
        self.params()
        self.to_features(lambda b, j: self.tok[:, b, j * P:(j + 1) * P], KT, self.xt, 0, [m])
        self.tok_busy = [self.pe.done.now()]
        m = self.project_features(t["mem_w_kv"], 0, KT, self.mem_kt, self.xt)
        for c in range(2):
            ks, outs, m = self.project_tokens(t["mem_w_kv"], D + c * BANK, BANK, self.xt)
            for b in range(TB):
                m1 = self.act([m], lambda e: e.copy(self.mem_v[:, b, c * BANK:(c + 1) * BANK], outs[b]))
                self.bank_free[ks[b]] = [m1]
        self.mem_ready = m1

    def load_mask(self, name):
        self.mask_in = self.load(self.mask[:], rows(self.t[name]), [self.dve.done.now()])

    def sliding_attention(self, j):
        t, nc = self.t, self.nc
        w = t["a_w_qkv"][j]
        self.load_mask("c_mask_window")
        m = self.load(self.small[:, 4, 0:A_HEADS], t["a_sinks"][j].partition_broadcast(P))
        sink = self.qrt[:, 0, 0:A_HEADS * TB]
        self.dve([m], lambda e: e.tensor_copy(
            sink.rearrange("p (h b) -> p h b", b=TB),
            self.small[:, 4, 0:A_HEADS].unsqueeze(2).broadcast_to([P, A_HEADS, TB])))
        heads = BANK // HD
        for c in range(2):
            ks, outs, m = self.project_tokens(w, c * BANK, BANK, self.xt)
            for b in range(TB):
                read, done = self.rope(outs[b], heads, b, self.tok[:, b, 0:BANK].rearrange(
                    "p (h d) -> p h d", d=HD), [m, *self.tok_busy])
                self.bank_free[ks[b]] = [read]
            self.turn_tokens(lambda b, i: self.tok[:, b, i * P:(i + 1) * P], 4,
                             self.qt[:, 4 * c:4 * c + 4, :], [done])
        kw = A_KV * HD
        ks, outs, m = self.project_tokens(w, 2 * BANK, BANK, self.xt)
        for b in range(TB):
            keys = self.tok[:, b, 0:2 * kw].rearrange("p (h c d) -> p h c d", c=2, d=HD)
            read, done = self.rope(outs[b][:, 0:kw], A_KV, b, keys[:, :, 0, :], [m, *self.tok_busy])
            done = self.dve([done], lambda e: e.tensor_copy(keys[:, :, 1, :], keys[:, :, 0, :]))
            m1 = self.act([read], lambda e: e.copy(self.v[:, b, 0:kw], outs[b][:, kw:2 * kw]))
            self.bank_free[ks[b]] = [m1]
        m = self.turn_tokens(lambda b, i: self.tok[:, b, i * P:(i + 1) * P], A_KV, self.kt, [done])

        def score(h, out):
            p0, n = (h % 2) * HD, h // (A_HEADS // A_KV)
            for b in range(TB):
                ins = nc.tensor.matmul(out[:, b, :], self.qt[p0:p0 + HD, h // 2, b * P:(b + 1) * P],
                                       self.kt[p0:p0 + HD, n, :], start=True, stop=True)
            return ins

        def value(h):
            n = h // (A_HEADS // A_KV)
            return [(0, (h % 2) * HD, HD, lambda c: self.v[:, c, n * HD:(n + 1) * HD])]

        self.attend([([2 * g, 2 * g + 1], slice(g, g + 1)) for g in range(A_HEADS // 2)], 2,
                    score, value, self.xt, [m, m1], HD ** -0.5, mask=True, sink=sink)
        self.out_project(t["a_w_o"][j], self.xt)

    def recurrent_block(self):
        t, nc = self.t, self.nc
        w, lru = t["b_w_in"][0], lambda off, n=1: self.cols("lru", off, n)
        conv_b, b_r, b_i, lam = (LRU_TAPS * KT + q * KT for q in range(4))
        gate, u = self.qt, self.kt
        r = self.v[:].rearrange("p b (j n) -> p (b j) n", n=SEQ)
        ig = self.e[:].rearrange("p a b c n -> p (a b c) n")
        ab, sp, w8, pos, neg = (self.small[:, q, 0:KT] for q in (0, 1, 5, 6, 7))
        lm = lru(lam, KT)
        m = self.dve([], lambda e: e.scalar_tensor_tensor(ab, lm, -1.0, lm, ALU.mult, ALU.max))
        m = self.act([m], lambda e: e.activation(ab, ab, ACT.Exp, scale=-1.0))
        m = self.log1p(ab, sp, w8, [m])
        self.dve([], lambda e: e.tensor_scalar(pos, lm, -1.0, 0.0, ALU.mult, ALU.max))
        m = self.dve([m, self.dve.done.now()], lambda e: e.tensor_tensor(sp, sp, pos, ALU.add))
        m = self.dve([m], lambda e: e.tensor_scalar(pos, sp, LRU_C, None, ALU.mult))
        lam_done = self.dve([m], lambda e: e.tensor_scalar(neg, sp, -LRU_C, None, ALU.mult))
        self.pe.wait(*self.xt.ready)
        for j in range(2 * KT):
            k = self.bank()
            out = self.psum[:, k, 0:SEQ]
            unit = self.w.take(rows(w)[:, :, j * P:(j + 1) * P])
            m = self.w.used.up(self.feature_out(out, unit, self.xt))
            if j < KT:
                m = self.act([m], lambda e: e.activation(gate[:, j, :], out, ACT.Gelu_apprx_tanh))
            else:
                i = j - KT
                tap = lambda q: lru(q * KT + i)
                m = self.act([m], lambda e: e.activation(u[:, i, :], out, ACT.Identity,
                                                         scale=tap(LRU_TAPS - 1), bias=lru(conv_b + i)))
                for d in range(1, LRU_TAPS):
                    m = self.dve([m], lambda e: e.scalar_tensor_tensor(
                        u[:, i, d:SEQ], out[:, 0:SEQ - d], tap(LRU_TAPS - 1 - d), u[:, i, d:SEQ],
                        ALU.mult, ALU.add))
            self.bank_free[k] = [m]
        self.xt.busy = [self.w.used.now()]
        self.split_out(self.xt, slice(0, KT), u[:], [m])
        self.pe.wait(*self.xt.ready)
        for name, dst, bias in (("b_w_rgate", r, b_r), ("b_w_igate", ig, b_i)):
            wg = t[name][0].rearrange("h (k p) n -> p (h k) n", p=P)
            for half in range(2):
                hi, lo = self.w.take(wg[:, 4 * half:4 * half + 4, :])
                for blk in range(2):
                    k = self.bank()
                    out = self.psum[:, k, :].rearrange("p (a n) -> p a n", a=2)
                    for a in range(2):
                        for q in range(2):
                            kt = 4 * half + 2 * blk + q
                            cs = slice(a * P, (a + 1) * P)
                            ins = product(nc, out[:, a, :], (hi[:, 2 * blk + q, cs], lo[:, 2 * blk + q, cs]),
                                          (self.xt.hi[:, kt, :], self.xt.lo[:, kt, :]), q == 0, q == 1)
                    m = self.w.used.up(ins) if blk == 1 else self.pe.done.up(ins)
                    for a in range(2):
                        jt = 4 * half + 2 * blk + a
                        m1 = self.act([m], lambda e: e.activation(dst[:, jt, :], out[:, a, :], ACT.Sigmoid,
                                                                  bias=lru(bias + jt)))
                    self.bank_free[k] = [m1]
        self.xt.busy = [self.w.used.now()]
        gates = m1
        th = self.pt[:].rearrange("p a b c n -> p (a b c) n")
        for j in range(KT):
            mt = self.act([gates, lam_done], lambda e: e.activation(th[:, j, :], r[:, j, :], ACT.Tanh,
                                                                    scale=pos[:, j:j + 1]))
        for j in range(KT):
            ma = self.act([mt], lambda e: e.activation(r[:, j, :], r[:, j, :], ACT.Exp, scale=neg[:, j:j + 1]))
        m = self.dve([gates], lambda e: e.tensor_tensor(ig, ig, u[:], ALU.mult))
        m = self.dve([mt, m], lambda e: e.tensor_scalar(u[:], th, 1.0, None, ALU.add))
        m = self.dve([m], lambda e: e.reciprocal(u[:], u[:]))
        m = self.dve([m], lambda e: e.tensor_tensor(th, th, u[:], ALU.mult))
        m = self.act([m], lambda e: e.activation(th, th, ACT.Sqrt, scale=2.0))
        m = self.dve([m], lambda e: e.tensor_tensor(th, th, ig, ALU.mult))
        for j in range(KT):
            m1 = self.dve([m, ma], lambda e: e.tensor_tensor_scan(u[:, j, :], r[:, j, :], th[:, j, :], 0.0,
                                                                  ALU.mult, ALU.add))
        m = self.dve([m1], lambda e: e.tensor_tensor(u[:], u[:], gate[:], ALU.mult))
        self.split_out(self.xt, slice(0, KT), u[:], [m])
        self.out_project(t["b_w_o"][0], self.xt)

    def latent_attention(self):
        t, nc = self.t, self.nc
        self.load_mask("c_mask_causal")
        w = rows(t["c_w_down"][0])
        width = C_QR + C_KVR + C_ROPE
        for col, n in ((0, 512), (512, width - 512)):
            ks, outs, m = self.project_tokens(t["c_w_down"][0], col, n, self.xt)
            for b in range(TB):
                m1 = self.act([m, *self.tok_busy], lambda e: e.copy(self.tok[:, b, col:col + n], outs[b]))
                self.bank_free[ks[b]] = [m1]
        self.tok_busy = []
        off = LRU_TAPS * KT + 4 * KT
        lat = lambda c0, n: (lambda b: self.tok[:, b, c0:c0 + n])
        dst = lambda c0, n: (lambda b: self.n_tok[:, b, c0:c0 + n])
        m = self.rms(lat(0, C_QR), C_QR, dst(0, C_QR), [m1], 8, self.n_busy)
        m = self.rms(lat(C_QR, C_KVR), C_KVR, dst(C_QR, C_KVR), [m1], 12)
        self.to_features(lambda b, j: self.n_tok[:, b, j * P:(j + 1) * P], 3, self.xt, 0, [m],
                         self.cols("lru", off, 3))
        self.to_features(lambda b, j: self.n_tok[:, b, C_QR + j * P:C_QR + (j + 1) * P], 2, self.xt, 3, [m],
                         self.cols("lru", off + 3, 2))
        self.n_busy = [*self.n_busy, self.pe.done.now()]
        kr = self.tok[:, :, 768:896].rearrange("p b (c d) -> p b c d", c=2)
        for b in range(TB):
            _, done = self.rope(self.tok[:, b, C_QR + C_KVR:width], 1, b, kr[:, b, 0:1, :], [m1])
            done = self.dve([done], lambda e: e.tensor_copy(kr[:, b, 1, :], kr[:, b, 0, :]))
        self.turn_tokens(lambda b, i: self.tok[:, b, 768:896], 1, self.krt[:].unsqueeze(1), [done])
        hw = C_NOPE + C_ROPE
        wq = rows(t["c_w_uq"][0])
        self.pe.wait(*self.xt.ready)
        for g in range(C_HEADS // 2):
            kf, k = self.bank(), self.bank()
            flat = self.psum[:, kf, :].rearrange("p (a n) -> p a n", a=2)
            out = self.psum[:, k, :].rearrange("p (b n) -> p b n", b=TB)
            for a in range(2):
                h = 2 * g + a
                hi, lo = self.w.take(wq[:, :, h * hw:(h + 1) * hw])
                self.feature_out(flat[:, a, :], (hi[:, :, 0:C_NOPE], lo[:, :, 0:C_NOPE]), self.xt)
                for b in range(TB):
                    tb = slice(b * P, (b + 1) * P)
                    for q in range(3):
                        ins = product(nc, out[:, b, a * C_ROPE:(a + 1) * C_ROPE],
                                      (self.xt.hi[:, q, tb], self.xt.lo[:, q, tb]),
                                      (hi[:, q, C_NOPE:hw], lo[:, q, C_NOPE:hw]), q == 0, q == 2)
                m = self.w.used.up(ins)
            m1 = self.act([m], lambda e: e.copy(self.qt[:, 2 * g:2 * g + 2, :], flat))
            self.bank_free[kf] = [m1]
            qr = self.tok[:, :, g * P:(g + 1) * P]
            for b in range(TB):
                read, done = self.rope(out[:, b, 0:P], 2, b, qr[:, b, :].rearrange("p (h d) -> p h d", h=2),
                                       [m])
            self.bank_free[k] = [read]
        self.turn_tokens(lambda b, i: self.tok[:, b, i * P:(i + 1) * P], C_HEADS // 2, self.qrt, [done])
        kvw = C_NOPE + C_V
        wkv = rows(t["c_w_ukv"][0])
        for g in range(C_HEADS // 2):
            hi, lo = self.w.take(wkv[:, :, g * 2 * kvw:(g + 1) * 2 * kvw])
            k = self.bank()
            out = self.psum[:, k, :].rearrange("p (a n) -> p a n", a=2)
            for a in range(2):
                cs = slice(a * kvw, a * kvw + C_NOPE)
                ins = self.feature_out(out[:, a, :], (hi[:, :, cs], lo[:, :, cs]), self.xt, 3)
            m = self.pe.done.up(ins)
            m1 = self.act([m], lambda e: e.copy(self.kt[:, 2 * g:2 * g + 2, :], out))
            self.bank_free[k] = [m1]
            k = self.bank()
            out = self.psum[:, k, :].rearrange("p (b n) -> p b n", b=TB)
            part = lambda a, q: a[:, q, :].rearrange("p (h d) -> p h d", h=2)[:, :, C_NOPE:kvw]
            for b in range(TB):
                tb = slice(b * P, (b + 1) * P)
                for q in range(2):
                    ins = product(nc, out[:, b, :].rearrange("p (h d) -> p h d", h=2),
                                  (self.xt.hi[:, 3 + q, tb], self.xt.lo[:, 3 + q, tb]),
                                  (part(hi, q), part(lo, q)), q == 0, q == 1)
            m = self.w.used.up(ins)
            m1 = self.act([m], lambda e: e.copy(self.v[:, :, g * 2 * C_V:(g + 1) * 2 * C_V], out))
            self.bank_free[k] = [m1]
        self.xt.busy = [m]

        def score(h, out):
            p0 = (h % 2) * C_ROPE
            for b in range(TB):
                tb = slice(b * P, (b + 1) * P)
                nc.tensor.matmul(out[:, b, :], self.qt[:, h, tb], self.kt[:, h, :], start=True, stop=False)
                ins = nc.tensor.matmul(out[:, b, :], self.qrt[p0:p0 + C_ROPE, h // 2, tb],
                                       self.krt[p0:p0 + C_ROPE, :], start=False, stop=True)
            return ins

        self.attend([([2 * g, 2 * g + 1], slice(2 * g, 2 * g + 2)) for g in range(C_HEADS // 2)], 2, score,
                    lambda h: [(h % 2, 0, C_V, lambda c: self.v[:, c, h * C_V:(h + 1) * C_V])],
                    self.xt, [m1], (C_NOPE + C_ROPE) ** -0.5, mask=True)
        self.out_project(t["c_w_o"][0], self.xt)

    def cross_attention(self, l):
        t, nc = self.t, self.nc
        m = self.project_features(t["x_w_q"][l], 0, KT, self.qt, self.xt)
        per_head = X_HD // P

        def score(h, out):
            for b in range(TB):
                for q in range(per_head):
                    ins = nc.tensor.matmul(out[:, b, :], self.qt[:, per_head * h + q, b * P:(b + 1) * P],
                                           self.mem_kt[:, per_head * h + q, :],
                                           start=q == 0, stop=q == per_head - 1)
            return ins

        def value(h):
            return [(q, 0, P, (lambda q: lambda c: self.mem_v[:, c, h * X_HD + q * P:h * X_HD + (q + 1) * P])(q))
                    for q in range(per_head)]

        self.attend([([h], slice(per_head * h, per_head * (h + 1))) for h in range(X_HEADS)], 1,
                    score, value, self.xt, [m, self.mem_ready], X_HD ** -0.5)
        self.out_project(t["x_w_o"][l], self.xt)

    def feed_forward(self, up, down, params, silu_half):
        nc, w, psum = self.nc, self.w, self.psum
        up, down = rows(up), rows(down)
        c0 = self.col[params]
        conv, act_out = self.qt, self.kt
        hid = self.hid
        for k in range(8):
            self.pe.wait(*self.bank_free[k])
        self.pe.wait(*self.xt.ready)
        zero = self.dve([], lambda e: e.memset(self.swap[:].bitcast(F32), 0.0))
        for k in range(4):
            self.pe.wait(zero)
            nc.tensor.matmul(psum[:, k, :], self.swap[:, 0:P], self.swap[:], start=True, stop=False,
                             skip_group_check=True)
        V, A = self.dve.done, self.act.done
        v0, a0 = V.n, A.n
        VT, AT = 6, 4

        def conv_tile(m, i):
            s = m % 2
            off = (lambda q: slice(c0 + q, c0 + q + 1)) if i is None else \
                  (lambda q: bass.ds(i * 2 + (c0 + q), 1))
            col = (lambda q: self.par[:, off(q)])
            out = psum[:, 4 + s, :].rearrange("p (a n) -> p a n", a=2)
            self.pe.wait(V.at(v0 + VT * (m - 2) + 4))
            for half in range(2):
                c = slice((half * FT + m) * P, (half * FT + m + 1) * P) if i is None else \
                    bass.ds(i * (2 * P) + (half * FT + m) * P, P)
                unit = w.take(up[:, :, c])
                made = w.used.up(self.feature_out(out[:, half, :], unit, self.xt))
            self.act.wait(made, V.at(v0 + VT * (m - 2) + 5))
            for half in range(2):
                t = half * FT + m
                base = self.act([], lambda e: e.activation(
                    conv[:, 2 * s + half, :], out[:, half, :], ACT.Identity,
                    scale=col((TAPS - 1) * 2 * FT + t), bias=col(TAPS * 2 * FT + t)))
            self.dve.wait(base)
            order = (silu_half, 1 - silu_half)
            for d in range(1, TAPS):
                for half in order:
                    t = half * FT + m
                    cv = conv[:, 2 * s + half, :]
                    self.dve([V.at(V.n - 1)] if d > 1 else [], lambda e: e.scalar_tensor_tensor(
                        cv[:, d:SEQ], out[:, half, 0:SEQ - d], col((TAPS - 1 - d) * 2 * FT + t),
                        cv[:, d:SEQ], ALU.mult, ALU.add))
            conv_done = V.now()
            sil, prod = act_out[:, s, :], act_out[:, 2 + s, :]
            ms = self.act([V.at(V.n - 1)], lambda e: e.activation(sil, conv[:, 2 * s + silu_half, :], ACT.Silu))
            mp = self.dve([ms, conv_done], lambda e: e.tensor_tensor(
                prod, sil, conv[:, 2 * s + 1 - silu_half, :], ALU.mult))
            hi, lo = hid.hi[:, s, :], hid.lo[:, s, :]
            mh = self.act([mp, made], lambda e: e.copy(hi, prod))
            return self.dve([mh], lambda e: e.tensor_tensor(lo, prod, hi.bitcast(F32), ALU.subtract))

        def down_tile(m, i, last=False):
            s = m % 2
            rowsel = slice(m, m + 1) if i is None else bass.ds(i * 2 + m, 1)
            hi, lo = w.take(down[:, rowsel, :])
            self.pe.wait(V.at(v0 + VT * (m + 1)))
            for b in range(TB):
                tb = slice(b * P, (b + 1) * P)
                for c in range(2):
                    cs = slice(c * BANK, (c + 1) * BANK)
                    mov = (hi[:, 0, cs], lo[:, 0, cs])
                    stat = (hid.hi[:, s, tb], hid.lo[:, s, tb])
                    for q, (x, y) in enumerate(((0, 0), (0, 1), (1, 0))):
                        ins = nc.tensor.matmul(psum[:, 2 * b + c, :], stat[x], mov[y], start=False,
                                               stop=last and q == 2, skip_group_check=True)
            return w.used.up(ins)

        self.act.wait(V.at(v0))
        conv_tile(0, None)
        per = w.counts(RING)
        per.update({V: 2 * VT, A: 2 * AT})
        with self.p.repeat((FT - 2) // 2, per) as i:
            for m in (1, 2):
                conv_tile(m, i)
                down_tile(m - 1, i)
        self.w.skip((FT - 2) // 2 * RING - RING)
        conv_tile(FT - 1, None)
        down_tile(FT - 2, None)
        m = down_tile(FT - 1, None, last=True)
        self.xt.busy = [m]
        for k in (4, 5):
            self.bank_free[k] = [V.now()]


    def norm_to_features(self, src, gain, after, busy=()):
        m = self.rms(lambda b: src[:, b, :], D, lambda b: self.n_tok[:, b, :], after, 8,
                     [*self.n_busy, *busy])
        self.to_features(lambda b, j: self.n_tok[:, b, j * P:(j + 1) * P], KT, self.xt, 0, [m], gain)
        self.n_busy = [self.pe.done.now()]

    def add_residual(self):
        acc_done = self.w.used.now()
        for b in range(TB):
            h = self.x_tok[:, b, :]
            m = self.dve([acc_done, *self.x_ready], lambda e: e.tensor_tensor(
                h, h, self.acc(b).rearrange("p a n -> p (a n)"), ALU.add))
        self.x_ready = [m]
        for k in range(4):
            self.bank_free[k] = [m]

    def second_memory(self, l):
        t = self.t
        w = t["w_mem_kv_2"][l]
        m = self.load(self.tok[:], rows(t["mem_2"]), [*self.tok_busy])
        self.norm_to_features(self.tok, self.cols("norms_2", (DEPTH_2 + l) * KT, KT), [m])
        self.tok_busy = [self.dve.done.now()]
        self.project_features(w, 0, D_MEMQ // P, self.mem_kt, self.xt)
        ks, outs, m = self.project_tokens(w, D_MEMQ, D_MEMQ, self.xt)
        for b in range(TB):
            m1 = self.act([m], lambda e: e.copy(self.mem_v[:, b, 0:D_MEMQ], outs[b]))
            self.bank_free[ks[b]] = [m1]
        self.mem_ready = m1

    def small_attention(self, heads, qt, kt, v, tile0, ready, **how):
        nc = self.nc
        extra = how.pop("extra", None)

        def score(h, out):
            p0 = (h % 2) * HD
            for b in range(TB):
                ins = nc.tensor.matmul(out[:, b, :], qt[p0:p0 + HD, h // 2, b * P:(b + 1) * P],
                                       kt[p0:p0 + HD, h // 2, :], start=True, stop=extra is None)
                if extra is not None:
                    ins = extra(h, p0, out[:, b, :])
            return ins

        self.attend([([2 * g, 2 * g + 1], slice(tile0 + g, tile0 + g + 1)) for g in range(heads // 2)], 2,
                    score, lambda h: [(0, (h % 2) * HD, HD, lambda c: v[:, c, h * HD:(h + 1) * HD])],
                    self.xt, ready, **how)

    def values_2(self, w, col0):
        for c, n in ((0, BANK), (BANK, D_MIX - BANK)):
            ks, outs, m = self.project_tokens(w, col0 + c, n, self.xt)
            for b in range(TB):
                m1 = self.act([m], lambda e: e.copy(self.v[:, b, c:c + n], outs[b]))
                self.bank_free[ks[b]] = [m1]
        return m1

    def forgetting_attention(self):
        t, nc = self.t, self.nc
        w = t["w_in_fox_2"][0]
        tiles = D_MIX // P
        self.load_mask("c_mask_causal")
        tri, ones = self.gain_row[:, 0:P], self.gain_row[:, P:2 * P]
        l0 = self.load(tri, t["c_triangle"], self.row_busy)
        l1 = self.load(self.small[:, 4, 0:MIX_HEADS], t["b_forget_2"][0].partition_broadcast(P))
        one = self.pool([], lambda e: e.memset(ones, 1.0))
        self.project_features(w, 0, tiles, self.qt, self.xt, scale=HD ** -0.5)
        self.project_features(w, D_MIX, tiles, self.kt, self.xt)
        self.values_2(w, 2 * D_MIX)
        ks, outs, m = self.project_tokens(w, 3 * D_MIX, MIX_HEADS, self.xt)
        z, ab, s, w8, neg, lf = (self.small[:, q, :] for q in (0, 1, 2, 3, 5, 6))
        H = MIX_HEADS
        for b in range(TB):
            m = self.dve([m, l1], lambda e: e.tensor_tensor(z[:, b * H:(b + 1) * H], outs[b],
                                                            self.small[:, 4, 0:H], ALU.add))
            self.bank_free[ks[b]] = [m]
        m = self.dve([m], lambda e: e.scalar_tensor_tensor(ab, z, -1.0, z, ALU.mult, ALU.max))
        m1 = self.dve([], lambda e: e.tensor_scalar(neg, z, 0.0, None, ALU.min))
        m = self.act([m], lambda e: e.activation(ab, ab, ACT.Exp, scale=-1.0))
        m = self.log1p(ab, s, w8, [m])
        m = self.dve([m, m1], lambda e: e.tensor_tensor(lf, neg, s, ALU.subtract))
        m2 = self.project_features(w, 3 * D_MIX + H, D_MEMQ // P, self.qrt, self.xt)
        k = self.bank()
        self.pe.wait(m, l0, one)
        out = self.psum[:, k, 0:2 * H]
        nc.tensor.matmul(out[:, 0:H], tri, lf[:, 0:H], start=True, stop=True)
        nc.tensor.matmul(out[:, H:2 * H], tri, lf[:, H:2 * H], start=True, stop=False)
        m = self.pe.done.up(nc.tensor.matmul(out[:, H:2 * H], ones, lf[:, 0:H], start=False, stop=True))
        csum = self.norm[:, 8:8 + 2 * H]
        m3 = self.dve([m], lambda e: e.tensor_copy(csum, out))
        neg_c = self.tok[:, :, 0:P]
        mz = self.dve([*self.tok_busy], lambda e: e.memset(neg_c, 0.0))
        for b in range(TB):
            for half in range(2):
                m4 = self.dve([mz, m3], lambda e: e.tensor_scalar(
                    neg_c[:, b, half * HD:half * HD + H], csum[:, b * H:(b + 1) * H], -1.0, None, ALU.mult))
        self.bank_free[k] = [m3]
        m = self.turn_tokens(lambda b, i: neg_c[:, b, :], 1, self.krt[:].unsqueeze(1), [m4])

        def minus_c(h, p0, out):
            return nc.tensor.matmul(out, self.ident[p0:p0 + HD, p0 + h:p0 + h + 1].broadcast_to([HD, P]),
                                    self.krt[p0:p0 + HD, :], start=False, stop=True)

        self.small_attention(MIX_HEADS, self.qt, self.kt, self.v, 0, [m, m2], mask=True, extra=minus_c,
                             row_add=lambda h, b: csum[:, b * H + h:b * H + h + 1])
        self.row_busy = [self.pe.done.now()]

    def dilated_attention(self):
        t = self.t
        w = t["w_in_dil_2"][0]
        self.load_mask("c_mask_dilated")
        for part, dst in ((0, self.qt), (1, self.kt)):
            for c, n in ((0, BANK), (BANK, D_MIX - BANK)):
                ks, outs, m = self.project_tokens(w, part * D_MIX + c, n, self.xt)
                for b in range(TB):
                    read, done = self.rope(outs[b], n // HD, b, self.tok[:, b, 0:n].rearrange(
                        "p (h d) -> p h d", d=HD), [m, *self.tok_busy])
                    self.bank_free[ks[b]] = [read]
                self.turn_tokens(lambda b, i: self.tok[:, b, i * P:(i + 1) * P], n // P,
                                 dst[:, c // P:(c + n) // P, :], [done])
        self.values_2(w, 2 * D_MIX)
        m = self.project_features(w, 3 * D_MIX, D_MEMQ // P, self.qrt, self.xt)
        self.small_attention(MIX_HEADS, self.qt, self.kt, self.v, 0, [m], scale=HD ** -0.5, mask=True)

    def build(self):
        t, p = self.t, self.p
        self.hid = Split(p, "hid", 2)
        self.mem_keys_values()
        self.turn_params()
        self.to_features(lambda b, j: self.x_tok[:, b, j * P:(j + 1) * P], KT, self.xt, 0, self.x_ready)
        self.x_ready.append(self.pe.done.now())
        kinds = [lambda j: self.sliding_attention(j), lambda j: self.recurrent_block(),
                 lambda j: self.latent_attention()]
        n = 0
        for l in range(DEPTH):
            kinds[l % 3](l // 3)
            self.residual_norm(l, 0)
            n += 1
            if n == self.stop:
                return self.finish(self.x_tok, self.x_ready)
            self.cross_attention(l)
            self.residual_norm(l, 1)
            n += 1
            if n == self.stop:
                return self.finish(self.x_tok, self.x_ready)
            self.feed_forward(t["f_w_up"][l], t["f_w_down"][l], ("f", l), 0)
            self.residual_norm(l, 2, last=l == DEPTH - 1)
            n += 1
            if n == self.stop:
                return self.finish(self.x_tok, self.x_ready)
        for l in range(DEPTH_2):
            self.second_memory(l)
            self.norm_to_features(self.x_tok, self.cols("norms_2", l * KT, KT), self.x_ready)
            if l % 2 == 0:
                self.forgetting_attention()
            else:
                self.dilated_attention()
            self.small_attention(MEM_HEADS, self.qrt, self.mem_kt, self.mem_v, D_MIX // P,
                                 [self.mem_ready], scale=HD ** -0.5)
            self.out_project(t["w_out_2"][l], self.xt)
            self.add_residual()
            n += 1
            if n == self.stop:
                return self.finish(self.x_tok, self.x_ready)
            self.norm_to_features(self.x_tok, self.cols("norms_2", (2 * DEPTH_2 + l) * KT, KT), self.x_ready)
            self.feed_forward(t["w_up_2"][l], t["w_down_2"][l], ("g", l), 1)
            self.add_residual()
            n += 1
            if n == self.stop:
                return self.finish(self.x_tok, self.x_ready)
        m0 = self.load(self.gain_row[:], t["norm_final_2"].partition_broadcast(P), self.row_busy)
        m = self.rms(lambda b: self.x_tok[:, b, :], D, lambda b: self.n_tok[:, b, :], self.x_ready, 8,
                     self.n_busy)
        for b in range(TB):
            z = self.n_tok[:, b, :]
            m1 = self.dve([m, m0], lambda e: e.tensor_tensor(z, z, self.gain_row[:], ALU.mult))
        self.finish(self.n_tok, [m1])

    def finish(self, src, after):
        self.units = self.w.next
        self.sp.wait(*after)
        m = self.stores.up(self.nc.sync.dma_start(rows(self.t["out"]), src[:]))
        self.sp.wait(m)


def two_stacks_kernel(nc, tensors, total_units, stop=None):
    with ExitStack() as ctx:
        t = dict(tensors)
        for name in ("x", "mem", "mem_2", "out"):
            t[name] = t[name].rearrange("a s d -> (a s) d")
        model = Model(nc, ctx, t, total_units, stop)
        model.build()
        return model.units


_INS = ["x", "mem", "a_w_qkv", "a_sinks", "a_w_o", "b_w_in", "b_conv_w", "b_conv_b", "b_w_rgate",
        "b_b_rgate", "b_w_igate", "b_b_igate", "b_lambda", "b_w_o", "c_w_down", "c_q_norm", "c_kv_norm",
        "c_w_uq", "c_w_ukv", "c_w_o", "mem_w_kv", "x_w_q", "x_w_o", "f_w_up", "f_conv_w", "f_conv_b",
        "f_w_down", "ln_g", "ln_b", "mem_2", "norm_mix_2", "norm_mem_2", "norm_ffn_2", "w_in_fox_2",
        "b_forget_2", "w_in_dil_2", "w_mem_kv_2", "w_out_2", "w_up_2", "conv_w_2", "conv_b_2",
        "w_down_2", "norm_final_2"]
UNITS = 635


def shape_constants():
    import numpy as np
    f = np.float32
    i, j = np.arange(SEQ)[:, None], np.arange(SEQ)[None, :]
    d = i - j
    inv = (f(1.0) / (f(10000.0) ** (np.arange(0, HD, 2, dtype=f) / f(HD)))).astype(f)
    ang = np.arange(SEQ, dtype=f)[:, None] * inv[None, :]
    cos, sin = np.cos(ang).astype(f), np.sin(ang).astype(f)
    neg = f(-1e30)
    count = ((d >= 0) & (d <= 128)).astype(int) + ((d >= 0) & (d % 4 == 0)) + ((d >= 0) & (d % 16 == 0))
    return {
        "c_ident": np.eye(P, dtype=f),
        "c_triangle": np.triu(np.ones((P, P), dtype=f)),
        "c_cos": np.concatenate([cos, cos], 1),
        "c_sin": np.concatenate([-sin, sin], 1),
        "c_mask_window": np.where((d >= 0) & (d < 128), f(0), neg).astype(f),
        "c_mask_causal": np.where(d >= 0, f(0), neg).astype(f),
        "c_mask_dilated": np.where(count > 0, np.log(np.maximum(count, 1)), neg).astype(f),
    }


def kernel(**inputs):
    import numpy as _np
    import concourse.bacc as _bacc
    from concourse import mybir as _mybir
    from concourse.bass_utils import run_bass_kernel_spmd as _run

    nc = _bacc.Bacc("TRN2", target_bir_lowering=False, num_devices=1)
    arrays, tensors = {}, {}
    for name, a in [(n, inputs[n]) for n in _INS] + list(shape_constants().items()):
        a = _np.ascontiguousarray(a)
        arrays[f"in_{name}_dram"] = a
        tensors[name] = nc.dram_tensor(f"in_{name}_dram", a.shape, _mybir.dt.from_np(a.dtype),
                                       kind="ExternalInput").ap()
    tensors["out"] = nc.dram_tensor("out_0_dram", (1, SEQ, D), F32, kind="ExternalOutput").ap()
    two_stacks_kernel(nc, tensors, UNITS)
    r = _run(nc, [arrays], core_ids=[0])
    return r.results[0]["out_0_dram"]
```

```python
from contextlib import ExitStack, contextmanager
import concourse.bass as bass
from concourse import mybir

F32 = mybir.dt.float32
F32R = mybir.dt.float32r
ACT = mybir.ActivationFunctionType
ALU = mybir.AluOpType
AX = mybir.AxisListType.X

P = 128
SEQ = 256
TB = SEQ // P
D = 1024
KT = D // P
DEPTH = 4
DEPTH_2 = 2
ALPHA = (2.0 * DEPTH) ** 0.25
LN_EPS = 1e-5
RMS_EPS = 1e-6
FF = 2816
FT = FF // P
TAPS = 3

A_HEADS, A_KV, HD = 16, 4, 64
C_HEADS, C_NOPE, C_ROPE, C_V, C_QR, C_KVR = 8, 128, 64, 128, 384, 256
X_HEADS, X_HD = 4, 256
LRU_TAPS, LRU_C = 4, 8.0
MIX_HEADS, MEM_HEADS = 12, 4
D_MIX, D_MEMQ = MIX_HEADS * HD, MEM_HEADS * HD

UNIT = 1024
RING = 6
AHEAD = 4
BANK = 512


class Count:

    def __init__(self, prog, name, by=1):
        self.prog, self.by, self.n = prog, by, 0
        self.sem = prog.ctx.enter_context(prog.nc.semaphore(name))

    def up(self, ins):
        ins.then_inc(self.sem, self.by)
        self.n += 1
        return self.now()

    def now(self):
        return (self, self.n, self.prog.loop is not None)

    def at(self, n):
        return (self, n, self.prog.loop is not None)


class Lane:

    def __init__(self, prog, eng, name):
        self.prog, self.eng = prog, eng
        self.done = Count(prog, name)
        self.seen = {}

    def wait(self, *marks):
        for m in marks:
            if isinstance(m, list):
                self.wait(*m)
                continue
            count, n, inside = m
            if n <= 0 and not inside:
                continue
            key = (count, inside)
            if self.seen.get(key, -1) >= n:
                continue
            self.seen[key] = n
            if inside:
                i, per = self.prog.loop
                self.eng.wait_ge(count.sem, i * (per[count] * count.by) + n * count.by)
            else:
                self.eng.wait_ge(count.sem, n * count.by)

    def __call__(self, after, issue):
        self.wait(*after)
        return self.done.up(issue(self.eng))


class Program:
    def __init__(self, nc, ctx):
        self.nc, self.ctx, self.loop = nc, ctx, None
        self.pe = Lane(self, nc.tensor, "pe_done")
        self.act = Lane(self, nc.scalar, "act_done")
        self.dve = Lane(self, nc.vector, "dve_done")
        self.pool = Lane(self, nc.gpsimd, "pool_done")
        self.sp = Lane(self, nc.sync, "sp_done")
        self.lanes = [self.pe, self.act, self.dve, self.pool, self.sp]

    @contextmanager
    def repeat(self, times, per):
        start = {c: c.n for c in per}
        for lane in self.lanes:
            lane.seen = {k: v for k, v in lane.seen.items() if not k[1]}
        with self.nc.Fori(0, times) as i:
            self.loop = (i, per)
            yield i
        self.loop = None
        for c, n in per.items():
            assert c.n - start[c] == n, (c.sem, c.n - start[c], n)
            c.n = start[c] + n * times
        for lane in self.lanes:
            lane.seen = {k: v for k, v in lane.seen.items() if not k[1]}

    def sbuf(self, name, shape, dt=F32):
        return self.ctx.enter_context(self.nc.sbuf_tensor(name, shape, dt))


class Split:

    def __init__(self, prog, name, tiles):
        self.hi = prog.sbuf(name + "_hi", [P, tiles, SEQ], F32R)
        self.lo = prog.sbuf(name + "_lo", [P, tiles, SEQ], F32R)
        self.ready, self.busy = [[]] * tiles, []


class WeightStream:

    def __init__(self, prog, total):
        self.prog, self.total = prog, total
        self.raw = prog.sbuf("w_raw", [P, RING, UNIT])
        self.hi = prog.sbuf("w_hi", [P, RING, UNIT], F32R)
        self.lo = prog.sbuf("w_lo", [P, RING, UNIT], F32R)
        self.landed = [Count(prog, f"w_landed{s}", 16) for s in range(RING)]
        self.hi_done = Count(prog, "w_hi_done")
        self.lo_done = Count(prog, "w_lo_done")
        self.used = Count(prog, "w_used")
        self.next = 0
        self.split_next = 0
        self.hold = None

    def counts(self, units):
        per = {c: units // RING for c in self.landed}
        per.update({self.hi_done: units, self.lo_done: units, self.used: units})
        return per

    def skip(self, units):
        self.next += units
        self.split_next += units

    def split(self):
        v, p = self.split_next, self.prog
        self.split_next += 1
        if v >= self.total and p.loop is None:
            return
        s = v % RING
        p.act.wait(self.landed[s].at(v // RING + 1), self.used.at(v - RING + 1))
        self.hi_done.up(p.nc.scalar.copy(self.hi[:, s, :], self.raw[:, s, :]))
        p.dve.wait(self.hi_done.at(v + 1))
        self.lo_done.up(p.nc.vector.tensor_tensor(
            self.lo[:, s, :], self.raw[:, s, :], self.hi[:, s, :].bitcast(F32), ALU.subtract))

    def catch_up(self):
        last = self.next - 1 + AHEAD
        if self.hold is not None:
            last = min(last, self.hold + RING - 1)
        while self.split_next <= last:
            self.split()

    def take(self, src):
        u, p = self.next, self.prog
        self.next += 1
        s, (_, k, n) = u % RING, src.shape
        p.sp.wait(self.lo_done.at(u - RING + 1))
        self.landed[s].up(p.nc.sync.dma_start(
            self.raw[:, s, 0:k * n].rearrange("p (k n) -> p k n", k=k), src))
        self.catch_up()
        p.pe.wait(self.lo_done.at(u + 1))
        return [t[:, s, 0:k * n].rearrange("p (k n) -> p k n", k=k) for t in (self.hi, self.lo)]


def product(nc, out, stat, mov, first, last):
    nc.tensor.matmul(out, stat[0], mov[0], start=first, stop=False)
    nc.tensor.matmul(out, stat[0], mov[1], start=False, stop=False)
    return nc.tensor.matmul(out, stat[1], mov[0], start=False, stop=last)


def rows(ap, n=P):
    return ap.rearrange("(k p) n -> p k n", p=n)


class Model:
    def __init__(self, nc, ctx, t, total):
        self.nc, self.t = nc, t
        p = self.p = Program(nc, ctx)
        self.pe, self.act, self.dve, self.pool, self.sp = p.pe, p.act, p.dve, p.pool, p.sp
        self.w = WeightStream(p, total)
        self.loads = [Count(p, f"load{i}", 16) for i in range(8)]
        self.load_turn = 0
        self.par_loads = Count(p, "parameter_loads", 16)
        self.const_loads = Count(p, "constant_loads", 16)
        self.stores = Count(p, "stores", 16)
        self.psum = ctx.enter_context(nc.psum_tensor("psum", [P, 8, BANK], F32))
        self.bank_free = [[] for _ in range(8)]
        self.turn = 0
        self.x_tok = p.sbuf("x_tok", [P, TB, D])
        self.n_tok = p.sbuf("n_tok", [P, TB, D])
        self.x_ready, self.n_busy = [], []
        self.xt = Split(p, "xt", KT)
        self.fresh = p.sbuf("fresh", [P, 2, 2, SEQ])
        self.fresh_busy = [[], []]
        self.fresh_turn = 0
        self.gain_row = p.sbuf("gain_row", [P, D])
        self.bias_row = p.sbuf("bias_row", [P, D])
        self.row_busy = []
        self.ident = p.sbuf("ident", [P, P])
        self.rope_cos = p.sbuf("rope_cos", [P, TB, HD])
        self.rope_sin = p.sbuf("rope_sin", [P, TB, HD])
        self.mask = p.sbuf("mask", [P, P + SEQ])
        self.mask_busy = []
        self.mem_kt = p.sbuf("mem_kt", [P, KT, SEQ])
        self.mem_v = p.sbuf("mem_v", [P, TB, D])
        self.qt = p.sbuf("qt", [P, KT, SEQ])
        self.kt = p.sbuf("kt", [P, KT, SEQ])
        self.v = p.sbuf("v", [P, TB, D])
        self.qrt = p.sbuf("qrt", [P, 4, SEQ])
        self.krt = p.sbuf("krt", [P, SEQ])
        self.e = p.sbuf("e", [P, 2, 2, TB * SEQ])
        self.pt = p.sbuf("pt", [P, 2, 2, TB * SEQ])
        self.tok = p.sbuf("tok", [P, TB, D])
        self.tok_busy = []
        self.swap = p.sbuf("swap", [P, BANK])
        self.swap_busy = []
        self.stat = p.sbuf("stat", [P, 2, 4, 4])
        self.norm = p.sbuf("norm", [P, 32])
        self.eps_pow = p.sbuf("eps_pow", [P, 2])
        self.small = p.sbuf("small", [P, 8, 24])
        self.zeros = p.sbuf("zeros", [P, BANK], F32R)
        self.zeros_done = self.dve([], lambda e: e.memset(self.zeros[:].bitcast(F32), 0.0))
        self.half_neg = self.pool([], lambda e: e.memset(self.eps_pow[:], -0.5))
        for dst, src in ((self.ident[:], t["c_ident"]), (self.rope_cos[:], rows(t["c_cos"])),
                         (self.rope_sin[:], rows(t["c_sin"]))):
            self.load(dst, src, (), self.const_loads)
        self.consts = self.const_loads.now()


    def load(self, dst, src, after=(), count=None):
        if count is None:
            count = self.loads[self.load_turn % len(self.loads)]
            self.load_turn += 1
            self.pool.wait(count.now())
        self.pool.wait(*after)
        with self.nc.allow_non_contiguous_dma(reason="small parameter"):
            ins = self.nc.gpsimd.dma_start(dst, src)
        return count.up(ins)

    def bank(self, wide=False):
        k = self.turn % 8 if wide else 4 + self.turn % 4
        self.turn += 1
        self.pe.wait(*self.bank_free[k])
        return k

    def params(self):
        t = self.t
        tile = lambda ap: ap.rearrange("t (m p) -> (t m) p", p=P)
        vec = lambda ap: ap.rearrange("(m p) -> m p", p=P)
        batches, self.col = [], {}
        half = (TAPS + 1) * 2 * FT // 2
        for name, w, b, depth in (("f", t["f_conv_w"], t["f_conv_b"], DEPTH),
                                  ("g", t["conv_w_2"], t["conv_b_2"], DEPTH_2)):
            for l in range(depth):
                taps = tile(w[l])
                batches.append(((name, l), [taps[0:half]]))
                batches.append((None, [taps[half:TAPS * 2 * FT], vec(b[l])]))
        batches.append(("ln_g", [tile(t["ln_g"].rearrange("l k n -> (l k) n"))]))
        batches.append(("ln_b", [tile(t["ln_b"].rearrange("l k n -> (l k) n"))]))
        batches.append(("norms_2", [tile(t["norm_mix_2"]), tile(t["norm_mem_2"]), tile(t["norm_ffn_2"])]))
        batches.append(("lru", [tile(t["b_conv_w"][0]), tile(t["b_conv_b"]), tile(t["b_b_rgate"]),
                                tile(t["b_b_igate"]), tile(t["b_lambda"]), tile(t["c_q_norm"]),
                                tile(t["c_kv_norm"])]))
        total = sum(a.shape[0] for _, parts in batches for a in parts)
        self.par = self.p.sbuf("par", [P, total])
        stage = self.e[:].rearrange("p a b n -> p (a b n)")
        self.par_jobs = []
        at = 0
        for j, (name, parts) in enumerate(batches):
            if name is not None:
                self.col[name] = at
            r = 0
            for a in parts:
                self.load(stage[r:r + a.shape[0], j * P:(j + 1) * P], a, (), self.par_loads)
                r += a.shape[0]
            self.par_jobs.append((stage[0:r, j * P:(j + 1) * P], r, at))
            at += r
        self.par_loaded = self.par_loads.now()

    def turn_params(self):
        for src, r, at in self.par_jobs:
            k = self.bank()
            m = self.pe([self.par_loaded, self.consts],
                        lambda e: e.transpose(self.psum[:, k, 0:r], src, self.ident[0:r, 0:r]))
            m = self.act([m], lambda e: e.copy(self.par[:, at:at + r], self.psum[:, k, 0:r]))
            self.bank_free[k] = [m]
        self.par_ready = m
        self.dve.wait(m)

    def cols(self, name, off, n):
        a = self.col[name] + off
        return self.par[:, a:a + n]

    def split_out(self, dst, tiles, src, after=(), scale=None):
        hi, lo = dst.hi[:, tiles, :], dst.lo[:, tiles, :]
        m = self.act([*after, *dst.busy], lambda e: e.copy(hi, src))
        m2 = self.dve([m], lambda e: e.tensor_tensor(lo, src, hi.bitcast(F32), ALU.subtract))
        for j in range(tiles.start, tiles.stop):
            dst.ready[j] = [m2]
        return m2

    def to_features(self, src, ntiles, dst, tile0, after, gain=None, bias=None):
        banks, marks = {}, {}
        for b in range(TB):
            self.pe.wait(self.consts)
            self.pe.wait(after[b])
            for j in range(ntiles):
                if j % 2 == 0 and b == 0:
                    banks[j] = self.bank()
                k = banks[j - j % 2]
                ins = self.nc.tensor.transpose(
                    self.psum[:, k, (j % 2) * SEQ + b * P:(j % 2) * SEQ + (b + 1) * P], src(b, j), self.ident[:])
                if b == TB - 1 and (j % 2 == 1 or j == ntiles - 1):
                    marks[j - j % 2] = self.pe.done.up(ins)
        scaled = None
        for j, m in marks.items():
            k, nt = banks[j], min(2, ntiles - j)
            out = self.psum[:, k, :].rearrange("p (a n) -> p a n", a=2)
            tiles = slice(tile0 + j, tile0 + j + nt)
            if gain is None:
                self.bank_free[k] = [self.split_out(dst, tiles, out[:, 0:nt, :], [m])]
                continue
            f = self.fresh_turn % 2
            self.fresh_turn += 1
            tmp = self.fresh[:, f]
            m1 = self.act([m, *self.fresh_busy[f]], lambda e: e.activation(
                tmp[:, 0, :], out[:, 0, :], ACT.Identity, scale=gain[:, j:j + 1],
                bias=0.0 if bias is None else bias[:, j:j + 1]))
            if nt == 2:
                g = gain[:, j + 1:j + 2]
                if bias is None:
                    m1 = self.dve([m1], lambda e: e.tensor_scalar(tmp[:, 1, :], out[:, 1, :], g, None, ALU.mult))
                else:
                    m1 = self.dve([m1], lambda e: e.tensor_scalar(
                        tmp[:, 1, :], out[:, 1, :], g, bias[:, j + 1:j + 2], ALU.mult, ALU.add))
            self.bank_free[k] = [m1]
            if scaled is not None:
                self.split_scaled(dst, *scaled)
            scaled = (f, tiles, nt, m1)
        if scaled is not None:
            self.split_scaled(dst, *scaled)

    def split_scaled(self, dst, f, tiles, nt, m):
        self.fresh_busy[f] = [self.split_out(dst, tiles, self.fresh[:, f, 0:nt, :], [m])]

    def rsqrt(self, src, col, eps, after):
        r = self.norm[:, col:col + 2]
        m = self.dve(after, lambda e: e.tensor_scalar(r, src, eps, None, ALU.add))
        return self.pool([m, self.half_neg], lambda e: e.tensor_tensor(r, r, self.eps_pow[:], ALU.pow))

    def feature_out(self, out, unit, x, x0=0):
        hi, lo = unit
        n = hi.shape[1]
        for k in range(n):
            self.pe.wait(x.ready[x0 + k])
            ins = product(self.nc, out, (hi[:, k, :], lo[:, k, :]),
                          (x.hi[:, x0 + k, :], x.lo[:, x0 + k, :]), k == 0, k == n - 1)
        return ins

    def token_out(self, outs, units, x, ktiles):
        k0 = 0
        for src in units:
            hi, lo = self.w.take(src)
            kn = hi.shape[1]
            for b in range(TB):
                tb = slice(b * P, (b + 1) * P)
                for k in range(kn):
                    self.pe.wait(x.ready[k0 + k])
                    ins = product(self.nc, outs[b], (x.hi[:, k0 + k, tb], x.lo[:, k0 + k, tb]),
                                  (hi[:, k, :], lo[:, k, :]), k0 + k == 0, k0 + k == ktiles - 1)
            k0 += kn
            m = self.w.used.up(ins)
        x.busy = [m]
        return m

    def project_features(self, w, col0, tiles, dst, x, scale=None):
        j0 = 0
        if w.shape[0] == D:
            ks = [self.bank(), self.bank()]
            units = [self.w.take(rows(w)[:, :, col0 + j * P:col0 + (j + 1) * P]) for j in range(2)]
            for k in range(KT):
                self.pe.wait(x.ready[k])
                for (hi, lo), b in zip(units, ks):
                    ins = product(self.nc, self.psum[:, b, 0:SEQ], (hi[:, k, :], lo[:, k, :]),
                                  (x.hi[:, k, :], x.lo[:, k, :]), k == 0, k == KT - 1)
                    if k == KT - 1:
                        m = self.w.used.up(ins)
                        d = dst[:, ks.index(b), :]
                        if scale is None:
                            m1 = self.act([m], lambda e: e.copy(d, self.psum[:, b, 0:SEQ]))
                        else:
                            m1 = self.act([m], lambda e: e.activation(d, self.psum[:, b, 0:SEQ], ACT.Copy,
                                                                      scale=scale))
                        self.bank_free[b] = [m1]
            j0 = 2
        for j in range(j0, tiles, 2):
            nt = min(2, tiles - j)
            k = self.bank()
            out = self.psum[:, k, :].rearrange("p (a n) -> p a n", a=2)
            for a in range(nt):
                c = col0 + (j + a) * P
                unit = self.w.take(rows(w)[:, :, c:c + P])
                m = self.w.used.up(self.feature_out(out[:, a, :], unit, x))
            d = dst[:, j:j + nt, :]
            if scale is None:
                m1 = self.act([m], lambda e: e.copy(d, out[:, 0:nt, :]))
            else:
                m1 = self.act([m], lambda e: e.activation(d, out[:, 0:nt, :], ACT.Copy, scale=scale))
            self.bank_free[k] = [m1]
        x.busy = [m]
        return m1

    def project_tokens(self, w, col0, n, x):
        kn = 2 if n > 256 else 4 if n > P else KT
        ks = [self.bank() for _ in range(TB)]
        outs = [self.psum[:, k, 0:n] for k in ks]
        units = [rows(w)[:, j:j + kn, col0:col0 + n] for j in range(0, KT, kn)]
        m = self.token_out(outs, units, x, KT)
        return ks, outs, m

    def out_project(self, w, x, part_done):
        half = lambda c: [rows(w)[:, j:j + 2, c * BANK:(c + 1) * BANK] for j in range(0, KT, 2)]
        for b in range(TB):
            self.pe.wait(*self.bank_free[2 * b])
        m = self.token_out([self.psum[:, 2 * b, :] for b in range(TB)], half(0), x, KT)
        for b in range(TB):
            self.pe.wait(*self.bank_free[2 * b + 1])
        self.w.hold = self.w.next
        for b in range(TB):
            part_done(b, 0, m)
        units = [self.w.take(src) for src in half(1)]
        for b in range(TB):
            tb = slice(b * P, (b + 1) * P)
            for k in range(KT):
                hi, lo = units[k // 2]
                ins = product(self.nc, self.psum[:, 2 * b + 1, :], (x.hi[:, k, tb], x.lo[:, k, tb]),
                              (hi[:, k % 2, :], lo[:, k % 2, :]), k == 0, k == KT - 1)
                if b == TB - 1 and k % 2 == 1:
                    m = self.w.used.up(ins)
            if b < TB - 1:
                m = self.pe.done.up(ins)
            part_done(b, 1, m)
        self.w.hold = None
        x.busy = [m]

    def rope(self, src, heads, b, dst, after):
        src = src.rearrange("p (h d) -> p h d", d=HD)
        cos = self.rope_cos[:, b, :].unsqueeze(1).broadcast_to([P, heads, HD])
        sin = self.rope_sin[:, b, :].unsqueeze(1).broadcast_to([P, heads, HD])
        swap = self.swap[:, 0:heads * HD].rearrange("p (h d) -> p h d", d=HD)
        h = HD // 2
        self.dve(after, lambda e: e.tensor_tensor(dst, src, cos, ALU.mult))
        self.dve(self.swap_busy, lambda e: e.tensor_tensor(swap[:, :, 0:h], src[:, :, h:HD], sin[:, :, 0:h],
                                                           ALU.mult))
        m = self.dve([], lambda e: e.tensor_tensor(swap[:, :, h:HD], src[:, :, 0:h], sin[:, :, h:HD], ALU.mult))
        done = self.dve([m], lambda e: e.tensor_tensor(dst, dst, swap, ALU.add))
        self.swap_busy = [done]
        return m, done

    def turn_half(self, half, ntiles, dst, done):
        m = self.turn_tokens(lambda b, i: self.tok[:, b, half * BANK + i * P:half * BANK + (i + 1) * P],
                             ntiles, dst, [done])
        self.tok_half_busy[half] = self.tok_busy
        return m

    def rotated(self, w, col, n, half, dst, waiting):
        ks, outs, m = self.project_tokens(w, col, n, self.xt)
        for b in range(TB):
            read, done = self.rope(outs[b], n // HD, b, self.tok[:, b, half * BANK:half * BANK + n].rearrange(
                "p (h d) -> p h d", d=HD), [m, *self.tok_half_busy[half]])
            self.bank_free[ks[b]] = [read]
        if waiting is not None:
            self.turn_half(*waiting)
        return (half, n // P, dst, done)

    def turn_tokens(self, src, ntiles, dst, after):
        for j in range(0, ntiles, 2):
            nt = min(2, ntiles - j)
            k = self.bank()
            out = self.psum[:, k, :].rearrange("p (a n) -> p a n", a=2)
            self.pe.wait(*after)
            for a in range(nt):
                for b in range(TB):
                    ins = self.nc.tensor.transpose(out[:, a, b * P:(b + 1) * P], src(b, j + a), self.ident[:])
            m = self.pe.done.up(ins)
            m1 = self.act([m], lambda e: e.copy(dst[:, j:j + nt, :], out[:, 0:nt, :]))
            self.bank_free[k] = [m1]
        self.tok_busy = [m]
        return m1

    def attend(self, groups, per, score, value, dst, ready, scale=1.0, mask=False, row_add=None,
               sink=None):
        nc = self.nc
        if mask:
            self.dve.wait(*self.mask_in)
            keys = [slice(0, P), slice(P, P + SEQ)]
            turned = [(slice(0, SEQ), 0), (slice(SEQ, SEQ + P), P)]
            width = P + SEQ
        else:
            keys = [slice(b * SEQ, (b + 1) * SEQ) for b in range(TB)]
            turned = [(slice(c * SEQ, (c + 1) * SEQ), 0) for c in range(TB)]
            width = TB * SEQ
        self.pe.wait(*ready)
        pt_busy = [[], []]
        scored, transposed = None, None
        for g in range(len(groups) + 2):
            if g < len(groups):
                banks = []
                for h in groups[g][0]:
                    k = self.bank(wide=True)
                    m = self.pe.done.up(score(h, lambda b: self.psum[:, k, keys[b]]))
                    banks.append((h, k, m))
            if transposed is not None:
                s, heads, tiles, mt = transposed
                k = self.bank(wide=True)
                self.pe.wait(mt)
                for i, h in enumerate(heads):
                    for slot, p0, wide, vals in value(h):
                        for c, (cols, q0) in enumerate(turned):
                            ins = nc.tensor.matmul(
                                self.psum[p0:p0 + wide, k, slot * SEQ + q0:(slot + 1) * SEQ], vals(c),
                                self.pt[:, s, i, cols], start=c == 0, stop=c == TB - 1)
                m = self.pe.done.up(ins)
                pt_busy[s] = [m]
                values_done = (k, tiles, m)
            else:
                values_done = None
            if scored is not None:
                s, heads, tiles, sm, rs, after, es = scored
                if sink is not None:
                    after = [self.dve(after, lambda v: v.tensor_tensor(sm, sm, es, ALU.add))]
                m = self.dve(after, lambda v: v.reciprocal(rs, sm))
                for i in range(len(heads)):
                    for b in range(TB):
                        e = self.e[:, s, i, keys[b]]
                        mn = self.dve([m], lambda v: v.tensor_scalar(
                            e, e, rs[:, TB * i + b:TB * i + b + 1], None, ALU.mult))
            if values_done is not None:
                k, out_tiles, m = values_done
                nt = out_tiles.stop - out_tiles.start
                out = self.psum[:, k, 0:nt * SEQ].rearrange("p (a n) -> p a n", a=nt)
                self.bank_free[k] = [self.split_out(dst, out_tiles, out, [m])]
            if scored is not None:
                for i, h in enumerate(heads):
                    k = self.bank(wide=True)
                    self.pe.wait(mn)
                    for c, (cols, q0) in enumerate(turned):
                        for b in range(q0 // P, TB):
                            ins = nc.tensor.transpose(
                                self.psum[:, k, cols.start + b * P - q0:cols.start + (b + 1) * P - q0],
                                self.e[:, s, i, keys[b].start + c * P:keys[b].start + (c + 1) * P],
                                self.ident[:])
                    m = self.pe.done.up(ins)
                    mt = self.act([m, *pt_busy[s]], lambda v: v.copy(
                        self.pt[:, s, i, 0:width], self.psum[:, k, 0:width]))
                    self.bank_free[k] = [mt]
                scored = (s, heads, tiles, mt)
            current = None
            if g < len(groups):
                s, (heads, tiles) = g % 2, groups[g]
                n = per * TB
                mx, nm, sm, rs = (self.stat[:, s, q, 0:n] for q in range(4))
                sources, es = [], None
                for i, (h, k, m) in enumerate(banks):
                    src = self.psum[:, k, :]
                    if mask:
                        e = self.e[:, s, i, :]
                        if row_add is None:
                            m = self.dve([m], lambda v: v.scalar_tensor_tensor(
                                e[:, 0:width], src[:, 0:width], scale, self.mask[:, 0:width],
                                ALU.mult, ALU.add))
                        else:
                            for b in range(TB):
                                m = self.dve([m], lambda v: v.scalar_tensor_tensor(
                                    e[:, keys[b]], src[:, keys[b]], row_add(h, b), self.mask[:, keys[b]],
                                    ALU.add, ALU.add))
                        self.bank_free[k] = [m]
                        src = e
                        for b in range(TB):
                            m = self.dve([m] if b == 0 else [], lambda v: v.tensor_reduce(
                                mx[:, TB * i + b:TB * i + b + 1], src[:, keys[b]], AX, ALU.max))
                    else:
                        m = self.dve([m], lambda v: v.tensor_reduce(
                            mx[:, TB * i:TB * i + TB], src.rearrange("p (b n) -> p b n", b=TB), AX, ALU.max))
                    sources.append((src, k))
                if sink is not None:
                    h0 = heads[0] * TB
                    m = self.dve([m], lambda v: v.tensor_tensor(mx, mx, sink[:, h0:h0 + n], ALU.max))
                nm_done = m = self.dve([m], lambda v: v.tensor_scalar(
                    nm, mx, -(1.0 if mask else scale), None, ALU.mult))
                if sink is not None:
                    es = self.small[:, s, 0:n]
                    m = self.dve([m], lambda v: v.tensor_tensor(es, nm, sink[:, h0:h0 + n], ALU.add))
                    self.act([m], lambda v: v.activation(es, es, ACT.Exp))
                for i, (src, k) in enumerate(sources):
                    for b in range(TB):
                        m = self.act([nm_done], lambda v: v.activation(
                            self.e[:, s, i, keys[b]], src[:, keys[b]], ACT.Exp,
                            bias=nm[:, TB * i + b:TB * i + b + 1], scale=1.0 if mask else scale,
                            accum_out=sm[:, TB * i + b:TB * i + b + 1]))
                    if not mask:
                        self.bank_free[k] = [m]
                current = (s, heads, tiles, sm, rs, [m], es)
            transposed, scored = scored, current
        return m


    def norm_sink(self, l, k):
        t, busy = self.t, self.row_busy
        ld1 = self.load(self.gain_row[:], t["ln_g"][l, k].partition_broadcast(P), busy)
        ld2 = self.load(self.bias_row[:], t["ln_b"][l, k].partition_broadcast(P))
        self.rows_in = [ld1, ld2]
        self.normed = [None] * TB
        stats = self.small[:, 2:4, 0:12]
        mv = self.norm[:, 0:4].rearrange("p (b s) -> p b s", b=TB)

        def part(b, c, mark):
            cs = slice(c * BANK, (c + 1) * BANK)
            z = self.n_tok[:, b, :]
            if b == TB - 1 and c == 1:
                self.norm_apply(0)
            m = self.dve([mark, *self.x_ready, *self.n_busy], lambda e: e.scalar_tensor_tensor(
                z[:, cs], self.x_tok[:, b, cs], ALPHA, self.psum[:, 2 * b + c, :], ALU.mult, ALU.add))
            self.bank_free[2 * b + c] = [m]
            m = self.dve([m], lambda e: e.bn_stats(stats[:, b, 6 * c:6 * c + 6], z[:, cs]))
            if c == 1:
                m = self.dve([m], lambda e: e.bn_aggr(mv[:, b, :], stats[:, b, :]))
                r = self.norm[:, 4 + b:5 + b]
                m = self.dve([m], lambda e: e.tensor_scalar(r, mv[:, b, 1:2], LN_EPS, None, ALU.add))
                m = self.pool([m, self.half_neg], lambda e: e.tensor_tensor(r, r, self.eps_pow[:, 0:1], ALU.pow))
                self.normed[b] = (m, z, mv[:, b, 0:1], r)
        return part

    def norm_apply(self, b):
        m, z, mean, r = self.normed[b]
        self.normed[b] = self.dve([m], lambda e: e.tensor_scalar(z, z, mean, r, ALU.subtract, ALU.mult))

    def norm_finish(self, l, k, last=False):
        idx = l * 3 + k
        self.norm_apply(1)
        done = self.normed[1]
        if not last:
            self.to_features(lambda b, j: self.n_tok[:, b, j * P:(j + 1) * P], KT, self.xt, 0,
                             self.normed, self.cols("ln_g", idx * KT, KT), self.cols("ln_b", idx * KT, KT))
            pe_read = self.pe.done.now()
        for b in range(TB):
            z, x = self.n_tok[:, b, :], self.x_tok[:, b, :]
            m = self.pool([done, *self.rows_in], lambda e: e.tensor_tensor(x, z, self.gain_row[:], ALU.mult))
            m = self.pool([m], lambda e: e.tensor_tensor(x, x, self.bias_row[:], ALU.add))
        self.x_ready = self.row_busy = [m]
        self.n_busy = [m] if last else [m, pe_read]

    def rms(self, src, width, dst, after, col, busy=()):
        before = self.act.done.now()
        squares = self.e[:].rearrange("p a b n -> p (a b n)")
        for b in range(TB):
            m = self.act([*after, before], lambda e: e.activation(
                squares[:, b * D:b * D + width], src(b), ACT.Square,
                accum_out=self.norm[:, col + b:col + b + 1]))
        m = self.dve([m], lambda e: e.tensor_scalar(
            self.norm[:, col:col + 2], self.norm[:, col:col + 2], 1.0 / width, None, ALU.mult))
        r = self.rsqrt(self.norm[:, col:col + 2], col + 2, RMS_EPS, [m])
        for b in range(TB):
            m = self.dve([r, *busy], lambda e: e.tensor_scalar(
                dst(b), src(b), self.norm[:, col + 2 + b:col + 3 + b], None, ALU.mult))
        return m

    def log1p(self, e, s, w, after):
        m = self.dve(after, lambda v: v.tensor_scalar(w, e, 2.0, None, ALU.add))
        m = self.dve([m], lambda v: v.reciprocal(w, w))
        m = self.dve([m], lambda v: v.tensor_tensor(s, e, w, ALU.mult))
        m = self.dve([m], lambda v: v.tensor_tensor(w, s, s, ALU.mult))
        m = self.dve([m], lambda v: v.tensor_scalar(e, w, 1.0 / 15, None, ALU.mult))
        for c in (13, 11, 9, 7, 5, 3):
            m = self.dve([m], lambda v: v.scalar_tensor_tensor(e, e, 1.0 / c, w, ALU.add, ALU.mult))
        m = self.dve([m], lambda v: v.scalar_tensor_tensor(s, e, 1.0, s, ALU.add, ALU.mult))
        return self.dve([m], lambda v: v.tensor_scalar(s, s, 2.0, None, ALU.mult))


    def mem_keys_values(self):
        t = self.t
        first = Count(self.p, "memory_load", 16)
        m = first.up(self.nc.sync.dma_start(self.tok[:], rows(t["mem"])))
        self.x_ready = [self.load(self.x_tok[:], rows(t["x"]))]
        self.params()
        self.to_features(lambda b, j: self.tok[:, b, j * P:(j + 1) * P], KT, self.xt, 0, [m, m])
        self.tok_busy = [self.pe.done.now()]
        m = self.project_features(t["mem_w_kv"], 0, KT, self.mem_kt, self.xt)
        for c in range(2):
            ks, outs, m = self.project_tokens(t["mem_w_kv"], D + c * BANK, BANK, self.xt)
            for b in range(TB):
                m1 = self.act([m], lambda e: e.copy(self.mem_v[:, b, c * BANK:(c + 1) * BANK], outs[b]))
                self.bank_free[ks[b]] = [m1]
        self.mem_ready = m1

    def load_mask(self, name):
        src = self.t[name]
        self.mask_in = [self.load(self.mask[:, 0:P], src[0:P, 0:P], [self.dve.done.now()]),
                        self.load(self.mask[:, P:P + SEQ], src[P:SEQ, :])]

    def sliding_attention(self, j, part_done):
        t, nc = self.t, self.nc
        w = t["a_w_qkv"][j]
        self.load_mask("c_mask_window")
        m = self.load(self.small[:, 4, 0:A_HEADS], t["a_sinks"][j].partition_broadcast(P))
        sink = self.qrt[:, 0, 0:A_HEADS * TB]
        self.dve([m], lambda e: e.tensor_copy(
            sink.rearrange("p (h b) -> p h b", b=TB),
            self.small[:, 4, 0:A_HEADS].unsqueeze(2).broadcast_to([P, A_HEADS, TB])))
        kw = A_KV * HD
        ks, outs, m = self.project_tokens(w, 2 * BANK, kw, self.xt)
        for b in range(TB):
            keys = self.tok[:, b, 0:2 * kw].rearrange("p (h c d) -> p h c d", c=2, d=HD)
            read, done = self.rope(outs[b], A_KV, b, keys[:, :, 0, :], [m, *self.tok_busy])
            done = self.dve([done], lambda e: e.tensor_copy(keys[:, :, 1, :], keys[:, :, 0, :]))
            self.bank_free[ks[b]] = [read]
        self.tok_half_busy = [[], self.tok_busy]
        waiting = (0, A_KV, self.kt[:, 0:A_KV, :], done)
        for c in range(2):
            waiting = self.rotated(w, c * BANK, BANK, 1 - c, self.qt[:, 4 * c:4 * c + 4, :], waiting)
        ks, outs, m = self.project_tokens(w, 2 * BANK + kw, kw, self.xt)
        for b in range(TB):
            m1 = self.act([m], lambda e: e.copy(self.v[:, b, 0:kw], outs[b]))
            self.bank_free[ks[b]] = [m1]
        m = self.turn_half(*waiting)
        self.tok_busy = [self.pe.done.now()]

        def score(h, out):
            p0, n = (h % 2) * HD, h // (A_HEADS // A_KV)
            for b in range(TB):
                o = out(b)
                ins = nc.tensor.matmul(o, self.qt[p0:p0 + HD, h // 2, b * P:(b + 1) * P],
                                       self.kt[p0:p0 + HD, n, 0:o.shape[1]], start=True, stop=True)
            return ins

        def value(h):
            n = h // (A_HEADS // A_KV)
            return [(0, (h % 2) * HD, HD, lambda c: self.v[:, c, n * HD:(n + 1) * HD])]

        self.attend([([2 * g, 2 * g + 1], slice(g, g + 1)) for g in range(A_HEADS // 2)], 2,
                    score, value, self.xt, [m, m1], HD ** -0.5, mask=True, sink=sink)
        self.out_project(t["a_w_o"][j], self.xt, part_done)

    def recurrent_block(self, part_done):
        t, nc = self.t, self.nc
        w, lru = t["b_w_in"][0], lambda off, n=1: self.cols("lru", off, n)
        conv_b, b_r, b_i, lam = (LRU_TAPS * KT + q * KT for q in range(4))
        gate, u = self.qt, self.kt
        r = self.v[:].rearrange("p b (j n) -> p (b j) n", n=SEQ)
        ig = self.e[:].rearrange("p a b (c n) -> p (a b c) n", n=SEQ)
        ab, sp, w8, pos, neg = (self.small[:, q, 0:KT] for q in (0, 1, 5, 6, 7))
        lm = lru(lam, KT)
        m = self.dve([], lambda e: e.scalar_tensor_tensor(ab, lm, -1.0, lm, ALU.mult, ALU.max))
        m = self.act([m], lambda e: e.activation(ab, ab, ACT.Exp, scale=-1.0))
        m = self.log1p(ab, sp, w8, [m])
        self.dve([], lambda e: e.tensor_scalar(pos, lm, -1.0, 0.0, ALU.mult, ALU.max))
        m = self.dve([m, self.dve.done.now()], lambda e: e.tensor_tensor(sp, sp, pos, ALU.add))
        m = self.dve([m], lambda e: e.tensor_scalar(pos, sp, LRU_C, None, ALU.mult))
        lam_done = self.dve([m], lambda e: e.tensor_scalar(neg, sp, -LRU_C, None, ALU.mult))
        for j in range(2 * KT):
            k = self.bank()
            out = self.psum[:, k, 0:SEQ]
            unit = self.w.take(rows(w)[:, :, j * P:(j + 1) * P])
            m = self.w.used.up(self.feature_out(out, unit, self.xt))
            if j < KT:
                m = self.act([m], lambda e: e.activation(gate[:, j, :], out, ACT.Gelu_apprx_tanh))
            else:
                i = j - KT
                tap = lambda q: lru(q * KT + i)
                m = self.act([m], lambda e: e.activation(u[:, i, :], out, ACT.Identity,
                                                         scale=tap(LRU_TAPS - 1), bias=lru(conv_b + i)))
                for d in range(1, LRU_TAPS):
                    m = self.dve([m], lambda e: e.scalar_tensor_tensor(
                        u[:, i, d:SEQ], out[:, 0:SEQ - d], tap(LRU_TAPS - 1 - d), u[:, i, d:SEQ],
                        ALU.mult, ALU.add))
            self.bank_free[k] = [m]
        self.xt.busy = [self.w.used.now()]
        self.split_out(self.xt, slice(0, KT), u[:], [m])
        th = self.pt[:].rearrange("p a b (c n) -> p (a b c) n", n=SEQ)
        gates = {}
        for half in range(2):
            for name, dst, bias in (("b_w_rgate", r, b_r), ("b_w_igate", ig, b_i)):
                wg = t[name][0].rearrange("h (k p) n -> p (h k) n", p=P)
                hi, lo = self.w.take(wg[:, 4 * half:4 * half + 4, :])
                for blk in range(2):
                    k = self.bank()
                    out = self.psum[:, k, :].rearrange("p (a n) -> p a n", a=2)
                    for a in range(2):
                        for q in range(2):
                            kt = 4 * half + 2 * blk + q
                            self.pe.wait(self.xt.ready[kt])
                            cs = slice(a * P, (a + 1) * P)
                            ins = product(nc, out[:, a, :], (hi[:, 2 * blk + q, cs], lo[:, 2 * blk + q, cs]),
                                          (self.xt.hi[:, kt, :], self.xt.lo[:, kt, :]), q == 0, q == 1)
                    m = self.w.used.up(ins) if blk == 1 else self.pe.done.up(ins)
                    for a in range(2):
                        jt = 4 * half + 2 * blk + a
                        m1 = self.act([m], lambda e: e.activation(dst[:, jt, :], out[:, a, :], ACT.Sigmoid,
                                                                  bias=lru(bias + jt)))
                    self.bank_free[k] = [m1]
            gates[half] = m1
        self.xt.busy = [self.w.used.now()]
        for j in range(KT):
            mt = self.act([gates[1], lam_done], lambda e: e.activation(th[:, j, :], r[:, j, :], ACT.Tanh,
                                                                       scale=pos[:, j:j + 1]))
        halves = [slice(0, KT // 2), slice(KT // 2, KT)]
        roots = []
        for h in halves:
            m = self.dve([gates[1]], lambda e: e.tensor_tensor(ig[:, h, :], ig[:, h, :], u[:, h, :], ALU.mult))
            m = self.dve([mt, m], lambda e: e.tensor_scalar(u[:, h, :], th[:, h, :], 1.0, None, ALU.add))
            m = self.dve([m], lambda e: e.reciprocal(u[:, h, :], u[:, h, :]))
            roots.append(self.dve([m], lambda e: e.tensor_tensor(th[:, h, :], th[:, h, :], u[:, h, :], ALU.mult)))
        for j in range(KT):
            ma = self.act([mt], lambda e: e.activation(r[:, j, :], r[:, j, :], ACT.Exp, scale=neg[:, j:j + 1]))
        roots = [self.act([m], lambda e: e.activation(th[:, h, :], th[:, h, :], ACT.Sqrt, scale=2.0))
                 for h, m in zip(halves, roots)]
        for h, m in zip(halves, roots):
            m = self.dve([m], lambda e: e.tensor_tensor(th[:, h, :], th[:, h, :], ig[:, h, :], ALU.mult))
            for j in range(h.start, h.stop):
                m1 = self.dve([m, ma], lambda e: e.tensor_tensor_scan(u[:, j, :], r[:, j, :], th[:, j, :], 0.0,
                                                                      ALU.mult, ALU.add))
            for q in range(h.start, h.stop, 2):
                qs = slice(q, q + 2)
                m = self.dve([m1], lambda e: e.tensor_tensor(u[:, qs, :], u[:, qs, :], gate[:, qs, :], ALU.mult))
                self.split_out(self.xt, qs, u[:, qs, :], [m])
        self.out_project(t["b_w_o"][0], self.xt, part_done)

    def latent_attention(self, part_done):
        t, nc = self.t, self.nc
        self.load_mask("c_mask_causal")
        w = rows(t["c_w_down"][0])
        width = C_QR + C_KVR + C_ROPE
        for col, n in ((0, 512), (512, width - 512)):
            ks, outs, m = self.project_tokens(t["c_w_down"][0], col, n, self.xt)
            for b in range(TB):
                m1 = self.act([m, *self.tok_busy], lambda e: e.copy(self.tok[:, b, col:col + n], outs[b]))
                self.bank_free[ks[b]] = [m1]
        self.tok_busy = []
        off = LRU_TAPS * KT + 4 * KT
        lat = lambda c0, n: (lambda b: self.tok[:, b, c0:c0 + n])
        dst = lambda c0, n: (lambda b: self.n_tok[:, b, c0:c0 + n])
        m = self.rms(lat(0, C_QR), C_QR, dst(0, C_QR), [m1], 8, self.n_busy)
        m = self.rms(lat(C_QR, C_KVR), C_KVR, dst(C_QR, C_KVR), [m1], 12)
        self.to_features(lambda b, j: self.n_tok[:, b, j * P:(j + 1) * P], 3, self.xt, 0, [m, m],
                         self.cols("lru", off, 3))
        self.to_features(lambda b, j: self.n_tok[:, b, C_QR + j * P:C_QR + (j + 1) * P], 2, self.xt, 3, [m, m],
                         self.cols("lru", off + 3, 2))
        self.n_busy = [*self.n_busy, self.pe.done.now()]
        kr = self.tok[:, :, 768:896].rearrange("p b (c d) -> p b c d", c=2)
        for b in range(TB):
            _, done = self.rope(self.tok[:, b, C_QR + C_KVR:width], 1, b, kr[:, b, 0:1, :], [m1])
            done = self.dve([done], lambda e: e.tensor_copy(kr[:, b, 1, :], kr[:, b, 0, :]))
        self.turn_tokens(lambda b, i: self.tok[:, b, 768:896], 1, self.krt[:].unsqueeze(1), [done])
        hw = C_NOPE + C_ROPE
        wq = rows(t["c_w_uq"][0])
        for g in range(C_HEADS // 2):
            kf, k = self.bank(), self.bank()
            flat = self.psum[:, kf, :].rearrange("p (a n) -> p a n", a=2)
            out = self.psum[:, k, :].rearrange("p (b n) -> p b n", b=TB)
            for a in range(2):
                h = 2 * g + a
                hi, lo = self.w.take(wq[:, :, h * hw:(h + 1) * hw])
                self.feature_out(flat[:, a, :], (hi[:, :, 0:C_NOPE], lo[:, :, 0:C_NOPE]), self.xt)
                for b in range(TB):
                    tb = slice(b * P, (b + 1) * P)
                    for q in range(3):
                        ins = product(nc, out[:, b, a * C_ROPE:(a + 1) * C_ROPE],
                                      (self.xt.hi[:, q, tb], self.xt.lo[:, q, tb]),
                                      (hi[:, q, C_NOPE:hw], lo[:, q, C_NOPE:hw]), q == 0, q == 2)
                m = self.w.used.up(ins)
            m1 = self.act([m], lambda e: e.copy(self.qt[:, 2 * g:2 * g + 2, :], flat))
            self.bank_free[kf] = [m1]
            qr = self.tok[:, :, g * P:(g + 1) * P]
            for b in range(TB):
                read, done = self.rope(out[:, b, 0:P], 2, b, qr[:, b, :].rearrange("p (h d) -> p h d", h=2),
                                       [m])
            self.bank_free[k] = [read]
        self.turn_tokens(lambda b, i: self.tok[:, b, i * P:(i + 1) * P], C_HEADS // 2, self.qrt, [done])
        kvw = C_NOPE + C_V
        wkv = rows(t["c_w_ukv"][0])
        for g in range(C_HEADS // 2):
            hi, lo = self.w.take(wkv[:, :, g * 2 * kvw:(g + 1) * 2 * kvw])
            k = self.bank()
            out = self.psum[:, k, :].rearrange("p (a n) -> p a n", a=2)
            for a in range(2):
                cs = slice(a * kvw, a * kvw + C_NOPE)
                ins = self.feature_out(out[:, a, :], (hi[:, :, cs], lo[:, :, cs]), self.xt, 3)
            m = self.pe.done.up(ins)
            m1 = self.act([m], lambda e: e.copy(self.kt[:, 2 * g:2 * g + 2, :], out))
            self.bank_free[k] = [m1]
            k = self.bank()
            out = self.psum[:, k, :].rearrange("p (b n) -> p b n", b=TB)
            part = lambda a, q: a[:, q, :].rearrange("p (h d) -> p h d", h=2)[:, :, C_NOPE:kvw]
            for b in range(TB):
                tb = slice(b * P, (b + 1) * P)
                for q in range(2):
                    ins = product(nc, out[:, b, :].rearrange("p (h d) -> p h d", h=2),
                                  (self.xt.hi[:, 3 + q, tb], self.xt.lo[:, 3 + q, tb]),
                                  (part(hi, q), part(lo, q)), q == 0, q == 1)
            m = self.w.used.up(ins)
            m1 = self.act([m], lambda e: e.copy(self.v[:, :, g * 2 * C_V:(g + 1) * 2 * C_V], out))
            self.bank_free[k] = [m1]
        self.xt.busy = [m]

        def score(h, out):
            p0 = (h % 2) * C_ROPE
            for b in range(TB):
                tb = slice(b * P, (b + 1) * P)
                o = out(b)
                n = o.shape[1]
                nc.tensor.matmul(o, self.qt[:, h, tb], self.kt[:, h, 0:n], start=True, stop=False)
                ins = nc.tensor.matmul(o, self.qrt[p0:p0 + C_ROPE, h // 2, tb],
                                       self.krt[p0:p0 + C_ROPE, 0:n], start=False, stop=True)
            return ins

        self.attend([([2 * g, 2 * g + 1], slice(2 * g, 2 * g + 2)) for g in range(C_HEADS // 2)], 2, score,
                    lambda h: [(h % 2, 0, C_V, lambda c: self.v[:, c, h * C_V:(h + 1) * C_V])],
                    self.xt, [m1], (C_NOPE + C_ROPE) ** -0.5, mask=True)
        self.out_project(t["c_w_o"][0], self.xt, part_done)

    def cross_attention(self, l, part_done):
        t, nc = self.t, self.nc
        m = self.project_features(t["x_w_q"][l], 0, KT, self.qt, self.xt)
        per_head = X_HD // P

        def score(h, out):
            for b in range(TB):
                for q in range(per_head):
                    ins = nc.tensor.matmul(out(b), self.qt[:, per_head * h + q, b * P:(b + 1) * P],
                                           self.mem_kt[:, per_head * h + q, :],
                                           start=q == 0, stop=q == per_head - 1)
            return ins

        def value(h):
            return [(q, 0, P, (lambda q: lambda c: self.mem_v[:, c, h * X_HD + q * P:h * X_HD + (q + 1) * P])(q))
                    for q in range(per_head)]

        self.attend([([h], slice(per_head * h, per_head * (h + 1))) for h in range(X_HEADS)], 1,
                    score, value, self.xt, [m, self.mem_ready], X_HD ** -0.5)
        self.out_project(t["x_w_o"][l], self.xt, part_done)

    def seed_accumulators(self):
        for k in range(4):
            self.pe.wait(self.zeros_done, *self.bank_free[k])
            self.nc.tensor.matmul(self.psum[:, k, :], self.zeros[:, 0:P], self.zeros[:], start=True,
                                  stop=False, skip_group_check=True)

    def feed_forward(self, up, down, params, silu_half):
        nc, w, psum = self.nc, self.w, self.psum
        up, down = rows(up), rows(down)
        c0 = self.col[params]
        conv, act_out = self.qt, self.kt
        hid = self.hid
        for k in range(4, 8):
            self.pe.wait(*self.bank_free[k])
        V, A = self.dve.done, self.act.done
        v0, a0 = V.n, A.n
        VT, AT = 6, 4

        def conv_tile(m, i):
            s = m % 2
            off = (lambda q: slice(c0 + q, c0 + q + 1)) if i is None else \
                  (lambda q: bass.ds(i * 2 + (c0 + q), 1))
            col = (lambda q: self.par[:, off(q)])
            out = psum[:, 4 + s, :].rearrange("p (a n) -> p a n", a=2)
            self.pe.wait(V.at(v0 + VT * (m - 2) + 4))
            if m == 0:
                out = [out[:, 0, :], psum[:, 6, 0:SEQ]]
                units = [w.take(up[:, :, half * FT * P:half * FT * P + P]) for half in range(2)]
                for k in range(KT):
                    self.pe.wait(self.xt.ready[k])
                    for half, (hi, lo) in enumerate(units):
                        ins = product(nc, out[half], (hi[:, k, :], lo[:, k, :]),
                                      (self.xt.hi[:, k, :], self.xt.lo[:, k, :]), k == 0, k == KT - 1)
                        if k == KT - 1:
                            made = w.used.up(ins)
            else:
                out = [out[:, 0, :], out[:, 1, :]]
                for half in range(2):
                    c = slice((half * FT + m) * P, (half * FT + m + 1) * P) if i is None else \
                        bass.ds(i * (2 * P) + (half * FT + m) * P, P)
                    unit = w.take(up[:, :, c])
                    made = w.used.up(self.feature_out(out[half], unit, self.xt))
            self.act.wait(made, V.at(v0 + VT * (m - 2) + 5))
            for half in range(2):
                t = half * FT + m
                base = self.act([], lambda e: e.activation(
                    conv[:, 2 * s + half, :], out[half], ACT.Identity,
                    scale=col((TAPS - 1) * 2 * FT + t), bias=col(TAPS * 2 * FT + t)))
            self.dve.wait(base)
            order = (silu_half, 1 - silu_half)
            for d in range(1, TAPS):
                for half in order:
                    t = half * FT + m
                    cv = conv[:, 2 * s + half, :]
                    self.dve([V.at(V.n - 1)] if d > 1 else [], lambda e: e.scalar_tensor_tensor(
                        cv[:, d:SEQ], out[half][:, 0:SEQ - d], col((TAPS - 1 - d) * 2 * FT + t),
                        cv[:, d:SEQ], ALU.mult, ALU.add))
            conv_done = V.now()
            sil, prod = act_out[:, s, :], act_out[:, 2 + s, :]
            ms = self.act([V.at(V.n - 1)], lambda e: e.activation(sil, conv[:, 2 * s + silu_half, :], ACT.Silu))
            mp = self.dve([ms, conv_done], lambda e: e.tensor_tensor(
                prod, sil, conv[:, 2 * s + 1 - silu_half, :], ALU.mult))
            hi, lo = hid.hi[:, s, :], hid.lo[:, s, :]
            mh = self.act([mp, made], lambda e: e.copy(hi, prod))
            return self.dve([mh], lambda e: e.tensor_tensor(lo, prod, hi.bitcast(F32), ALU.subtract))

        def down_tile(m, i, last=False):
            s = m % 2
            rowsel = slice(m, m + 1) if i is None else bass.ds(i * 2 + m, 1)
            hi, lo = w.take(down[:, rowsel, :])
            self.pe.wait(V.at(v0 + VT * (m + 1)))
            marks = []
            for b in range(TB):
                if last and b > 0:
                    marks.append(self.pe.done.up(ins))
                tb = slice(b * P, (b + 1) * P)
                for c in range(2):
                    cs = slice(c * BANK, (c + 1) * BANK)
                    mov = (hi[:, 0, cs], lo[:, 0, cs])
                    stat = (hid.hi[:, s, tb], hid.lo[:, s, tb])
                    for q, (x, y) in enumerate(((0, 0), (0, 1), (1, 0))):
                        ins = nc.tensor.matmul(psum[:, 2 * b + c, :], stat[x], mov[y], start=False,
                                               stop=last and q == 2, skip_group_check=True)
            return [*marks, w.used.up(ins)]

        self.act.wait(V.at(v0))
        conv_tile(0, None)
        per = w.counts(RING)
        per.update({V: 2 * VT, A: 2 * AT})
        with self.p.repeat((FT - 2) // 2, per) as i:
            for m in (1, 2):
                conv_tile(m, i)
                down_tile(m - 1, i)
        self.w.skip((FT - 2) // 2 * RING - RING)
        conv_tile(FT - 1, None)
        down_tile(FT - 2, None)
        m = down_tile(FT - 1, None, last=True)
        self.xt.busy = [m[-1]]
        for k in range(4, 8):
            self.bank_free[k] = [V.now()]
        return m


    def norm_to_features(self, src, gain, after):
        m = self.rms(lambda b: src[:, b, :], D, lambda b: self.n_tok[:, b, :], after, 8,
                     self.n_busy)
        self.to_features(lambda b, j: self.n_tok[:, b, j * P:(j + 1) * P], KT, self.xt, 0, [m, m], gain)
        self.n_busy = [self.pe.done.now()]

    def add_part(self, b, c, mark):
        h = self.x_tok[:, b, c * BANK:(c + 1) * BANK]
        m = self.dve([mark, *self.x_ready], lambda e: e.tensor_tensor(h, h, self.psum[:, 2 * b + c, :], ALU.add))
        self.bank_free[2 * b + c] = [m]
        if b == TB - 1 and c == 1:
            self.x_ready = [m]

    def second_memory_norm(self):
        m = self.load(self.tok[:], rows(self.t["mem_2"]), [*self.tok_busy])
        tok = lambda b: self.tok[:, b, :]
        return self.rms(tok, D, tok, [m], 12)

    def second_memory_features(self, l, done):
        self.to_features(lambda b, j: self.tok[:, b, j * P:(j + 1) * P], KT, self.xt, 0, [done, done],
                         self.cols("norms_2", (DEPTH_2 + l) * KT, KT))
        self.tok_busy = [self.pe.done.now()]

    def second_memory(self, l):
        w = self.t["w_mem_kv_2"][l]
        self.project_features(w, 0, D_MEMQ // P, self.mem_kt, self.xt)
        ks, outs, m = self.project_tokens(w, D_MEMQ, D_MEMQ, self.xt)
        for b in range(TB):
            m1 = self.act([m], lambda e: e.copy(self.mem_v[:, b, 0:D_MEMQ], outs[b]))
            self.bank_free[ks[b]] = [m1]
        self.mem_ready = m1

    def small_attention(self, heads, qt, kt, v, tile0, ready, **how):
        nc = self.nc
        extra = how.pop("extra", None)

        def score(h, out):
            p0 = (h % 2) * HD
            for b in range(TB):
                o = out(b)
                ins = nc.tensor.matmul(o, qt[p0:p0 + HD, h // 2, b * P:(b + 1) * P],
                                       kt[p0:p0 + HD, h // 2, 0:o.shape[1]], start=True, stop=extra is None)
                if extra is not None:
                    ins = extra(h, p0, o)
            return ins

        self.attend([([2 * g, 2 * g + 1], slice(tile0 + g, tile0 + g + 1)) for g in range(heads // 2)], 2,
                    score, lambda h: [(0, (h % 2) * HD, HD, lambda c: v[:, c, h * HD:(h + 1) * HD])],
                    self.xt, ready, **how)

    def values_2(self, w, col0):
        for c, n in ((0, BANK), (BANK, D_MIX - BANK)):
            ks, outs, m = self.project_tokens(w, col0 + c, n, self.xt)
            for b in range(TB):
                m1 = self.act([m], lambda e: e.copy(self.v[:, b, c:c + n], outs[b]))
                self.bank_free[ks[b]] = [m1]
        return m1

    def forgetting_attention(self):
        t, nc = self.t, self.nc
        w = t["w_in_fox_2"][0]
        tiles = D_MIX // P
        self.load_mask("c_mask_causal")
        tri, ones = self.gain_row[:, 0:P], self.gain_row[:, P:2 * P]
        l0 = self.load(tri, t["c_triangle"], self.row_busy)
        l1 = self.load(self.small[:, 4, 0:MIX_HEADS], t["b_forget_2"][0].partition_broadcast(P))
        one = self.pool([], lambda e: e.memset(ones, 1.0))
        self.project_features(w, 0, tiles, self.qt, self.xt, scale=HD ** -0.5)
        self.project_features(w, D_MIX, tiles, self.kt, self.xt)
        self.values_2(w, 2 * D_MIX)
        ks, outs, m = self.project_tokens(w, 3 * D_MIX, MIX_HEADS, self.xt)
        z, ab, s, w8, neg, lf = (self.small[:, q, :] for q in (0, 1, 2, 3, 5, 6))
        H = MIX_HEADS
        for b in range(TB):
            m = self.dve([m, l1], lambda e: e.tensor_tensor(z[:, b * H:(b + 1) * H], outs[b],
                                                            self.small[:, 4, 0:H], ALU.add))
            self.bank_free[ks[b]] = [m]
        m = self.dve([m], lambda e: e.scalar_tensor_tensor(ab, z, -1.0, z, ALU.mult, ALU.max))
        m1 = self.dve([], lambda e: e.tensor_scalar(neg, z, 0.0, None, ALU.min))
        m = self.act([m], lambda e: e.activation(ab, ab, ACT.Exp, scale=-1.0))
        m = self.log1p(ab, s, w8, [m])
        m = self.dve([m, m1], lambda e: e.tensor_tensor(lf, neg, s, ALU.subtract))
        m2 = self.project_features(w, 3 * D_MIX + H, D_MEMQ // P, self.qrt, self.xt)
        k = self.bank()
        self.pe.wait(m, l0, one)
        out = self.psum[:, k, 0:2 * H]
        nc.tensor.matmul(out[:, 0:H], tri, lf[:, 0:H], start=True, stop=True)
        nc.tensor.matmul(out[:, H:2 * H], tri, lf[:, H:2 * H], start=True, stop=False)
        m = self.pe.done.up(nc.tensor.matmul(out[:, H:2 * H], ones, lf[:, 0:H], start=False, stop=True))
        csum = self.norm[:, 8:8 + 2 * H]
        m3 = self.dve([m], lambda e: e.tensor_copy(csum, out))
        neg_c = self.tok[:, :, 0:P]
        mz = self.dve([*self.tok_busy], lambda e: e.memset(neg_c, 0.0))
        for b in range(TB):
            for half in range(2):
                m4 = self.dve([mz, m3], lambda e: e.tensor_scalar(
                    neg_c[:, b, half * HD:half * HD + H], csum[:, b * H:(b + 1) * H], -1.0, None, ALU.mult))
        self.bank_free[k] = [m3]
        m = self.turn_tokens(lambda b, i: neg_c[:, b, :], 1, self.krt[:].unsqueeze(1), [m4])

        def minus_c(h, p0, out):
            return nc.tensor.matmul(out, self.ident[p0:p0 + HD, p0 + h:p0 + h + 1].broadcast_to([HD, P]),
                                    self.krt[p0:p0 + HD, 0:out.shape[1]], start=False, stop=True)

        self.small_attention(MIX_HEADS, self.qt, self.kt, self.v, 0, [m, m2], mask=True, extra=minus_c,
                             row_add=lambda h, b: csum[:, b * H + h:b * H + h + 1])
        self.row_busy = [self.pe.done.now()]

    def dilated_attention(self):
        t = self.t
        w = t["w_in_dil_2"][0]
        self.load_mask("c_mask_dilated")
        waiting, half = None, 0
        self.tok_half_busy = [self.tok_busy, self.tok_busy]
        for part, dst in ((0, self.qt), (1, self.kt)):
            for c, n in ((0, BANK), (BANK, D_MIX - BANK)):
                waiting = self.rotated(w, part * D_MIX + c, n, half, dst[:, c // P:(c + n) // P, :], waiting)
                half = 1 - half
        self.values_2(w, 2 * D_MIX)
        self.turn_half(*waiting)
        m = self.project_features(w, 3 * D_MIX, D_MEMQ // P, self.qrt, self.xt)
        self.small_attention(MIX_HEADS, self.qt, self.kt, self.v, 0, [m], scale=HD ** -0.5, mask=True)

    def build(self):
        t, p = self.t, self.p
        self.hid = Split(p, "hid", 2)
        self.mem_keys_values()
        self.turn_params()
        self.to_features(lambda b, j: self.x_tok[:, b, j * P:(j + 1) * P], KT, self.xt, 0, self.x_ready * 2)
        self.x_ready.append(self.pe.done.now())
        kinds = [self.sliding_attention, lambda j, f: self.recurrent_block(f),
                 lambda j, f: self.latent_attention(f)]
        for l in range(DEPTH):
            last = l == DEPTH - 1
            kinds[l % 3](l // 3, self.norm_sink(l, 0))
            self.norm_finish(l, 0)
            self.cross_attention(l, self.norm_sink(l, 1))
            self.seed_accumulators()
            self.norm_finish(l, 1)
            if last:
                mem_tok = self.second_memory_norm()
            sink = self.norm_sink(l, 2)
            m = self.feed_forward(t["f_w_up"][l], t["f_w_down"][l], ("f", l), 0)
            if last:
                self.second_memory_features(0, mem_tok)
            for b in range(TB):
                for c in range(2):
                    sink(b, c, m[b])
            self.norm_finish(l, 2, last)
        for l in range(DEPTH_2):
            self.second_memory(l)
            self.norm_to_features(self.x_tok, self.cols("norms_2", l * KT, KT), self.x_ready)
            if l % 2 == 0:
                self.forgetting_attention()
            else:
                self.dilated_attention()
            self.small_attention(MEM_HEADS, self.qrt, self.mem_kt, self.mem_v, D_MIX // P,
                                 [self.mem_ready], scale=HD ** -0.5)
            self.out_project(t["w_out_2"][l], self.xt, self.add_part)
            self.seed_accumulators()
            self.norm_to_features(self.x_tok, self.cols("norms_2", (2 * DEPTH_2 + l) * KT, KT), self.x_ready)
            if l < DEPTH_2 - 1:
                mem_tok = self.second_memory_norm()
            m = self.feed_forward(t["w_up_2"][l], t["w_down_2"][l], ("g", l), 1)
            if l < DEPTH_2 - 1:
                self.second_memory_features(l + 1, mem_tok)
            for b in range(TB):
                for c in range(2):
                    self.add_part(b, c, m[b])
        m0 = self.load(self.gain_row[:], t["norm_final_2"].partition_broadcast(P), self.row_busy)
        m = self.rms(lambda b: self.x_tok[:, b, :], D, lambda b: self.n_tok[:, b, :], self.x_ready, 8,
                     self.n_busy)
        for b in range(TB):
            z = self.n_tok[:, b, :]
            m1 = self.dve([m, m0], lambda e: e.tensor_tensor(z, z, self.gain_row[:], ALU.mult))
        self.finish(self.n_tok, [m1])

    def finish(self, src, after):
        self.units = self.w.next
        self.sp.wait(*after)
        m = self.stores.up(self.nc.sync.dma_start(rows(self.t["out"]), src[:]))
        self.sp.wait(m)


def two_stacks_kernel(nc, tensors, total_units):
    with ExitStack() as ctx:
        t = dict(tensors)
        for name in ("x", "mem", "mem_2", "out"):
            t[name] = t[name].rearrange("a s d -> (a s) d")
        model = Model(nc, ctx, t, total_units)
        model.build()
        return model.units


_INS = ["x", "mem", "a_w_qkv", "a_sinks", "a_w_o", "b_w_in", "b_conv_w", "b_conv_b", "b_w_rgate",
        "b_b_rgate", "b_w_igate", "b_b_igate", "b_lambda", "b_w_o", "c_w_down", "c_q_norm", "c_kv_norm",
        "c_w_uq", "c_w_ukv", "c_w_o", "mem_w_kv", "x_w_q", "x_w_o", "f_w_up", "f_conv_w", "f_conv_b",
        "f_w_down", "ln_g", "ln_b", "mem_2", "norm_mix_2", "norm_mem_2", "norm_ffn_2", "w_in_fox_2",
        "b_forget_2", "w_in_dil_2", "w_mem_kv_2", "w_out_2", "w_up_2", "conv_w_2", "conv_b_2",
        "w_down_2", "norm_final_2"]
UNITS = 635


def shape_constants():
    import numpy as np
    f = np.float32
    i, j = np.arange(SEQ)[:, None], np.arange(SEQ)[None, :]
    d = i - j
    inv = (f(1.0) / (f(10000.0) ** (np.arange(0, HD, 2, dtype=f) / f(HD)))).astype(f)
    ang = np.arange(SEQ, dtype=f)[:, None] * inv[None, :]
    cos, sin = np.cos(ang).astype(f), np.sin(ang).astype(f)
    neg = f(-1e30)
    count = ((d >= 0) & (d <= 128)).astype(int) + ((d >= 0) & (d % 4 == 0)) + ((d >= 0) & (d % 16 == 0))
    return {
        "c_ident": np.eye(P, dtype=f),
        "c_triangle": np.triu(np.ones((P, P), dtype=f)),
        "c_cos": np.concatenate([cos, cos], 1),
        "c_sin": np.concatenate([-sin, sin], 1),
        "c_mask_window": np.where((d >= 0) & (d < 128), f(0), neg).astype(f),
        "c_mask_causal": np.where(d >= 0, f(0), neg).astype(f),
        "c_mask_dilated": np.where(count > 0, np.log(np.maximum(count, 1)), neg).astype(f),
    }


def kernel(**inputs):
    import numpy as _np
    import concourse.bacc as _bacc
    from concourse import mybir as _mybir
    from concourse.bass_utils import run_bass_kernel_spmd as _run

    nc = _bacc.Bacc("TRN2", target_bir_lowering=False, num_devices=1)
    arrays, tensors = {}, {}
    for name, a in [(n, inputs[n]) for n in _INS] + list(shape_constants().items()):
        a = _np.ascontiguousarray(a)
        arrays[f"in_{name}_dram"] = a
        tensors[name] = nc.dram_tensor(f"in_{name}_dram", a.shape, _mybir.dt.from_np(a.dtype),
                                       kind="ExternalInput").ap()
    tensors["out"] = nc.dram_tensor("out_0_dram", (1, SEQ, D), F32, kind="ExternalOutput").ap()
    two_stacks_kernel(nc, tensors, UNITS)
    r = _run(nc, [arrays], core_ids=[0])
    return r.results[0]["out_0_dram"]
```

```python
from contextlib import ExitStack, contextmanager
import concourse.bass as bass
from concourse import mybir

F32 = mybir.dt.float32
F32R = mybir.dt.float32r
ACT = mybir.ActivationFunctionType
ALU = mybir.AluOpType
AX = mybir.AxisListType.X

P = 128
SEQ = 256
TB = SEQ // P
D = 1024
KT = D // P
DEPTH = 4
DEPTH_2 = 2
ALPHA = (2.0 * DEPTH) ** 0.25
LN_EPS = 1e-5
RMS_EPS = 1e-6
FF = 2816
FT = FF // P
TAPS = 3

A_HEADS, A_KV, HD = 16, 4, 64
C_HEADS, C_NOPE, C_ROPE, C_V, C_QR, C_KVR = 8, 128, 64, 128, 384, 256
X_HEADS, X_HD = 4, 256
LRU_TAPS, LRU_C = 4, 8.0
MIX_HEADS, MEM_HEADS = 12, 4
D_MIX, D_MEMQ = MIX_HEADS * HD, MEM_HEADS * HD

UNIT = 1024
RING = 6
AHEAD = 4
BANK = 512


class Count:

    def __init__(self, prog, name, by=1):
        self.prog, self.by, self.n = prog, by, 0
        self.sem = prog.ctx.enter_context(prog.nc.semaphore(name))

    def up(self, ins):
        ins.then_inc(self.sem, self.by)
        self.n += 1
        return self.now()

    def now(self):
        return (self, self.n, self.prog.loop is not None)

    def at(self, n):
        return (self, n, self.prog.loop is not None)


class Lane:

    def __init__(self, prog, eng, name):
        self.prog, self.eng = prog, eng
        self.done = Count(prog, name)
        self.seen = {}

    def wait(self, *marks):
        for m in marks:
            if isinstance(m, list):
                self.wait(*m)
                continue
            count, n, inside = m
            if n <= 0 and not inside:
                continue
            key = (count, inside)
            if self.seen.get(key, -1) >= n:
                continue
            self.seen[key] = n
            if inside:
                i, per = self.prog.loop
                self.eng.wait_ge(count.sem, i * (per[count] * count.by) + n * count.by)
            else:
                self.eng.wait_ge(count.sem, n * count.by)

    def __call__(self, after, issue):
        self.wait(*after)
        return self.done.up(issue(self.eng))


class Program:
    def __init__(self, nc, ctx):
        self.nc, self.ctx, self.loop = nc, ctx, None
        self.pe = Lane(self, nc.tensor, "pe_done")
        self.act = Lane(self, nc.scalar, "act_done")
        self.dve = Lane(self, nc.vector, "dve_done")
        self.pool = Lane(self, nc.gpsimd, "pool_done")
        self.sp = Lane(self, nc.sync, "sp_done")
        self.lanes = [self.pe, self.act, self.dve, self.pool, self.sp]

    @contextmanager
    def repeat(self, times, per):
        start = {c: c.n for c in per}
        for lane in self.lanes:
            lane.seen = {k: v for k, v in lane.seen.items() if not k[1]}
        with self.nc.Fori(0, times) as i:
            self.loop = (i, per)
            yield i
        self.loop = None
        for c, n in per.items():
            assert c.n - start[c] == n, (c.sem, c.n - start[c], n)
            c.n = start[c] + n * times
        for lane in self.lanes:
            lane.seen = {k: v for k, v in lane.seen.items() if not k[1]}

    def sbuf(self, name, shape, dt=F32):
        return self.ctx.enter_context(self.nc.sbuf_tensor(name, shape, dt))


class Split:

    def __init__(self, hi, lo):
        self.hi, self.lo, tiles = hi, lo, hi.shape[1]
        self.ready, self.busy = [[]] * tiles, []


class WeightStream:

    def __init__(self, prog, total):
        self.prog, self.total = prog, total
        self.raw = prog.sbuf("w_raw", [P, RING, UNIT])
        self.hi = prog.sbuf("w_hi", [P, RING, UNIT], F32R)
        self.lo = prog.sbuf("w_lo", [P, RING, UNIT], F32R)
        self.landed = [Count(prog, f"w_landed{s}", 16) for s in range(RING)]
        self.parts = Count(prog, "w_parts", 16)
        self.hi_done = Count(prog, "w_hi_done")
        self.lo_done = Count(prog, "w_lo_done")
        self.used = Count(prog, "w_used")
        self.next = 0
        self.split_next = 0
        self.hold = None

    def counts(self, units):
        per = {c: units // RING for c in self.landed}
        per.update({self.hi_done: units, self.lo_done: units, self.used: units})
        return per

    def skip(self, units):
        self.next += units
        self.split_next += units

    def split(self):
        v, p = self.split_next, self.prog
        self.split_next += 1
        if v >= self.total and p.loop is None:
            return
        s = v % RING
        p.act.wait(self.landed[s].at(v // RING + 1), self.used.at(v - RING + 1))
        self.hi_done.up(p.nc.scalar.copy(self.hi[:, s, :], self.raw[:, s, :]))
        p.dve.wait(self.hi_done.at(v + 1))
        self.lo_done.up(p.nc.vector.tensor_tensor(
            self.lo[:, s, :], self.raw[:, s, :], self.hi[:, s, :].bitcast(F32), ALU.subtract))

    def catch_up(self):
        last = self.next - 1 + AHEAD
        if self.hold is not None:
            last = min(last, self.hold + RING - 1)
        while self.split_next <= last:
            self.split()

    def take(self, src):
        u, p = self.next, self.prog
        self.next += 1
        s, k, n = u % RING, src.shape[1], src.shape[-1]
        p.sp.wait(self.lo_done.at(u - RING + 1))
        if len(src.shape) == 3:
            self.landed[s].up(p.nc.sync.dma_start(
                self.raw[:, s, 0:k * n].rearrange("p (k n) -> p k n", k=k), src))
        else:
            heads = src.shape[2]
            n *= heads
            for q in range(k):
                last = q == k - 1
                if last:
                    p.sp.wait(self.parts.now())
                (self.landed[s] if last else self.parts).up(p.nc.sync.dma_start(
                    self.raw[:, s, q * n:(q + 1) * n].rearrange("p (h n) -> p h n", h=heads), src[:, q]))
        self.catch_up()
        p.pe.wait(self.lo_done.at(u + 1))
        return [t[:, s, 0:k * n].rearrange("p (k n) -> p k n", k=k) for t in (self.hi, self.lo)]


def product(nc, out, stat, mov, first, last):
    nc.tensor.matmul(out, stat[0], mov[0], start=first, stop=False)
    nc.tensor.matmul(out, stat[0], mov[1], start=False, stop=False)
    return nc.tensor.matmul(out, stat[1], mov[0], start=False, stop=last)


def rows(ap, n=P):
    return ap.rearrange("(k p) n -> p k n", p=n)


class Model:
    def __init__(self, nc, ctx, t, total):
        self.nc, self.t = nc, t
        p = self.p = Program(nc, ctx)
        self.pe, self.act, self.dve, self.pool, self.sp = p.pe, p.act, p.dve, p.pool, p.sp
        self.w = WeightStream(p, total)
        self.loads = [Count(p, f"load{i}", 16) for i in range(8)]
        self.load_turn = 0
        self.par_loads = Count(p, "parameter_loads", 16)
        self.const_loads = Count(p, "constant_loads", 16)
        self.stores = Count(p, "stores", 16)
        self.psum = ctx.enter_context(nc.psum_tensor("psum", [P, 8, BANK], F32))
        self.bank_free = [[] for _ in range(8)]
        self.turn, self.accumulating = 0, False
        self.x_tok = p.sbuf("x_tok", [P, TB, D])
        self.n_tok = p.sbuf("n_tok", [P, TB, D])
        self.x_ready, self.n_busy = [], []
        self.normed, self.squared, self.factor = [None] * TB, [None] * TB, [None] * TB
        self.xt = self.split_operand("xt", KT)
        self.hid = self.split_operand("hid", 2)
        self.fresh = p.sbuf("fresh", [P, 2, 2, SEQ])
        self.fresh_busy = [[], []]
        self.fresh_turn = 0
        self.gain_row = p.sbuf("gain_row", [P, D])
        self.bias_row = p.sbuf("bias_row", [P, D])
        self.row_busy = []
        self.ident = p.sbuf("ident", [P, P])
        self.rope_cos = p.sbuf("rope_cos", [P, TB, HD])
        self.rope_sin = p.sbuf("rope_sin", [P, TB, HD])
        self.mask = p.sbuf("mask", [P, P + SEQ])
        self.mask_busy = []
        self.mem_kt = p.sbuf("mem_kt", [P, KT, SEQ])
        self.mem_v = p.sbuf("mem_v", [P, TB, D])
        self.qt = p.sbuf("qt", [P, KT, SEQ])
        self.kt = p.sbuf("kt", [P, KT, SEQ])
        self.v = p.sbuf("v", [P, TB, D])
        self.qrt = p.sbuf("qrt", [P, 4, SEQ])
        self.krt = p.sbuf("krt", [P, 2, SEQ])
        self.e = p.sbuf("e", [P, 2, 2, TB * SEQ])
        self.pt = p.sbuf("pt", [P, 2, 2, TB * SEQ])
        self.tok = p.sbuf("tok", [P, TB, D])
        self.tok_busy = []
        self.swap = p.sbuf("swap", [P, BANK])
        self.swap_busy = []
        self.stat = p.sbuf("stat", [P, 2, 4, 4])
        self.norm = p.sbuf("norm", [P, 32])
        self.eps_pow = p.sbuf("eps_pow", [P, 2])
        self.small = p.sbuf("small", [P, 8, 24])
        self.zeros = p.sbuf("zeros", [P, BANK], F32R)
        self.zeros_done = self.dve([], lambda e: e.memset(self.zeros[:].bitcast(F32), 0.0))
        self.half_neg = self.pool([], lambda e: e.memset(self.eps_pow[:], -0.5))
        for dst, src in ((self.ident[:], t["c_ident"]), (self.rope_cos[:], rows(t["c_cos"])),
                         (self.rope_sin[:], rows(t["c_sin"]))):
            self.load(dst, src, (), self.const_loads)
        self.consts = self.const_loads.now()


    def split_operand(self, name, tiles):
        return Split(*[self.p.sbuf(f"{name}_{part}", [P, tiles, SEQ], F32R)[:] for part in ("hi", "lo")])

    def load(self, dst, src, after=(), count=None):
        if count is None:
            count = self.loads[self.load_turn % len(self.loads)]
            self.load_turn += 1
            self.pool.wait(count.now())
        self.pool.wait(*after)
        with self.nc.allow_non_contiguous_dma(reason="small parameter"):
            ins = self.nc.gpsimd.dma_start(dst, src)
        return count.up(ins)

    def bank(self):
        k = 4 + self.turn % 4 if self.accumulating else self.turn % 8
        self.turn += 1
        self.pe.wait(*self.bank_free[k])
        return k

    def params(self):
        t = self.t
        tile = lambda ap: ap.rearrange("t (m p) -> (t m) p", p=P)
        vec = lambda ap: ap.rearrange("(m p) -> m p", p=P)
        batches, self.col = [], {}
        half = (TAPS + 1) * 2 * FT // 2
        for name, w, b, depth in (("f", t["f_conv_w"], t["f_conv_b"], DEPTH),
                                  ("g", t["conv_w_2"], t["conv_b_2"], DEPTH_2)):
            for l in range(depth):
                taps = tile(w[l])
                batches.append(((name, l), [taps[0:half]]))
                batches.append((None, [taps[half:TAPS * 2 * FT], vec(b[l])]))
        batches.append(("ln_g", [tile(t["ln_g"].rearrange("l k n -> (l k) n"))]))
        batches.append(("ln_b", [tile(t["ln_b"].rearrange("l k n -> (l k) n"))]))
        batches.append(("norms_2", [tile(t["norm_mix_2"]), tile(t["norm_mem_2"]), tile(t["norm_ffn_2"])]))
        batches.append(("lru", [tile(t["b_conv_w"][0]), tile(t["b_conv_b"]), tile(t["b_b_rgate"]),
                                tile(t["b_b_igate"]), tile(t["b_lambda"]), tile(t["c_q_norm"]),
                                tile(t["c_kv_norm"])]))
        total = sum(a.shape[0] for _, parts in batches for a in parts)
        self.par = self.p.sbuf("par", [P, total])
        stage = self.e[:].rearrange("p a b n -> p (a b n)")
        self.par_jobs = []
        at = 0
        for j, (name, parts) in enumerate(batches):
            if name is not None:
                self.col[name] = at
            r = 0
            for a in parts:
                self.load(stage[r:r + a.shape[0], j * P:(j + 1) * P], a, (), self.par_loads)
                r += a.shape[0]
            self.par_jobs.append((stage[0:r, j * P:(j + 1) * P], r, at))
            at += r
        self.par_loaded = self.par_loads.now()

    def turn_params(self):
        for src, r, at in self.par_jobs:
            k = self.bank()
            m = self.pe([self.par_loaded, self.consts],
                        lambda e: e.transpose(self.psum[:, k, 0:r], src, self.ident[0:r, 0:r]))
            m = self.act([m], lambda e: e.copy(self.par[:, at:at + r], self.psum[:, k, 0:r]))
            self.bank_free[k] = [m]
        self.par_ready = m
        self.dve.wait(m)

    def cols(self, name, off, n):
        a = self.col[name] + off
        return self.par[:, a:a + n]

    def split_out(self, dst, tiles, src, after=(), scale=None):
        hi, lo = dst.hi[:, tiles, :], dst.lo[:, tiles, :]
        m = self.act([*after, *dst.busy], lambda e: e.copy(hi, src))
        m2 = self.dve([m], lambda e: e.tensor_tensor(lo, src, hi.bitcast(F32), ALU.subtract))
        for j in range(tiles.start, tiles.stop):
            dst.ready[j] = [m2]
        return m2

    def to_features(self, src, ntiles, dst, tile0, after, gain=None, bias=None):
        banks, marks = {}, {}
        for b in range(TB):
            self.pe.wait(self.consts)
            self.pe.wait(after[b])
            for j in range(ntiles):
                if j % 2 == 0 and b == 0:
                    banks[j] = self.bank()
                k = banks[j - j % 2]
                ins = self.nc.tensor.transpose(
                    self.psum[:, k, (j % 2) * SEQ + b * P:(j % 2) * SEQ + (b + 1) * P], src(b, j), self.ident[:])
                if b == TB - 1 and (j % 2 == 1 or j == ntiles - 1):
                    marks[j - j % 2] = self.pe.done.up(ins)
        scaled = None
        for j, m in marks.items():
            k, nt = banks[j], min(2, ntiles - j)
            out = self.psum[:, k, :].rearrange("p (a n) -> p a n", a=2)
            tiles = slice(tile0 + j, tile0 + j + nt)
            if gain is None:
                self.bank_free[k] = [self.split_out(dst, tiles, out[:, 0:nt, :], [m])]
                continue
            f = self.fresh_turn % 2
            self.fresh_turn += 1
            tmp = self.fresh[:, f]
            m1 = self.act([m, *self.fresh_busy[f]], lambda e: e.activation(
                tmp[:, 0, :], out[:, 0, :], ACT.Identity, scale=gain[:, j:j + 1],
                bias=0.0 if bias is None else bias[:, j:j + 1]))
            if nt == 2:
                g = gain[:, j + 1:j + 2]
                if bias is None:
                    m1 = self.dve([m1], lambda e: e.tensor_scalar(tmp[:, 1, :], out[:, 1, :], g, None, ALU.mult))
                else:
                    m1 = self.dve([m1], lambda e: e.tensor_scalar(
                        tmp[:, 1, :], out[:, 1, :], g, bias[:, j + 1:j + 2], ALU.mult, ALU.add))
            self.bank_free[k] = [m1]
            if scaled is not None:
                self.split_scaled(dst, *scaled)
            scaled = (f, tiles, nt, m1)
        if scaled is not None:
            self.split_scaled(dst, *scaled)

    def split_scaled(self, dst, f, tiles, nt, m):
        self.fresh_busy[f] = [self.split_out(dst, tiles, self.fresh[:, f, 0:nt, :], [m])]

    def rsqrt(self, src, col, eps, after):
        r = self.norm[:, col:col + 2]
        m = self.dve(after, lambda e: e.tensor_scalar(r, src, eps, None, ALU.add))
        return self.pool([m, self.half_neg], lambda e: e.tensor_tensor(r, r, self.eps_pow[:], ALU.pow))

    def feature_out(self, out, unit, x, x0=0):
        hi, lo = unit
        n = hi.shape[1]
        for k in range(n):
            self.pe.wait(x.ready[x0 + k])
            ins = product(self.nc, out, (hi[:, k, :], lo[:, k, :]),
                          (x.hi[:, x0 + k, :], x.lo[:, x0 + k, :]), k == 0, k == n - 1)
        return ins

    def token_out(self, outs, units, x, ktiles, between=None):
        k0 = 0
        for u, src in enumerate(units):
            if between is not None and u == between[0]:
                between[1]()
            hi, lo = self.w.take(src)
            kn = hi.shape[1]
            for b in range(TB):
                tb = slice(b * P, (b + 1) * P)
                for k in range(kn):
                    self.pe.wait(x.ready[k0 + k])
                    ins = product(self.nc, outs[b], (x.hi[:, k0 + k, tb], x.lo[:, k0 + k, tb]),
                                  (hi[:, k, :], lo[:, k, :]), k0 + k == 0, k0 + k == ktiles - 1)
            k0 += kn
            m = self.w.used.up(ins)
        x.busy = [m]
        return m

    def project_features(self, w, col0, tiles, dst, x, scale=None):
        j0 = 0
        if w.shape[0] == D:
            ks = [self.bank(), self.bank()]
            units = [self.w.take(rows(w)[:, :, col0 + j * P:col0 + (j + 1) * P]) for j in range(2)]
            for k in range(KT):
                self.pe.wait(x.ready[k])
                for (hi, lo), b in zip(units, ks):
                    ins = product(self.nc, self.psum[:, b, 0:SEQ], (hi[:, k, :], lo[:, k, :]),
                                  (x.hi[:, k, :], x.lo[:, k, :]), k == 0, k == KT - 1)
                    if k == KT - 1:
                        m = self.w.used.up(ins)
                        m1 = self.copy_out(dst, ks.index(b), 1, self.psum[:, b:b + 1, 0:SEQ], m, scale)
                        self.bank_free[b] = [m1]
            j0 = 2
        for j in range(j0, tiles, 2):
            nt = min(2, tiles - j)
            k = self.bank()
            out = self.psum[:, k, :].rearrange("p (a n) -> p a n", a=2)
            for a in range(nt):
                c = col0 + (j + a) * P
                unit = self.w.take(rows(w)[:, :, c:c + P])
                m = self.w.used.up(self.feature_out(out[:, a, :], unit, x))
            m1 = self.copy_out(dst, j, nt, out[:, 0:nt, :], m, scale)
            self.bank_free[k] = [m1]
        x.busy = [m]
        return m1

    def project_tokens(self, w, col0, n, x, between=None):
        kn = 2 if n > 256 else 4 if n > P else KT
        ks = [self.bank() for _ in range(TB)]
        outs = [self.psum[:, k, 0:n] for k in ks]
        units = [rows(w)[:, j:j + kn, col0:col0 + n] for j in range(0, KT, kn)]
        m = self.token_out(outs, units, x, KT, between)
        return ks, outs, m

    def out_project(self, w, x, part_done):
        half = lambda c: [rows(w)[:, j:j + 2, c * BANK:(c + 1) * BANK] for j in range(0, KT, 2)]
        for b in range(TB):
            self.pe.wait(*self.bank_free[2 * b])
        m = self.token_out([self.psum[:, 2 * b, :] for b in range(TB)], half(0), x, KT)
        for b in range(TB):
            self.pe.wait(*self.bank_free[2 * b + 1])
        self.w.hold = self.w.next
        for b in range(TB):
            part_done(b, 0, m)
        units = [self.w.take(src) for src in half(1)]
        for b in range(TB):
            tb = slice(b * P, (b + 1) * P)
            for k in range(KT):
                hi, lo = units[k // 2]
                ins = product(self.nc, self.psum[:, 2 * b + 1, :], (x.hi[:, k, tb], x.lo[:, k, tb]),
                              (hi[:, k % 2, :], lo[:, k % 2, :]), k == 0, k == KT - 1)
                if b == TB - 1 and k % 2 == 1:
                    m = self.w.used.up(ins)
            if b < TB - 1:
                m = self.pe.done.up(ins)
            part_done(b, 1, m)
        self.w.hold = None
        x.busy = [m]

    def rope(self, src, heads, b, dst, after):
        src = src.rearrange("p (h d) -> p h d", d=HD)
        cos = self.rope_cos[:, b, :].unsqueeze(1).broadcast_to([P, heads, HD])
        sin = self.rope_sin[:, b, :].unsqueeze(1).broadcast_to([P, heads, HD])
        swap = self.swap[:, 0:heads * HD].rearrange("p (h d) -> p h d", d=HD)
        h = HD // 2
        self.dve(after, lambda e: e.tensor_tensor(dst, src, cos, ALU.mult))
        self.dve(self.swap_busy, lambda e: e.tensor_tensor(swap[:, :, 0:h], src[:, :, h:HD], sin[:, :, 0:h],
                                                           ALU.mult))
        m = self.dve([], lambda e: e.tensor_tensor(swap[:, :, h:HD], src[:, :, 0:h], sin[:, :, h:HD], ALU.mult))
        done = self.dve([m], lambda e: e.tensor_tensor(dst, dst, swap, ALU.add))
        self.swap_busy = [done]
        return m, done

    def turn_half(self, half, ntiles, dst, done):
        m = self.turn_tokens(lambda b, i: self.tok[:, b, half * BANK + i * P:half * BANK + (i + 1) * P],
                             ntiles, dst, [done])
        self.tok_half_busy[half] = self.tok_busy
        return m

    def rotated(self, w, col, n, half, dst, waiting):
        ks, outs, m = self.project_tokens(w, col, n, self.xt)
        for b in range(TB):
            read, done = self.rope(outs[b], n // HD, b, self.tok[:, b, half * BANK:half * BANK + n].rearrange(
                "p (h d) -> p h d", d=HD), [m, *self.tok_half_busy[half]])
            self.bank_free[ks[b]] = [read]
        if waiting is not None:
            self.turn_half(*waiting)
        return (half, n // P, dst, done)

    def copy_out(self, dst, j, nt, src, m, scale=None):
        copy = lambda d, v: self.act([m], lambda e: e.copy(d, v) if scale is None else e.activation(
            d, v, ACT.Copy, scale=scale))
        if not callable(dst):
            return copy(dst[:, j:j + nt, :], src)
        for half in range(2):
            ps = slice(half * HD, (half + 1) * HD)
            for a in range(nt):
                mark = copy(dst(2 * (j + a) + half)[ps, :], src[ps, a, :])
        return mark

    def zero_padding(self, tiles):
        after = [lane.done.now() for lane in (self.pe, self.act, self.dve)]
        for half in range(2):
            mark = self.dve(after, lambda e: e.memset(
                tiles[(1 - half) * HD:(2 - half) * HD, half:tiles.shape[1]:2, :], 0.0))
        return mark

    def turn_tokens(self, src, ntiles, dst, after):
        for j in range(0, ntiles, 2):
            nt = min(2, ntiles - j)
            k = self.bank()
            out = self.psum[:, k, :].rearrange("p (a n) -> p a n", a=2)
            self.pe.wait(*after)
            for a in range(nt):
                for b in range(TB):
                    ins = self.nc.tensor.transpose(out[:, a, b * P:(b + 1) * P], src(b, j + a), self.ident[:])
            m = self.pe.done.up(ins)
            m1 = self.copy_out(dst, j, nt, out[:, 0:nt, :], m)
            self.bank_free[k] = [m1]
        self.tok_busy = [m]
        return m1

    def attend(self, groups, per, score, value, dst, ready, scale=1.0, mask=False, row_add=None,
               sink=None):
        nc = self.nc
        if mask:
            self.dve.wait(*self.mask_in)
            keys = [slice(0, P), slice(P, P + SEQ)]
            turned = [(slice(0, SEQ), 0), (slice(SEQ, SEQ + P), P)]
            width = P + SEQ
        else:
            keys = [slice(b * SEQ, (b + 1) * SEQ) for b in range(TB)]
            turned = [(slice(c * SEQ, (c + 1) * SEQ), 0) for c in range(TB)]
            width = TB * SEQ
        self.pe.wait(*ready)
        pt_busy, e_busy = [[], []], [[], []]

        def scores(g):
            banks = []
            for h in groups[g][0]:
                k = self.bank()
                banks.append((k, self.pe.done.up(score(h, lambda b: self.psum[:, k, keys[b]]))))
            return banks

        def split_output(out):
            if out is not None:
                k, tiles, m = out
                nt = tiles.stop - tiles.start
                part = self.psum[:, k, 0:nt * SEQ].rearrange("p (a n) -> p a n", a=nt)
                self.bank_free[k] = [self.split_out(dst, tiles, part, [m])]

        def exponentials(g, banks, out):
            s, (heads, tiles) = g % 2, groups[g]
            n = per * TB
            self.dve.wait(*e_busy[s])
            mx, nm, sm, rs = (self.stat[:, s, q, 0:n] for q in range(4))
            sources, es = [], None
            for i, (h, (k, m)) in enumerate(zip(heads, banks)):
                src = self.psum[:, k, :]
                if mask:
                    e = self.e[:, s, i, :]
                    if row_add is None:
                        m = self.dve([m], lambda v: v.scalar_tensor_tensor(
                            e[:, 0:width], src[:, 0:width], scale, self.mask[:, 0:width],
                            ALU.mult, ALU.add))
                    else:
                        for b in range(TB):
                            m = self.dve([m], lambda v: v.scalar_tensor_tensor(
                                e[:, keys[b]], src[:, keys[b]], row_add(h, b), self.mask[:, keys[b]],
                                ALU.add, ALU.add))
                    self.bank_free[k] = [m]
                    src = e
                    for b in range(TB):
                        m = self.dve([m] if b == 0 else [], lambda v: v.tensor_reduce(
                            mx[:, TB * i + b:TB * i + b + 1], src[:, keys[b]], AX, ALU.max))
                else:
                    m = self.dve([m], lambda v: v.tensor_reduce(
                        mx[:, TB * i:TB * i + TB], src.rearrange("p (b n) -> p b n", b=TB), AX, ALU.max))
                sources.append((src, k))
            if sink is not None:
                h0 = heads[0] * TB
                m = self.dve([m], lambda v: v.tensor_tensor(mx, mx, sink[:, h0:h0 + n], ALU.max))
            nm_done = m = self.dve([m], lambda v: v.tensor_scalar(
                nm, mx, -(1.0 if mask else scale), None, ALU.mult))
            if sink is not None:
                es = self.small[:, s, 0:n]
                m = self.dve([m], lambda v: v.tensor_tensor(es, nm, sink[:, h0:h0 + n], ALU.add))
            split_output(out)
            if sink is not None:
                self.act([m], lambda v: v.activation(es, es, ACT.Exp))
            for i, (src, k) in enumerate(sources):
                for b in range(TB):
                    m = self.act([nm_done], lambda v: v.activation(
                        self.e[:, s, i, keys[b]], src[:, keys[b]], ACT.Exp,
                        bias=nm[:, TB * i + b:TB * i + b + 1], scale=1.0 if mask else scale,
                        accum_out=sm[:, TB * i + b:TB * i + b + 1]))
                if not mask:
                    self.bank_free[k] = [m]
            return (s, heads, tiles, sm, rs, m, es)

        def values(group):
            s, heads, tiles, mt = group
            k = self.bank()
            for i, h in enumerate(heads):
                self.pe.wait(mt[i])
                for slot, p0, wide, vals in value(h):
                    for c, (cols, q0) in enumerate(turned):
                        ins = nc.tensor.matmul(
                            self.psum[p0:p0 + wide, k, slot * SEQ + q0:(slot + 1) * SEQ], vals(c),
                            self.pt[:, s, i, cols], start=c == 0, stop=c == TB - 1)
            m = self.pe.done.up(ins)
            pt_busy[s] = [m]
            return (k, tiles, m)

        def normalise(group):
            s, heads, tiles, sm, rs, after, es = group
            if sink is not None:
                after = self.dve([after], lambda v: v.tensor_tensor(sm, sm, es, ALU.add))
            m = self.dve([after], lambda v: v.reciprocal(rs, sm))
            marks = []
            for i in range(len(heads)):
                for b in range(TB):
                    e = self.e[:, s, i, keys[b]]
                    mn = self.dve([m], lambda v: v.tensor_scalar(
                        e, e, rs[:, TB * i + b:TB * i + b + 1], None, ALU.mult))
                marks.append(mn)
            return marks

        def transposes(group, normed):
            s, heads, tiles = group[0:3]
            marks = []
            for i, h in enumerate(heads):
                k = self.bank()
                self.pe.wait(normed[i])
                for c, (cols, q0) in enumerate(turned):
                    for b in range(q0 // P, TB):
                        ins = nc.tensor.transpose(
                            self.psum[:, k, cols.start + b * P - q0:cols.start + (b + 1) * P - q0],
                            self.e[:, s, i, keys[b].start + c * P:keys[b].start + (c + 1) * P],
                            self.ident[:])
                m = self.pe.done.up(ins)
                mt = self.act([m, *pt_busy[s]], lambda v: v.copy(
                    self.pt[:, s, i, 0:width], self.psum[:, k, 0:width]))
                self.bank_free[k] = [mt]
                marks.append(mt)
            e_busy[s] = [m]
            return (s, heads, tiles, marks)

        n = len(groups)
        banks = scores(0)
        expd = turned_over = out = None
        for g in range(n + 2):
            ahead = scores(g + 1) if g + 1 < n else None
            if g < n:
                current, out = exponentials(g, banks, out), None
            else:
                current = None
            normed = normalise(expd) if expd is not None else None
            if out is not None:
                split_output(out)
            out = values(turned_over) if turned_over is not None else None
            turned_over = transposes(expd, normed) if expd is not None else None
            banks, expd = ahead, current
        split_output(out)


    def norm_sink(self, l, k, last=False):
        t, busy = self.t, self.row_busy
        ld1 = self.load(self.gain_row[:], t["ln_g"][l, k].partition_broadcast(P), busy)
        ld2 = self.load(self.bias_row[:], t["ln_b"][l, k].partition_broadcast(P))
        self.rows_in = [ld1, ld2]
        self.normed = [None] * TB
        stats = self.small[:, 2:4, 0:12]
        mv = self.norm[:, 0:4].rearrange("p (b s) -> p b s", b=TB)

        def part(b, c, mark):
            cs = slice(c * BANK, (c + 1) * BANK)
            z = self.n_tok[:, b, :]
            if b == TB - 1 and c == 1:
                self.norm_apply(0)
                if last:
                    self.last_x(0)
            m = self.dve([mark, *self.x_ready, *self.n_busy], lambda e: e.scalar_tensor_tensor(
                z[:, cs], self.x_tok[:, b, cs], ALPHA, self.psum[:, 2 * b + c, :], ALU.mult, ALU.add))
            self.bank_free[2 * b + c] = [m]
            m = self.dve([m], lambda e: e.bn_stats(stats[:, b, 6 * c:6 * c + 6], z[:, cs]))
            if c == 1:
                m = self.dve([m], lambda e: e.bn_aggr(mv[:, b, :], stats[:, b, :]))
                r = self.norm[:, 4 + b:5 + b]
                m = self.dve([m], lambda e: e.tensor_scalar(r, mv[:, b, 1:2], LN_EPS, None, ALU.add))
                m = self.pool([m, self.half_neg], lambda e: e.tensor_tensor(r, r, self.eps_pow[:, 0:1], ALU.pow))
                self.normed[b] = (m, z, mv[:, b, 0:1], r)
        return part

    def norm_apply(self, b):
        m, z, mean, r = self.normed[b]
        self.normed[b] = self.dve([m], lambda e: e.tensor_scalar(z, z, mean, r, ALU.subtract, ALU.mult))

    def norm_finish(self, l, k):
        idx = l * 3 + k
        self.norm_apply(1)
        done = self.normed[1]
        self.to_features(lambda b, j: self.n_tok[:, b, j * P:(j + 1) * P], KT, self.xt, 0,
                         self.normed, self.cols("ln_g", idx * KT, KT), self.cols("ln_b", idx * KT, KT))
        pe_read = self.pe.done.now()
        for b in range(TB):
            z, x = self.n_tok[:, b, :], self.x_tok[:, b, :]
            m = self.pool([done, *self.rows_in], lambda e: e.tensor_tensor(x, z, self.gain_row[:], ALU.mult))
            m = self.pool([m], lambda e: e.tensor_tensor(x, x, self.bias_row[:], ALU.add))
        self.x_ready = self.row_busy = [m]
        self.n_busy = [m, pe_read]

    def last_x(self, b):
        z, x = self.n_tok[:, b, :], self.x_tok[:, b, :]
        m = self.dve([self.normed[b], *self.rows_in], lambda e: e.tensor_tensor(x, z, self.gain_row[:], ALU.mult))
        m = self.dve([m], lambda e: e.tensor_tensor(x, x, self.bias_row[:], ALU.add))
        for c in range(2):
            self.squares(b, c, m)
        self.x_ready = self.row_busy = self.n_busy = [m]

    def norm_finish_last(self):
        self.norm_apply(1)
        self.rms_factor(0)
        self.last_x(1)
        self.rms_apply(0)
        self.rms_factor(1)

    def squares(self, b, c, mark):
        if b == 0 and c == 0:
            mark = [mark, self.act.done.now()]
        self.squared[b] = self.act([mark], lambda e: e.activation(
            self.e[:, b, c, :], self.x_tok[:, b, c * BANK:(c + 1) * BANK], ACT.Square,
            accum_out=self.norm[:, 16 + 2 * b + c:17 + 2 * b + c]))

    def rms_factor(self, b):
        r = self.norm[:, 20 + b:21 + b]
        part = [self.norm[:, 16 + 2 * b + c:17 + 2 * b + c] for c in range(2)]
        m = self.dve([self.squared[b]], lambda e: e.tensor_tensor(r, part[0], part[1], ALU.add))
        m = self.dve([m], lambda e: e.tensor_scalar(r, r, 1.0 / D, RMS_EPS, ALU.mult, ALU.add))
        self.factor[b] = self.pool([m, self.half_neg], lambda e: e.tensor_tensor(
            r, r, self.eps_pow[:, 0:1], ALU.pow))

    def rms_apply(self, b):
        self.normed[b] = self.dve([self.factor[b], *self.n_busy], lambda e: e.tensor_scalar(
            self.n_tok[:, b, :], self.x_tok[:, b, :], self.norm[:, 20 + b:21 + b], None, ALU.mult))

    def rms(self, src, width, dst, after, col, busy=()):
        before = self.act.done.now()
        squares = self.e[:].rearrange("p a b n -> p (a b n)")
        for b in range(TB):
            m = self.act([*after, before], lambda e: e.activation(
                squares[:, b * D:b * D + width], src(b), ACT.Square,
                accum_out=self.norm[:, col + b:col + b + 1]))
        m = self.dve([m], lambda e: e.tensor_scalar(
            self.norm[:, col:col + 2], self.norm[:, col:col + 2], 1.0 / width, None, ALU.mult))
        r = self.rsqrt(self.norm[:, col:col + 2], col + 2, RMS_EPS, [m])
        for b in range(TB):
            m = self.dve([r, *busy], lambda e: e.tensor_scalar(
                dst(b), src(b), self.norm[:, col + 2 + b:col + 3 + b], None, ALU.mult))
        return m

    def log1p(self, e, s, w, after):
        m = self.dve(after, lambda v: v.tensor_scalar(w, e, 2.0, None, ALU.add))
        m = self.dve([m], lambda v: v.reciprocal(w, w))
        m = self.dve([m], lambda v: v.tensor_tensor(s, e, w, ALU.mult))
        m = self.dve([m], lambda v: v.tensor_tensor(w, s, s, ALU.mult))
        m = self.dve([m], lambda v: v.tensor_scalar(e, w, 1.0 / 15, None, ALU.mult))
        for c in (13, 11, 9, 7, 5, 3):
            m = self.dve([m], lambda v: v.scalar_tensor_tensor(e, e, 1.0 / c, w, ALU.add, ALU.mult))
        m = self.dve([m], lambda v: v.scalar_tensor_tensor(s, e, 1.0, s, ALU.add, ALU.mult))
        return self.dve([m], lambda v: v.tensor_scalar(s, s, 2.0, None, ALU.mult))


    def mem_keys_values(self):
        t = self.t
        first = Count(self.p, "memory_load", 16)
        landed = [first.up(self.nc.sync.dma_start(self.tok[:, b, :], t["mem"][b * P:(b + 1) * P, :]))
                  for b in range(TB)]
        self.sp.wait(landed[-1])
        self.params()
        self.x_ready = [self.load(self.x_tok[:], rows(t["x"]))]
        self.to_features(lambda b, j: self.tok[:, b, j * P:(j + 1) * P], KT, self.xt, 0, [landed[-1]] * TB)
        self.tok_busy = [self.pe.done.now()]
        m = self.project_features(t["mem_w_kv"], 0, KT, self.mem_kt, self.xt)
        for c in range(2):
            ks, outs, m = self.project_tokens(t["mem_w_kv"], D + c * BANK, BANK, self.xt)
            for b in range(TB):
                m1 = self.act([m], lambda e: e.copy(self.mem_v[:, b, c * BANK:(c + 1) * BANK], outs[b]))
                self.bank_free[ks[b]] = [m1]
        self.mem_ready = m1

    def load_mask(self, name):
        src = self.t[name]
        self.mask_in = [self.load(self.mask[:, 0:P], src[0:P, 0:P], [self.dve.done.now()]),
                        self.load(self.mask[:, P:P + SEQ], src[P:SEQ, :])]

    def sliding_attention(self, j, part_done):
        t, nc = self.t, self.nc
        w = t["a_w_qkv"][j]
        zeroed = self.zero_padding(self.kt)
        padded = lambda i: self.kt[:, i, :]
        self.load_mask("c_mask_window")
        m = self.load(self.small[:, 4, 0:A_HEADS], t["a_sinks"][j].partition_broadcast(P))
        sink = self.qrt[:, 0, 0:A_HEADS * TB]
        self.dve([m], lambda e: e.tensor_copy(
            sink.rearrange("p (h b) -> p h b", b=TB),
            self.small[:, 4, 0:A_HEADS].unsqueeze(2).broadcast_to([P, A_HEADS, TB])))
        kw = A_KV * HD
        ks, outs, m = self.project_tokens(w, 2 * BANK, kw, self.xt)
        for b in range(TB):
            keys = self.tok[:, b, 0:2 * kw].rearrange("p (h c d) -> p h c d", c=2, d=HD)
            read, done = self.rope(outs[b], A_KV, b, keys[:, :, 0, :], [m, *self.tok_busy])
            done = self.dve([done], lambda e: e.tensor_copy(keys[:, :, 1, :], keys[:, :, 0, :]))
            self.bank_free[ks[b]] = [read]
        self.tok_half_busy = [[], self.tok_busy]
        waiting = (0, A_KV, padded, done)
        for c in range(2):
            waiting = self.rotated(w, c * BANK, BANK, 1 - c, self.qt[:, 4 * c:4 * c + 4, :], waiting)
        ks, outs, m = self.project_tokens(w, 2 * BANK + kw, kw, self.xt)
        for b in range(TB):
            m1 = self.act([m], lambda e: e.copy(self.v[:, b, 0:kw], outs[b]))
            self.bank_free[ks[b]] = [m1]
        m = self.turn_half(*waiting)
        self.tok_busy = [self.pe.done.now()]

        def score(h, out):
            keys = padded(2 * (h // (A_HEADS // A_KV)) + h % 2)
            for b in range(TB):
                o = out(b)
                ins = nc.tensor.matmul(o, self.qt[:, h // 2, b * P:(b + 1) * P], keys[:, 0:o.shape[1]],
                                       start=True, stop=True)
            return ins

        def value(h):
            n = h // (A_HEADS // A_KV)
            return [(0, (h % 2) * HD, HD, lambda c: self.v[:, c, n * HD:(n + 1) * HD])]

        self.attend([([2 * g, 2 * g + 1], slice(g, g + 1)) for g in range(A_HEADS // 2)], 2,
                    score, value, self.xt, [m, m1, zeroed], HD ** -0.5, mask=True, sink=sink)
        self.out_project(t["a_w_o"][j], self.xt, part_done)

    def recurrent_block(self, part_done):
        t = self.t
        w, lru = t["b_w_in"][0], lambda off, n=1: self.cols("lru", off, n)
        conv_b, b_r, b_i, lam = (LRU_TAPS * KT + q * KT for q in range(4))
        gate, u = self.qt, self.kt
        self.accumulating = True
        r = self.v[:].rearrange("p b (j n) -> p (b j) n", n=SEQ)
        ig = self.e[:].rearrange("p a b (c n) -> p (a b c) n", n=SEQ)

        def gate_products(j):
            self.pe.wait(*self.bank_free[j])
            for a in range(2):
                c = (2 * j + a) * P
                m = self.w.used.up(self.feature_out(self.psum[:, j, a * SEQ:(a + 1) * SEQ],
                                                    self.w.take(rows(w)[:, :, c:c + P]), self.xt))
            return m

        ab, sp, w8, pos, neg = (self.small[:, q, 0:KT] for q in (0, 1, 5, 6, 7))
        lm = lru(lam, KT)
        m = self.dve([], lambda e: e.scalar_tensor_tensor(ab, lm, -1.0, lm, ALU.mult, ALU.max))
        m = self.act([m], lambda e: e.activation(ab, ab, ACT.Exp, scale=-1.0))
        m = self.log1p(ab, sp, w8, [m])
        self.dve([], lambda e: e.tensor_scalar(pos, lm, -1.0, 0.0, ALU.mult, ALU.max))
        m = self.dve([m, self.dve.done.now()], lambda e: e.tensor_tensor(sp, sp, pos, ALU.add))
        m = self.dve([m], lambda e: e.tensor_scalar(pos, sp, LRU_C, None, ALU.mult))
        lam_done = self.dve([m], lambda e: e.tensor_scalar(neg, sp, -LRU_C, None, ALU.mult))
        th = self.pt[:].rearrange("p a b (c n) -> p (a b c) n", n=SEQ)

        def conv_tiles(blk):
            for i in (2 * blk, 2 * blk + 1):
                k = self.bank()
                out = self.psum[:, k, 0:SEQ]
                unit = self.w.take(rows(w)[:, :, D + i * P:D + (i + 1) * P])
                m = self.w.used.up(self.feature_out(out, unit, self.xt))
                tap = lambda q: lru(q * KT + i)
                m = self.act([m], lambda e: e.activation(u[:, i, :], out, ACT.Identity,
                                                         scale=tap(LRU_TAPS - 1), bias=lru(conv_b + i)))
                for d in range(1, LRU_TAPS):
                    m = self.dve([m], lambda e: e.scalar_tensor_tensor(
                        u[:, i, d:SEQ], out[:, 0:SEQ - d], tap(LRU_TAPS - 1 - d), u[:, i, d:SEQ],
                        ALU.mult, ALU.add))
                self.bank_free[k] = [m]
            return m

        def sigmoids(blk):
            for name, dst, bias in (("b_w_rgate", r, b_r), ("b_w_igate", ig, b_i)):
                hi, lo = self.w.take(rows(t[name][0, blk]))
                k = self.bank()
                out = self.psum[:, k, :].rearrange("p (a n) -> p a n", a=2)
                for a in range(2):
                    cs = slice(a * P, (a + 1) * P)
                    ins = self.feature_out(out[:, a, :], (hi[:, :, cs], lo[:, :, cs]), self.hid)
                m = self.w.used.up(ins)
                for a in range(2):
                    jt = 2 * blk + a
                    m1 = self.act([m], lambda e: e.activation(dst[:, jt, :], out[:, a, :], ACT.Sigmoid,
                                                              bias=lru(bias + jt)))
                self.bank_free[k] = [m1]
            self.hid.busy = [m]
            return m1

        def decays(h, gates):
            for j in range(h.start, h.stop):
                mt = self.act([gates, lam_done], lambda e: e.activation(
                    th[:, j, :], r[:, j, :], ACT.Tanh, scale=pos[:, j:j + 1]))
            for j in range(h.start, h.stop):
                ma = self.act([mt], lambda e: e.activation(r[:, j, :], r[:, j, :], ACT.Exp, scale=neg[:, j:j + 1]))
            m = self.pool([gates], lambda e: e.tensor_tensor(ig[:, h, :], ig[:, h, :], u[:, h, :], ALU.mult))
            m = self.dve([ma, m], lambda e: e.tensor_tensor(u[:, h, :], r[:, h, :], r[:, h, :], ALU.mult))
            return ma, self.dve([m], lambda e: e.scalar_tensor_tensor(
                th[:, h, :], u[:, h, :], 1.0, th[:, h, :], ALU.add, ALU.mult))

        halves = [slice(0, KT // 2), slice(KT // 2, KT)]
        for blk in range(KT // 2):
            m = conv_tiles(blk)
            if blk > 0:
                gates = sigmoids(blk - 1)
            if blk == 2:
                gates_0 = gates
            self.split_out(self.hid, slice(0, 2), u[:, 2 * blk:2 * blk + 2, :], [m])
        decayed = [decays(halves[0], gates_0)]
        gate_made = [gate_products(0)]
        gates = sigmoids(KT // 2 - 1)
        decayed.append(decays(halves[1], gates))
        gate_made.append(gate_products(1))
        roots = [self.act([m], lambda e: e.activation(th[:, h, :], th[:, h, :], ACT.Sqrt))
                 for h, (_, m) in zip(halves, decayed)]

        def gated(j, after):
            pair = slice(2 * j, 2 * j + 2)
            m = self.act([gate_made[j]], lambda e: e.activation(
                gate[:, pair, :], self.psum[:, j, :].rearrange("p (a n) -> p a n", a=2), ACT.Gelu_apprx_tanh))
            self.bank_free[j] = [m]
            return lambda: self.dve([m, after], lambda e: e.tensor_tensor(
                u[:, pair, :], u[:, pair, :], gate[:, pair, :], ALU.mult))

        made = []
        for h, m, (ma, _) in zip(halves, roots, decayed):
            m = self.dve([m], lambda e: e.tensor_tensor(th[:, h, :], th[:, h, :], ig[:, h, :], ALU.mult))
            for j in range(h.start, h.stop):
                m1 = self.dve([m, ma], lambda e: e.tensor_tensor_scan(u[:, j, :], r[:, j, :], th[:, j, :], 0.0,
                                                                      ALU.mult, ALU.add))
            if h.start == 0:
                made = [step() for step in [gated(0, m1), gated(1, m1)]]
            gate_made.append(gate_products(len(gate_made)))
        self.xt.busy = [self.w.used.now()]
        late = [gated(2, m1), gated(3, m1)]
        for j in range(KT // 2):
            pair = slice(2 * j, 2 * j + 2)
            m = made[j] if j < 2 else late[j - 2]()
            self.split_out(self.xt, pair, u[:, pair, :], [m])
        self.accumulating = False
        self.out_project(t["b_w_o"][0], self.xt, part_done)

    def latent_attention(self, part_done):
        t, nc = self.t, self.nc
        self.load_mask("c_mask_causal")
        zeroed = self.zero_padding(self.krt)
        c_kv = C_KVR + C_ROPE
        ks, outs, m = self.project_tokens(t["c_w_down"][0], C_QR, c_kv, self.xt)
        for b in range(TB):
            kv_in = self.act([m, *self.tok_busy], lambda e: e.copy(self.tok[:, b, C_QR:C_QR + c_kv], outs[b]))
            self.bank_free[ks[b]] = [kv_in]
        off = LRU_TAPS * KT + 4 * KT
        lat = lambda c0, n: (lambda b: self.tok[:, b, c0:c0 + n])
        dst = lambda c0, n: (lambda b: self.n_tok[:, b, c0:c0 + n])
        kv_normed = self.rms(lat(C_QR, C_KVR), C_KVR, dst(C_QR, C_KVR), [kv_in], 12, self.n_busy)
        kr = self.tok[:, :, 768:896].rearrange("p b (c d) -> p b c d", c=2)
        for b in range(TB):
            _, done = self.rope(self.tok[:, b, C_QR + C_KVR:C_QR + c_kv], 1, b, kr[:, b, 0:1, :], [kv_in])
            done = self.dve([done], lambda e: e.tensor_copy(kr[:, b, 1, :], kr[:, b, 0, :]))

        def turn_latent():
            self.to_features(lambda b, j: self.n_tok[:, b, C_QR + j * P:C_QR + (j + 1) * P], 2, self.hid, 0,
                             [kv_normed] * 2, self.cols("lru", off + 3, 2))
            self.turn_tokens(lambda b, i: self.tok[:, b, 768:896], 1,
                             lambda i: self.krt[:, i, :], [done])

        ks, outs, m = self.project_tokens(t["c_w_down"][0], 0, C_QR, self.xt, (3, turn_latent))
        for b in range(TB):
            q_in = self.act([m, *self.tok_busy], lambda e: e.copy(self.tok[:, b, 0:C_QR], outs[b]))
            self.bank_free[ks[b]] = [q_in]
        q_normed = self.rms(lat(0, C_QR), C_QR, dst(0, C_QR), [q_in], 8)
        kvw = C_NOPE + C_V
        wkv = rows(t["c_w_ukv"][0])
        for g in range(C_HEADS // 2):
            if g == C_HEADS // 2 - 1:
                self.to_features(lambda b, j: self.n_tok[:, b, j * P:(j + 1) * P], 3, self.xt, 0,
                                 [q_normed] * 2, self.cols("lru", off, 3))
                self.n_busy = [*self.n_busy, self.pe.done.now()]
            hi, lo = self.w.take(wkv[:, :, g * 2 * kvw:(g + 1) * 2 * kvw])
            k = self.bank()
            out = self.psum[:, k, :].rearrange("p (a n) -> p a n", a=2)
            for a in range(2):
                cs = slice(a * kvw, a * kvw + C_NOPE)
                ins = self.feature_out(out[:, a, :], (hi[:, :, cs], lo[:, :, cs]), self.hid)
            m = self.pe.done.up(ins)
            m1 = self.act([m], lambda e: e.copy(self.kt[:, 2 * g:2 * g + 2, :], out))
            self.bank_free[k] = [m1]
            k = self.bank()
            out = self.psum[:, k, :].rearrange("p (b n) -> p b n", b=TB)
            part = lambda a, q: a[:, q, :].rearrange("p (h d) -> p h d", h=2)[:, :, C_NOPE:kvw]
            for b in range(TB):
                tb = slice(b * P, (b + 1) * P)
                for q in range(2):
                    ins = product(nc, out[:, b, :].rearrange("p (h d) -> p h d", h=2),
                                  (self.hid.hi[:, q, tb], self.hid.lo[:, q, tb]),
                                  (part(hi, q), part(lo, q)), q == 0, q == 1)
            m = self.w.used.up(ins)
            v_done = self.act([m], lambda e: e.copy(self.v[:, :, g * 2 * C_V:(g + 1) * 2 * C_V], out))
            self.bank_free[k] = [v_done]
        wq = t["c_w_uq"][0].rearrange("(k p) (h n) -> p k h n", p=P, h=C_HEADS)
        for g in range(2):
            hi, lo = self.w.take(wq[:, :, 4 * g:4 * g + 4, C_NOPE:C_NOPE + C_ROPE])
            k = self.bank()
            out = self.psum[:, k, :].rearrange("p (b n) -> p b n", b=TB)
            for b in range(TB):
                tb = slice(b * P, (b + 1) * P)
                for q in range(3):
                    self.pe.wait(self.xt.ready[q])
                    ins = product(nc, out[:, b, :], (self.xt.hi[:, q, tb], self.xt.lo[:, q, tb]),
                                  (hi[:, q, :], lo[:, q, :]), q == 0, q == 2)
            m = self.w.used.up(ins)
            qr = self.tok[:, :, g * SEQ:(g + 1) * SEQ]
            for b in range(TB):
                read, done = self.rope(out[:, b, :], 4, b, qr[:, b, :].rearrange("p (h d) -> p h d", h=4), [m])
            self.bank_free[k] = [read]
        for g in range(C_HEADS // 2):
            hi, lo = self.w.take(wq[:, :, 2 * g:2 * g + 2, 0:C_NOPE])
            k = self.bank()
            out = self.psum[:, k, :].rearrange("p (a n) -> p a n", a=2)
            for a in range(2):
                cs = slice(a * C_NOPE, (a + 1) * C_NOPE)
                ins = self.feature_out(out[:, a, :], (hi[:, :, cs], lo[:, :, cs]), self.xt)
            m = self.w.used.up(ins)
            m1 = self.act([m], lambda e: e.copy(self.qt[:, 2 * g:2 * g + 2, :], out))
            self.bank_free[k] = [m1]
            if g == 2:
                self.turn_tokens(lambda b, i: self.tok[:, b, i * P:(i + 1) * P], C_HEADS // 2, self.qrt, [done])
        self.xt.busy = [m]

        def score(h, out):
            for b in range(TB):
                tb = slice(b * P, (b + 1) * P)
                o = out(b)
                n = o.shape[1]
                nc.tensor.matmul(o, self.qt[:, h, tb], self.kt[:, h, 0:n], start=True, stop=False)
                ins = nc.tensor.matmul(o, self.qrt[:, h // 2, tb], self.krt[:, h % 2, 0:n],
                                       start=False, stop=True)
            return ins

        self.attend([([2 * g, 2 * g + 1], slice(2 * g, 2 * g + 2)) for g in range(C_HEADS // 2)], 2, score,
                    lambda h: [(h % 2, 0, C_V, lambda c: self.v[:, c, h * C_V:(h + 1) * C_V])],
                    self.xt, [m1, v_done, zeroed], (C_NOPE + C_ROPE) ** -0.5, mask=True)
        self.out_project(t["c_w_o"][0], self.xt, part_done)

    def cross_attention(self, l, part_done):
        t, nc = self.t, self.nc
        m = self.project_features(t["x_w_q"][l], 0, KT, self.qt, self.xt)
        per_head = X_HD // P

        def score(h, out):
            for b in range(TB):
                for q in range(per_head):
                    ins = nc.tensor.matmul(out(b), self.qt[:, per_head * h + q, b * P:(b + 1) * P],
                                           self.mem_kt[:, per_head * h + q, :],
                                           start=q == 0, stop=q == per_head - 1)
            return ins

        def value(h):
            return [(q, 0, P, (lambda q: lambda c: self.mem_v[:, c, h * X_HD + q * P:h * X_HD + (q + 1) * P])(q))
                    for q in range(per_head)]

        self.attend([([h], slice(per_head * h, per_head * (h + 1))) for h in range(X_HEADS)], 1,
                    score, value, self.xt, [m, self.mem_ready], X_HD ** -0.5)
        self.out_project(t["x_w_o"][l], self.xt, part_done)

    def seed_accumulators(self):
        self.accumulating = True
        for k in range(4):
            self.pe.wait(self.zeros_done, *self.bank_free[k])
            self.nc.tensor.matmul(self.psum[:, k, :], self.zeros[:, 0:P], self.zeros[:], start=True,
                                  stop=False, skip_group_check=True)

    def feed_forward(self, up, down, params, silu_half):
        nc, w, psum = self.nc, self.w, self.psum
        up, down = rows(up), rows(down)
        c0 = self.col[params]
        conv, act_out = self.qt, self.kt
        hid = self.hid
        banks = [4 + (self.turn + q) % 4 for q in range(4)]
        slot_bank = [banks[0], banks[2]]
        V, A = self.dve.done, self.act.done
        v0 = V.n
        VT, AT = 6, 4

        def conv_tile(m, i):
            s = m % 2
            off = (lambda q: slice(c0 + q, c0 + q + 1)) if i is None else \
                  (lambda q: bass.ds(i * 2 + (c0 + q), 1))
            col = (lambda q: self.par[:, off(q)])
            out = psum[:, slot_bank[s], :].rearrange("p (a n) -> p a n", a=2)
            if m < 2:
                self.pe.wait(*self.bank_free[slot_bank[s]])
            else:
                self.pe.wait(V.at(v0 + VT * (m - 2) + 4))
            if m == 0:
                out = [out[:, 0, :], psum[:, banks[1], 0:SEQ]]
                self.pe.wait(*self.bank_free[banks[1]])
                units = [w.take(up[:, :, half * FT * P:half * FT * P + P]) for half in range(2)]
                for k in range(KT):
                    self.pe.wait(self.xt.ready[k])
                    for half, (hi, lo) in enumerate(units):
                        ins = product(nc, out[half], (hi[:, k, :], lo[:, k, :]),
                                      (self.xt.hi[:, k, :], self.xt.lo[:, k, :]), k == 0, k == KT - 1)
                        if k == KT - 1:
                            made = w.used.up(ins)
            else:
                out = [out[:, 0, :], out[:, 1, :]]
                for half in range(2):
                    c = slice((half * FT + m) * P, (half * FT + m + 1) * P) if i is None else \
                        bass.ds(i * (2 * P) + (half * FT + m) * P, P)
                    unit = w.take(up[:, :, c])
                    made = w.used.up(self.feature_out(out[half], unit, self.xt))
            freed = [down_tile(m - 2, i)] if m >= 2 else []
            self.act.wait(made)
            if m >= 2:
                self.act.wait(V.at(v0 + VT * (m - 2) + 5))
            for half in range(2):
                t = half * FT + m
                base = self.act([], lambda e: e.activation(
                    conv[:, 2 * s + half, :], out[half], ACT.Identity,
                    scale=col((TAPS - 1) * 2 * FT + t), bias=col(TAPS * 2 * FT + t)))
            self.dve.wait(base)
            order = (silu_half, 1 - silu_half)
            for d in range(1, TAPS):
                for half in order:
                    t = half * FT + m
                    cv = conv[:, 2 * s + half, :]
                    self.dve([V.at(V.n - 1)] if d > 1 else [], lambda e: e.scalar_tensor_tensor(
                        cv[:, d:SEQ], out[half][:, 0:SEQ - d], col((TAPS - 1 - d) * 2 * FT + t),
                        cv[:, d:SEQ], ALU.mult, ALU.add))
            conv_done = V.now()
            sil, prod = act_out[:, s, :], act_out[:, 2 + s, :]
            ms = self.act([V.at(V.n - 1)], lambda e: e.activation(sil, conv[:, 2 * s + silu_half, :], ACT.Silu))
            mp = self.dve([ms, conv_done], lambda e: e.tensor_tensor(
                prod, sil, conv[:, 2 * s + 1 - silu_half, :], ALU.mult))
            hi, lo = hid.hi[:, s, :], hid.lo[:, s, :]
            mh = self.act([mp, *freed], lambda e: e.copy(hi, prod))
            self.dve([mh], lambda e: e.tensor_tensor(lo, prod, hi.bitcast(F32), ALU.subtract))

        def down_tile(m, i):
            s = m % 2
            rowsel = slice(m, m + 1) if i is None else bass.ds(i * 2 + m, 1)
            hi, lo = w.take(down[:, rowsel, :])
            self.pe.wait(V.at(v0 + VT * (m + 1)))
            for b in range(TB):
                for c in range(2):
                    ins = down_part(s, (hi, lo), b, c, False)
            return w.used.up(ins)

        def down_part(s, unit, b, c, last):
            cs, tb = slice(c * BANK, (c + 1) * BANK), slice(b * P, (b + 1) * P)
            stat = (hid.hi[:, s, tb], hid.lo[:, s, tb])
            for x, y in ((0, 0), (0, 1), (1, 0)):
                ins = nc.tensor.matmul(psum[:, 2 * b + c, :], stat[x], unit[y][:, 0, cs], start=False,
                                       stop=last and x == 1, skip_group_check=True)
            return ins

        conv_tile(0, None)
        conv_tile(1, None)
        per = w.counts(RING)
        per.update({V: 2 * VT, A: 2 * AT})
        turns = (FT - 4) // 2
        with self.p.repeat(turns, per) as i:
            for m in (2, 3):
                conv_tile(m, i)
        w.skip((turns - 1) * RING)
        conv_tile(FT - 2, None)
        conv_tile(FT - 1, None)
        w.hold = w.next
        units = [w.take(down[:, m:m + 1, :]) for m in (FT - 2, FT - 1)]
        marks = []
        for b in range(TB):
            for c in range(2):
                for m in (FT - 2, FT - 1):
                    self.pe.wait(V.at(v0 + VT * (m + 1)))
                    ins = down_part(m % 2, units[m - FT + 2], b, c, m == FT - 1)
                    if b == TB - 1 and c == 1:
                        marks.append(w.used.up(ins))
                if b < TB - 1 or c == 0:
                    marks.append(self.pe.done.up(ins))
        w.hold = None
        marks = [marks[0:2], [marks[2], marks[4]]]
        self.xt.busy = [marks[-1][-1]]
        for k in range(4, 8):
            self.bank_free[k] = [V.now()]
        return marks


    def norm_to_features(self, gain):
        self.rms_apply(1)
        self.to_features(lambda b, j: self.n_tok[:, b, j * P:(j + 1) * P], KT, self.xt, 0, self.normed, gain)
        self.n_busy = [self.pe.done.now()]

    def add_part(self, b, c, mark):
        if b == TB - 1 and c == 1:
            self.rms_apply(0)
        h = self.x_tok[:, b, c * BANK:(c + 1) * BANK]
        m = self.dve([mark, *self.x_ready], lambda e: e.tensor_tensor(h, h, self.psum[:, 2 * b + c, :], ALU.add))
        self.bank_free[2 * b + c] = [m]
        self.squares(b, c, m)
        if c == 1:
            self.rms_factor(b)
        if b == TB - 1 and c == 1:
            self.x_ready = [m]

    def second_memory_norm(self):
        m = self.load(self.tok[:], rows(self.t["mem_2"]), [*self.tok_busy])
        tok = lambda b: self.tok[:, b, :]
        return self.rms(tok, D, tok, [m], 12)

    def second_memory_features(self, l, done):
        self.to_features(lambda b, j: self.tok[:, b, j * P:(j + 1) * P], KT, self.xt, 0, [done, done],
                         self.cols("norms_2", (DEPTH_2 + l) * KT, KT))
        self.tok_busy = [self.pe.done.now()]

    def second_memory(self, l):
        w = self.t["w_mem_kv_2"][l]
        self.project_features(w, 0, D_MEMQ // P, lambda i: self.mem_kt[:, i, :], self.xt)
        ks, outs, m = self.project_tokens(w, D_MEMQ, D_MEMQ, self.xt)
        for b in range(TB):
            m1 = self.act([m], lambda e: e.copy(self.mem_v[:, b, 0:D_MEMQ], outs[b]))
            self.bank_free[ks[b]] = [m1]
        self.mem_ready = m1

    def small_attention(self, heads, qt, kt, v, tile0, ready, **how):
        nc = self.nc
        extra = how.pop("extra", None)

        def score(h, out):
            for b in range(TB):
                o = out(b)
                ins = nc.tensor.matmul(o, qt[:, h // 2, b * P:(b + 1) * P], kt(h)[:, 0:o.shape[1]],
                                       start=True, stop=extra is None)
                if extra is not None:
                    ins = extra(h, o)
            return ins

        self.attend([([2 * g, 2 * g + 1], slice(tile0 + g, tile0 + g + 1)) for g in range(heads // 2)], 2,
                    score, lambda h: [(0, (h % 2) * HD, HD, lambda c: v[:, c, h * HD:(h + 1) * HD])],
                    self.xt, ready, **how)

    def values_2(self, w, col0):
        for c, n in ((0, BANK), (BANK, D_MIX - BANK)):
            ks, outs, m = self.project_tokens(w, col0 + c, n, self.xt)
            for b in range(TB):
                m1 = self.act([m], lambda e: e.copy(self.v[:, b, c:c + n], outs[b]))
                self.bank_free[ks[b]] = [m1]
        return m1

    def mixer_keys(self, i):
        return self.kt[:, i, :] if i < KT else self.mem_kt[:, i - KT + MEM_HEADS, :]

    def forgetting_attention(self):
        t, nc = self.t, self.nc
        w = t["w_in_fox_2"][0]
        tiles = D_MIX // P
        zeroed = self.zero_padding(self.kt)
        self.load_mask("c_mask_causal")
        tri, ones = self.gain_row[:, 0:P], self.gain_row[:, P:2 * P]
        l0 = self.load(tri, t["c_triangle"], self.row_busy)
        l1 = self.load(self.small[:, 4, 0:MIX_HEADS], t["b_forget_2"][0].partition_broadcast(P))
        one = self.pool([], lambda e: e.memset(ones, 1.0))
        self.project_features(w, 0, tiles, self.qt, self.xt, scale=HD ** -0.5)
        self.project_features(w, D_MIX, tiles, self.mixer_keys, self.xt)
        self.values_2(w, 2 * D_MIX)
        ks, outs, m = self.project_tokens(w, 3 * D_MIX, MIX_HEADS, self.xt)
        z, ab, s, w8, neg, lf = (self.small[:, q, :] for q in (0, 1, 2, 3, 5, 6))
        H = MIX_HEADS
        for b in range(TB):
            m = self.dve([m, l1], lambda e: e.tensor_tensor(z[:, b * H:(b + 1) * H], outs[b],
                                                            self.small[:, 4, 0:H], ALU.add))
            self.bank_free[ks[b]] = [m]
        m = self.dve([m], lambda e: e.scalar_tensor_tensor(ab, z, -1.0, z, ALU.mult, ALU.max))
        m1 = self.dve([], lambda e: e.tensor_scalar(neg, z, 0.0, None, ALU.min))
        m = self.act([m], lambda e: e.activation(ab, ab, ACT.Exp, scale=-1.0))
        m = self.log1p(ab, s, w8, [m])
        m = self.dve([m, m1], lambda e: e.tensor_tensor(lf, neg, s, ALU.subtract))
        m2 = self.project_features(w, 3 * D_MIX + H, D_MEMQ // P, self.qrt, self.xt)
        k = self.bank()
        self.pe.wait(m, l0, one)
        out = self.psum[:, k, 0:2 * H]
        nc.tensor.matmul(out[:, 0:H], tri, lf[:, 0:H], start=True, stop=True)
        nc.tensor.matmul(out[:, H:2 * H], tri, lf[:, H:2 * H], start=True, stop=False)
        m = self.pe.done.up(nc.tensor.matmul(out[:, H:2 * H], ones, lf[:, 0:H], start=False, stop=True))
        csum = self.norm[:, 8:8 + 2 * H]
        m3 = self.dve([m], lambda e: e.tensor_copy(csum, out))
        neg_c = self.tok[:, :, 0:P]
        mz = self.dve([*self.tok_busy], lambda e: e.memset(neg_c, 0.0))
        for b in range(TB):
            m4 = self.dve([mz, m3], lambda e: e.tensor_scalar(
                neg_c[:, b, 0:H], csum[:, b * H:(b + 1) * H], -1.0, None, ALU.mult))
        self.bank_free[k] = [m3]
        m = self.turn_tokens(lambda b, i: neg_c[:, b, :], 1, self.krt, [m4])

        def minus_c(h, out):
            return nc.tensor.matmul(out, self.ident[:, h:h + 1].broadcast_to([P, P]),
                                    self.krt[:, 0, 0:out.shape[1]], start=False, stop=True)

        self.small_attention(MIX_HEADS, self.qt, self.mixer_keys, self.v, 0, [m, m2, zeroed], mask=True, extra=minus_c,
                             row_add=lambda h, b: csum[:, b * H + h:b * H + h + 1])
        self.row_busy = [self.pe.done.now()]

    def dilated_attention(self):
        t = self.t
        w = t["w_in_dil_2"][0]
        self.load_mask("c_mask_dilated")
        zeroed = self.zero_padding(self.kt)
        waiting, half = None, 0
        self.tok_half_busy = [self.tok_busy, self.tok_busy]
        for part in range(2):
            for c, n in ((0, BANK), (BANK, D_MIX - BANK)):
                dst = self.qt[:, c // P:(c + n) // P, :] if part == 0 else \
                    (lambda c: lambda i: self.mixer_keys(2 * (c // P) + i))(c)
                waiting = self.rotated(w, part * D_MIX + c, n, half, dst, waiting)
                half = 1 - half
        self.values_2(w, 2 * D_MIX)
        self.turn_half(*waiting)
        m = self.project_features(w, 3 * D_MIX, D_MEMQ // P, self.qrt, self.xt)
        self.small_attention(MIX_HEADS, self.qt, self.mixer_keys, self.v, 0, [m, zeroed], scale=HD ** -0.5, mask=True)

    def build(self):
        t, p = self.t, self.p
        self.mem_keys_values()
        self.turn_params()
        self.to_features(lambda b, j: self.x_tok[:, b, j * P:(j + 1) * P], KT, self.xt, 0, self.x_ready * 2)
        self.x_ready.append(self.pe.done.now())
        kinds = [self.sliding_attention, lambda j, f: self.recurrent_block(f),
                 lambda j, f: self.latent_attention(f)]
        for l in range(DEPTH):
            last = l == DEPTH - 1
            kinds[l % 3](l // 3, self.norm_sink(l, 0))
            self.norm_finish(l, 0)
            self.cross_attention(l, self.norm_sink(l, 1))
            self.seed_accumulators()
            self.norm_finish(l, 1)
            if last:
                mem_tok = self.second_memory_norm()
                mem_zeroed = self.zero_padding(self.mem_kt)
            sink = self.norm_sink(l, 2, last)
            m = self.feed_forward(t["f_w_up"][l], t["f_w_down"][l], ("f", l), 0)
            if last:
                self.second_memory_features(0, mem_tok)
            for b in range(TB):
                for c in range(2):
                    sink(b, c, m[b][c])
            self.accumulating = False
            if last:
                self.norm_finish_last()
            else:
                self.norm_finish(l, 2)
        for l in range(DEPTH_2):
            self.second_memory(l)
            self.norm_to_features(self.cols("norms_2", l * KT, KT))
            if l % 2 == 0:
                self.forgetting_attention()
            else:
                self.dilated_attention()
            self.small_attention(MEM_HEADS, self.qrt, lambda i: self.mem_kt[:, i, :], self.mem_v, D_MIX // P,
                                 [self.mem_ready, mem_zeroed], scale=HD ** -0.5)
            self.out_project(t["w_out_2"][l], self.xt, self.add_part)
            self.seed_accumulators()
            self.norm_to_features(self.cols("norms_2", (2 * DEPTH_2 + l) * KT, KT))
            if l < DEPTH_2 - 1:
                mem_tok = self.second_memory_norm()
            m = self.feed_forward(t["w_up_2"][l], t["w_down_2"][l], ("g", l), 1)
            if l < DEPTH_2 - 1:
                self.second_memory_features(l + 1, mem_tok)
            else:
                gain = self.load(self.gain_row[:], t["norm_final_2"].partition_broadcast(P), self.row_busy)
            for b in range(TB):
                for c in range(2):
                    self.add_part(b, c, m[b][c])
            self.accumulating = False
        self.rms_apply(1)
        for b in range(TB):
            z = self.n_tok[:, b, :]
            m = self.dve([self.normed[b], gain], lambda e: e.tensor_tensor(z, z, self.gain_row[:], ALU.mult))
            self.sp.wait(m)
            self.stores.up(self.nc.sync.dma_start(self.t["out"][b * P:(b + 1) * P, :], z))
        self.sp.wait(self.stores.now())
        self.units = self.w.next


def two_stacks_kernel(nc, tensors, total_units):
    with ExitStack() as ctx:
        t = dict(tensors)
        for name in ("x", "mem", "mem_2", "out"):
            t[name] = t[name].rearrange("a s d -> (a s) d")
        model = Model(nc, ctx, t, total_units)
        model.build()
        return model.units


_INS = ["x", "mem", "a_w_qkv", "a_sinks", "a_w_o", "b_w_in", "b_conv_w", "b_conv_b", "b_w_rgate",
        "b_b_rgate", "b_w_igate", "b_b_igate", "b_lambda", "b_w_o", "c_w_down", "c_q_norm", "c_kv_norm",
        "c_w_uq", "c_w_ukv", "c_w_o", "mem_w_kv", "x_w_q", "x_w_o", "f_w_up", "f_conv_w", "f_conv_b",
        "f_w_down", "ln_g", "ln_b", "mem_2", "norm_mix_2", "norm_mem_2", "norm_ffn_2", "w_in_fox_2",
        "b_forget_2", "w_in_dil_2", "w_mem_kv_2", "w_out_2", "w_up_2", "conv_w_2", "conv_b_2",
        "w_down_2", "norm_final_2"]
UNITS = 639


def shape_constants():
    import numpy as np
    f = np.float32
    i, j = np.arange(SEQ)[:, None], np.arange(SEQ)[None, :]
    d = i - j
    inv = (f(1.0) / (f(10000.0) ** (np.arange(0, HD, 2, dtype=f) / f(HD)))).astype(f)
    ang = np.arange(SEQ, dtype=f)[:, None] * inv[None, :]
    cos, sin = np.cos(ang).astype(f), np.sin(ang).astype(f)
    neg = f(-1e30)
    count = ((d >= 0) & (d <= 128)).astype(int) + ((d >= 0) & (d % 4 == 0)) + ((d >= 0) & (d % 16 == 0))
    return {
        "c_ident": np.eye(P, dtype=f),
        "c_triangle": np.triu(np.ones((P, P), dtype=f)),
        "c_cos": np.concatenate([cos, cos], 1),
        "c_sin": np.concatenate([-sin, sin], 1),
        "c_mask_window": np.where((d >= 0) & (d < 128), f(0), neg).astype(f),
        "c_mask_causal": np.where(d >= 0, f(0), neg).astype(f),
        "c_mask_dilated": np.where(count > 0, np.log(np.maximum(count, 1)), neg).astype(f),
    }


def kernel(**inputs):
    import numpy as _np
    import concourse.bacc as _bacc
    from concourse import mybir as _mybir
    from concourse.bass_utils import run_bass_kernel_spmd as _run

    nc = _bacc.Bacc("TRN2", target_bir_lowering=False, num_devices=1)
    arrays, tensors = {}, {}
    for name, a in [(n, inputs[n]) for n in _INS] + list(shape_constants().items()):
        a = _np.ascontiguousarray(a)
        arrays[f"in_{name}_dram"] = a
        tensors[name] = nc.dram_tensor(f"in_{name}_dram", a.shape, _mybir.dt.from_np(a.dtype),
                                       kind="ExternalInput").ap()
    tensors["out"] = nc.dram_tensor("out_0_dram", (1, SEQ, D), F32, kind="ExternalOutput").ap()
    two_stacks_kernel(nc, tensors, UNITS)
    r = _run(nc, [arrays], core_ids=[0])
    return r.results[0]["out_0_dram"]
```
